# Optimizing a Trainium2 kernel written in Bass

```python
import jax, jax.numpy as jnp
from jax import lax
import numpy as np
import math

D_MODEL = 1024
BATCH = 1
SEQ = 512
DEPTH = 1

CHUNK = 64

MIX_WIDTH = D_MODEL
CONV_W = MIX_WIDTH // 2
LRU_W = MIX_WIDTH - CONV_W
N_CONV_HEADS = 8
N_LRU_HEADS = 8
CONV_HD = CONV_W // N_CONV_HEADS
LRU_HD = LRU_W // N_LRU_HEADS
SHORT_CONV_K = 3
LRU_CONV_K = 4
LRU_C = 8.0
N_IN = 3 * CONV_W + 2 * LRU_W

PEER_HEADS = 8
PEER_TOPK = 16
N_KEYS = 128
N_EXPERTS = N_KEYS * N_KEYS
PEER_DK = 128
PEER_DK_HALF = PEER_DK // 2
PEER_BLOCK = 128

EPS = 1e-6


def rmsnorm(x, g):
    x32 = x.astype(jnp.float32)
    y = x32 * lax.rsqrt(jnp.mean(x32 * x32, axis=-1, keepdims=True) + EPS)
    return y.astype(x.dtype) * g

def head_rmsnorm(y, g, n_heads):
    b, s, w = y.shape
    yh = y.reshape(b, s, n_heads, w // n_heads).astype(jnp.float32)
    yh = yh * lax.rsqrt(jnp.mean(yh * yh, axis=-1, keepdims=True) + EPS)
    return yh.reshape(b, s, w).astype(y.dtype) * g

def modulate(h, shift, scale):
    return h * (1.0 + scale[:, None, :]) + shift[:, None, :]

def causal_dwconv(x, w):
    k_w = w.shape[0]
    s = x.shape[1]
    xp = jnp.pad(x, ((0, 0), (k_w - 1, 0), (0, 0)))
    out = xp[:, 0:s] * w[0]
    for k in range(1, k_w):
        out = out + xp[:, k:k + s] * w[k]
    return out

def rg_lru(xr, w_r, b_r, w_i, b_i, lam):
    b, s, _ = xr.shape
    xh = xr.reshape(b, s, N_LRU_HEADS, LRU_HD)
    r = jax.nn.sigmoid(jnp.einsum('bshi,hij->bshj', xh, w_r) + b_r).astype(jnp.float32)
    i = jax.nn.sigmoid(jnp.einsum('bshi,hij->bshj', xh, w_i) + b_i).astype(jnp.float32)
    log_a = -LRU_C * r * jax.nn.softplus(-lam.astype(jnp.float32))
    a = jnp.exp(log_a)
    u = jnp.sqrt(-jnp.expm1(2.0 * log_a)) * (i * xh.astype(jnp.float32))

    def combine(e1, e2):
        a1, b1 = e1
        a2, b2 = e2
        return a1 * a2, a2 * b1 + b2

    _, h = lax.associative_scan(combine, (a, u), axis=1)
    return h.reshape(b, s, LRU_W).astype(xr.dtype)

def peer(h, w_q, sub_keys, expert_u, expert_v):
    b, s, d = h.shape
    t = b * s
    hb = h.reshape(t // PEER_BLOCK, PEER_BLOCK, d)
    kk = PEER_TOPK * PEER_TOPK

    def block(xb):
        p = xb.shape[0]
        q = (xb @ w_q).reshape(p, PEER_HEADS, 2, PEER_DK_HALF)
        sc = jnp.einsum('phcd,hcnd->phcn', q, sub_keys).astype(jnp.float32)
        top_s, top_i = lax.top_k(sc, PEER_TOPK)
        cand_s = (top_s[:, :, 0, :, None] + top_s[:, :, 1, None, :]).reshape(p, PEER_HEADS, kk)
        cand_i = (top_i[:, :, 0, :, None] * N_KEYS + top_i[:, :, 1, None, :]).reshape(p, PEER_HEADS, kk)
        best_s, best_pos = lax.top_k(cand_s, PEER_TOPK)
        idx = jnp.take_along_axis(cand_i, best_pos, axis=-1)
        g = jax.nn.softmax(best_s, axis=-1)
        u_sel = expert_u[idx]
        act = jax.nn.gelu(jnp.einsum('phkd,pd->phk', u_sel, xb), approximate=False)
        coef = (g * act.astype(jnp.float32)).astype(xb.dtype)
        return jnp.einsum('phk,phkd->pd', coef, expert_v[idx])

    return lax.map(block, hb).reshape(b, s, d)

def first_inputs(seed: int = 0) -> dict:
    key = jax.random.key(seed)
    ks = jax.random.split(key, 24)
    f32 = jnp.float32
    L = DEPTH

    def nrm(k, shape, scale):
        return jax.random.normal(k, shape, f32) * scale

    a8 = jax.random.uniform(ks[13], (L, N_LRU_HEADS, LRU_HD), f32, 0.9, 0.999)
    a_base = a8 ** (1.0 / LRU_C)
    lru_lambda = jnp.log(a_base) - jnp.log1p(-a_base)

    return {
        "x": nrm(ks[0], (BATCH, SEQ, D_MODEL), 1.0),
        "c": nrm(ks[1], (BATCH, D_MODEL), 1.0),
        "w_ada": nrm(ks[2], (L, D_MODEL, 6 * D_MODEL), 0.5 * D_MODEL ** -0.5),
        "b_ada": nrm(ks[3], (L, 6 * D_MODEL), 0.02),
        "norm1_g": 1.0 + nrm(ks[4], (L, D_MODEL), 0.02),
        "w_in": nrm(ks[5], (L, D_MODEL, N_IN), D_MODEL ** -0.5),
        "conv_a_w": nrm(ks[6], (L, SHORT_CONV_K, CONV_W), SHORT_CONV_K ** -0.5),
        "conv_b_w": nrm(ks[7], (L, LRU_CONV_K, LRU_W), LRU_CONV_K ** -0.5),
        "conv_b_b": nrm(ks[8], (L, LRU_W), 0.02),
        "w_r": nrm(ks[9], (L, N_LRU_HEADS, LRU_HD, LRU_HD), LRU_HD ** -0.5),
        "b_r": nrm(ks[10], (L, N_LRU_HEADS, LRU_HD), 0.02),
        "w_i": nrm(ks[11], (L, N_LRU_HEADS, LRU_HD, LRU_HD), LRU_HD ** -0.5),
        "b_i": nrm(ks[12], (L, N_LRU_HEADS, LRU_HD), 0.02),
        "lru_lambda": lru_lambda,
        "gn_a": 1.0 + nrm(ks[14], (L, CONV_W), 0.02),
        "gn_b": 1.0 + nrm(ks[15], (L, LRU_W), 0.02),
        "w_out": nrm(ks[16], (L, MIX_WIDTH, D_MODEL), MIX_WIDTH ** -0.5),
        "norm2_g": 1.0 + nrm(ks[17], (L, D_MODEL), 0.02),
        "w_q": nrm(ks[18], (L, D_MODEL, PEER_HEADS * PEER_DK), D_MODEL ** -0.5),
        "sub_keys": nrm(ks[19], (L, PEER_HEADS, 2, N_KEYS, PEER_DK_HALF), PEER_DK_HALF ** -0.5),
        "expert_u": nrm(ks[20], (L, N_EXPERTS, D_MODEL), D_MODEL ** -0.5),
        "expert_v": nrm(ks[21], (L, N_EXPERTS, D_MODEL), PEER_HEADS ** -0.5),
        "final_g": 1.0 + nrm(ks[22], (D_MODEL,), 0.02),
    }

def first_block(x, c, w_ada, b_ada, norm1_g, w_in, conv_a_w, conv_b_w, conv_b_b,
              w_r, b_r, w_i, b_i, lru_lambda, gn_a, gn_b, w_out,
              norm2_g, w_q, sub_keys, expert_u, expert_v, final_g):
    c_act = jax.nn.silu(c)
    for l in range(DEPTH):
        ada = c_act @ w_ada[l] + b_ada[l]
        sh1, sc1, g1, sh2, sc2, g2 = jnp.split(ada, 6, axis=-1)

        h = modulate(rmsnorm(x, norm1_g[l]), sh1, sc1)
        z = h @ w_in[l]
        gate_b, gate_c, xa, xr, gr = jnp.split(
            z, [CONV_W, 2 * CONV_W, 3 * CONV_W, 3 * CONV_W + LRU_W], axis=-1)

        y_a = gate_b * causal_dwconv(gate_c * xa, conv_a_w[l])

        xr = causal_dwconv(xr, conv_b_w[l]) + conv_b_b[l]
        y_b = rg_lru(xr, w_r[l], b_r[l], w_i[l], b_i[l], lru_lambda[l]) * jax.nn.gelu(gr)

        y = jnp.concatenate([head_rmsnorm(y_a, gn_a[l], N_CONV_HEADS),
                             head_rmsnorm(y_b, gn_b[l], N_LRU_HEADS)], axis=-1) @ w_out[l]
        x = x + g1[:, None, :] * y

        h = modulate(rmsnorm(x, norm2_g[l]), sh2, sc2)
        x = x + g2[:, None, :] * peer(h, w_q[l], sub_keys[l], expert_u[l], expert_v[l])

    return rmsnorm(x, final_g)


MIX_WIDTH_2 = D_MODEL
MOBA_WIDTH = MIX_WIDTH_2 // 2
MOBA_HEAD_DIM = 64
MOBA_HEADS = MOBA_WIDTH // MOBA_HEAD_DIM
MOBA_BLOCK = 256
MOBA_TOPK = 3
QUERY_CHUNK = 128
GDN_WIDTH = MIX_WIDTH_2 - MOBA_WIDTH
GDN_HEAD_DIM = 128
GDN_HEADS = GDN_WIDTH // GDN_HEAD_DIM
GDN_CONV = 4
GDN_CHUNK = 64
IN_SPLITS = (MOBA_WIDTH,) * 4 + (GDN_WIDTH,) * 4 + (GDN_HEADS, GDN_HEADS)
IN_WIDTH = sum(IN_SPLITS)
RMS_EPS = 1e-6
NEG_INF = -1e30


def rms_norm(x, w):
    xf = x.astype(jnp.float32)
    y = xf * lax.rsqrt(jnp.mean(xf * xf, axis=-1, keepdims=True) + RMS_EPS)
    return (y * w.astype(jnp.float32)).astype(x.dtype)

def alibi_slopes(n_heads):
    start = 2.0 ** (-8.0 / n_heads)
    return jnp.asarray(start ** np.arange(1, n_heads + 1), dtype=jnp.float32)

def moba_attention(q, k, v):
    B, T, H, dh = q.shape
    nb = -(-T // MOBA_BLOCK)
    pad = nb * MOBA_BLOCK - T
    n_qc = T // QUERY_CHUNK
    k_sel = min(MOBA_TOPK, nb - 1)
    scale = dh ** -0.5
    slopes = alibi_slopes(H)
    qh = q.transpose(0, 2, 1, 3)
    pad_cfg = ((0, 0), (0, pad), (0, 0), (0, 0))
    kb = jnp.pad(k, pad_cfg).reshape(B, nb, MOBA_BLOCK, H, dh).transpose(0, 3, 1, 2, 4)
    vb = jnp.pad(v, pad_cfg).reshape(B, nb, MOBA_BLOCK, H, dh).transpose(0, 3, 1, 2, 4)
    kbar = jnp.mean(kb.astype(jnp.float32), axis=3)
    blk_off = jnp.arange(MOBA_BLOCK)
    head_idx = jnp.arange(H)[:, None, None]

    def chunk_attend(step):
        bi = step // n_qc
        q0 = (step % n_qc) * QUERY_CHUNK
        own = q0 // MOBA_BLOCK
        qc = lax.dynamic_slice_in_dim(qh[bi], q0, QUERY_CHUNK, axis=1)
        kb_b, vb_b = kb[bi], vb[bi]
        t_pos = q0 + jnp.arange(QUERY_CHUNK)
        k_own = lax.dynamic_index_in_dim(kb_b, own, axis=1, keepdims=False)
        v_own = lax.dynamic_index_in_dim(vb_b, own, axis=1, keepdims=False)
        dist_own = (t_pos[:, None] - (own * MOBA_BLOCK + blk_off)[None, :]).astype(jnp.float32)
        logit_own = (jnp.einsum('hqd,hkd->hqk', qc, k_own).astype(jnp.float32) * scale
                     - slopes[:, None, None] * dist_own)
        logit_own = jnp.where(dist_own >= 0, logit_own, NEG_INF)
        if k_sel == 0:
            p = jax.nn.softmax(logit_own, axis=-1).astype(v.dtype)
            return jnp.einsum('hqk,hkd->hqd', p, v_own)
        gate = jnp.einsum('hqd,hnd->hqn', qc.astype(jnp.float32), kbar[bi])
        gate = jnp.where(jnp.arange(nb) < own, gate, NEG_INF)
        _, sel = lax.top_k(gate, k_sel)
        k_g = kb_b[head_idx, sel]
        v_g = vb_b[head_idx, sel]
        s_sel = sel[..., None] * MOBA_BLOCK + blk_off
        dist_sel = (t_pos[None, :, None, None] - s_sel).astype(jnp.float32)
        logit_sel = (jnp.einsum('hqd,hqnkd->hqnk', qc, k_g).astype(jnp.float32) * scale
                     - slopes[:, None, None, None] * dist_sel)
        valid = (jnp.arange(k_sel) < own)[None, None, :, None]
        logit_sel = jnp.where(valid, logit_sel, NEG_INF).reshape(H, QUERY_CHUNK, k_sel * MOBA_BLOCK)
        p = jax.nn.softmax(jnp.concatenate([logit_sel, logit_own], axis=-1), axis=-1).astype(v.dtype)
        p_sel = p[..., :k_sel * MOBA_BLOCK].reshape(H, QUERY_CHUNK, k_sel, MOBA_BLOCK)
        p_own = p[..., k_sel * MOBA_BLOCK:]
        return (jnp.einsum('hqnk,hqnkd->hqd', p_sel, v_g)
                + jnp.einsum('hqk,hkd->hqd', p_own, v_own))

    out = lax.map(chunk_attend, jnp.arange(B * n_qc))
    out = out.reshape(B, n_qc, H, QUERY_CHUNK, dh).transpose(0, 1, 3, 2, 4)
    return out.reshape(B, T, H * dh)

def causal_depthwise_conv(x, w):
    K, C = w.shape
    return lax.conv_general_dilated(
        x, w[:, None, :].astype(x.dtype), window_strides=(1,), padding=((K - 1, 0),),
        dimension_numbers=('NWC', 'WIO', 'NWC'), feature_group_count=C)

def l2_normalize(x):
    return x * lax.rsqrt(jnp.sum(x * x, axis=-1, keepdims=True) + RMS_EPS)

def gated_delta_rule(q, k, v, g, beta):
    B, T, H, dk = q.shape
    dv = v.shape[-1]
    C = GDN_CHUNK
    nc = T // C
    q = l2_normalize(q) * (dk ** -0.5)
    k = l2_normalize(k)

    def chunks(t):
        return t.reshape(B, nc, C, H, -1).transpose(1, 0, 3, 2, 4)

    q, k, v = chunks(q), chunks(k), chunks(v)
    beta = beta.reshape(B, nc, C, H).transpose(1, 0, 3, 2)
    gc = jnp.cumsum(g.reshape(B, nc, C, H).transpose(1, 0, 3, 2), axis=-1)
    causal = jnp.tril(jnp.ones((C, C), dtype=bool))
    strict = jnp.tril(jnp.ones((C, C), dtype=bool), -1)
    decay = jnp.exp(jnp.where(causal, gc[..., :, None] - gc[..., None, :], -jnp.inf))
    k_beta = k * beta[..., None]
    a = jnp.where(strict, jnp.einsum('nbhid,nbhjd->nbhij', k_beta, k) * decay, 0.0)
    eye = jnp.eye(C, dtype=jnp.float32)
    t_inv = lax.linalg.triangular_solve(a + eye, jnp.broadcast_to(eye, a.shape),
                                        left_side=True, lower=True, unit_diagonal=True)
    u = t_inv @ (v * beta[..., None])
    w = t_inv @ (k_beta * jnp.exp(gc)[..., None])
    intra = jnp.where(causal, jnp.einsum('nbhid,nbhjd->nbhij', q, k) * decay, 0.0)
    q_dec = q * jnp.exp(gc)[..., None]
    k_dec = k * jnp.exp(gc[..., -1:] - gc)[..., None]
    g_last = jnp.exp(gc[..., -1])

    def step(S, xs):
        q_i, k_i, u_i, w_i, intra_i, gl = xs
        v_new = u_i - w_i @ S
        o = q_i @ S + intra_i @ v_new
        S = S * gl[..., None, None] + jnp.einsum('bhcd,bhce->bhde', k_i, v_new)
        return S, o

    S0 = jnp.zeros((B, H, dk, dv), dtype=jnp.float32)
    _, o = lax.scan(step, S0, (q_dec, k_dec, u, w, intra, g_last))
    return o.transpose(1, 0, 3, 2, 4).reshape(B, T, H, dv)

def hybrid_layer(x, norm_pre_w, w_in, conv_w, a_log, dt_bias, gdn_norm_w, w_out, norm_post_w):
    B, T, _ = x.shape
    h = rms_norm(x, norm_pre_w)
    proj = h @ w_in.astype(x.dtype)
    split_at = list(np.cumsum(IN_SPLITS)[:-1])
    a_q, a_k, a_v, a_z, d_q, d_k, d_v, d_z, d_b, d_a = jnp.split(proj, split_at, axis=-1)

    heads_a = lambda t: t.reshape(B, T, MOBA_HEADS, MOBA_HEAD_DIM)
    moba_out = moba_attention(heads_a(a_q), heads_a(a_k), heads_a(a_v)) * jax.nn.silu(a_z)

    qkv = jax.nn.silu(causal_depthwise_conv(jnp.concatenate([d_q, d_k, d_v], axis=-1), conv_w))
    g_q, g_k, g_v = jnp.split(qkv, 3, axis=-1)
    heads_b = lambda t: t.reshape(B, T, GDN_HEADS, GDN_HEAD_DIM).astype(jnp.float32)
    beta = jax.nn.sigmoid(d_b.astype(jnp.float32))
    g = -jnp.exp(a_log.astype(jnp.float32)) * jax.nn.softplus(
        d_a.astype(jnp.float32) + dt_bias.astype(jnp.float32))
    o = gated_delta_rule(heads_b(g_q), heads_b(g_k), heads_b(g_v), g, beta)
    gdn_out = rms_norm(o, gdn_norm_w).reshape(B, T, GDN_WIDTH).astype(x.dtype) * jax.nn.silu(d_z)

    mixed = jnp.concatenate([moba_out, gdn_out], axis=-1) @ w_out.astype(x.dtype)
    return x + rms_norm(mixed, norm_post_w)

def second_inputs(seed: int = 0) -> dict:
    key = jax.random.key(seed)
    ks = jax.random.split(key, 9)
    f32 = jnp.float32
    x = jax.random.normal(ks[0], (BATCH, SEQ, D_MODEL), f32)
    norm_pre_w = 1.0 + 0.05 * jax.random.normal(ks[1], (DEPTH, D_MODEL), f32)
    w_in = jax.random.normal(ks[2], (DEPTH, D_MODEL, IN_WIDTH), f32) * D_MODEL ** -0.5
    conv_w = jax.random.normal(ks[3], (DEPTH, GDN_CONV, 3 * GDN_WIDTH), f32) * GDN_CONV ** -0.5
    a_log = jnp.log(jax.random.uniform(ks[4], (DEPTH, GDN_HEADS), f32, minval=1.0, maxval=16.0))
    dt = jnp.exp(jax.random.uniform(ks[5], (DEPTH, GDN_HEADS), f32,
                                    minval=math.log(1e-3), maxval=math.log(1e-1)))
    dt_bias = dt + jnp.log(-jnp.expm1(-dt))
    gdn_norm_w = 1.0 + 0.05 * jax.random.normal(ks[6], (DEPTH, GDN_HEAD_DIM), f32)
    w_out = jax.random.normal(ks[7], (DEPTH, MIX_WIDTH_2, D_MODEL), f32) * MIX_WIDTH_2 ** -0.5
    norm_post_w = 1.0 + 0.05 * jax.random.normal(ks[8], (DEPTH, D_MODEL), f32)
    return {"x": x, "norm_pre_w": norm_pre_w, "w_in": w_in, "conv_w": conv_w,
            "a_log": a_log, "dt_bias": dt_bias, "gdn_norm_w": gdn_norm_w,
            "w_out": w_out, "norm_post_w": norm_post_w}

def second_block(x, norm_pre_w, w_in, conv_w, a_log, dt_bias, gdn_norm_w, w_out, norm_post_w):
    for layer in range(DEPTH):
        x = hybrid_layer(x, norm_pre_w[layer], w_in[layer], conv_w[layer], a_log[layer],
                         dt_bias[layer], gdn_norm_w[layer], w_out[layer], norm_post_w[layer])
    return x


def setup_inputs(seed=0):
    out = dict(first_inputs(seed))
    for name, value in second_inputs(seed + 1).items():
        if name != "x":
            out[name + "_2"] = value
    return out


def reference(
    x, c, w_ada, b_ada, norm1_g, w_in, conv_a_w, conv_b_w, conv_b_b, w_r, b_r, w_i, b_i,
    lru_lambda, gn_a, gn_b, w_out, norm2_g, w_q, sub_keys, expert_u, expert_v, final_g,
    norm_pre_w_2, w_in_2, conv_w_2, a_log_2, dt_bias_2, gdn_norm_w_2, w_out_2, norm_post_w_2,
):
    x = first_block(
        x, c, w_ada, b_ada, norm1_g, w_in, conv_a_w, conv_b_w, conv_b_b, w_r, b_r, w_i, b_i,
        lru_lambda, gn_a, gn_b, w_out, norm2_g, w_q, sub_keys, expert_u, expert_v, final_g,
    )
    return second_block(
        x, norm_pre_w_2, w_in_2, conv_w_2, a_log_2, dt_bias_2, gdn_norm_w_2, w_out_2,
        norm_post_w_2,
    )


_drawn_inputs = setup_inputs


def setup_inputs(seed=0):
    import zlib

    import numpy as np

    out = dict(_drawn_inputs(seed))
    spreads = {}
    factors = {'norm1_g': 3.989, 'b_r': 8.0, 'b_i': 8.0, 'gn_a': 7.615, 'gn_b': 7.588, 'norm2_g': 5.241}
    for name, (base, spread) in spreads.items():
        noise = np.random.default_rng([zlib.crc32(name.encode()), seed]).standard_normal(out[name].shape)
        drawn = base * np.exp(spread * noise) if base else spread * noise
        out[name] = __import__('jax').numpy.asarray(drawn.astype(out[name].dtype))
    for name, factor in factors.items():
        out[name] = (out[name] * factor).astype(out[name].dtype)
    return out
```

```python
from contextlib import ExitStack

import concourse.bass as bass
from concourse import mybir

P = 128
D = 1024
KC = D // P
T = 512
TB = T // P
F32 = mybir.dt.float32
F32R = mybir.dt.float32r
U32 = mybir.dt.uint32
ALU = mybir.AluOpType
ACT = mybir.ActivationFunctionType
AX_X = mybir.AxisListType.X

EPS = 1e-6
HEADS = 8
TOPK = 16
N_KEYS = 128
LOWEST = -3.0e38

RAW = 4
SPLIT = 2
U_IN = 0
U_OUT = U_IN + 20
U_Q = U_OUT + 8
U_EU = U_Q + 8
U_EV = U_EU + N_KEYS
U_IN2 = U_EV + N_KEYS
U_OUT2 = U_IN2 + 32
U_END = U_OUT2 + 8

QUAD = 4
WT = 32
GROUP = 4
ONEHOT = 16
TOK_PER_UNIT = 8

COLS = {}
_n = 0
for _name, _k in (("n1", 8), ("n2", 8), ("fin", 8), ("pre2", 8), ("post2", 8), ("gn", 8),
                  ("cbb", 4), ("br", 4), ("bi", 4), ("lam", 4), ("gdn", 1),
                  ("caw", 12), ("cbw", 16), ("c2w", 48), ("bada", 48), ("c", 8), ("alog", 4), ("dtb", 4)):
    COLS[_name] = _n
    _n += _k
N_COLS = _n


GH = 4
LEVELS = 7
MH = 8


def second_block_steps():
    steps = []
    for w in range(13):
        if w < 12:
            steps.append(("unit", w))
        steps.append(("conv", w))
        if w == 1:
            steps.append(("rates", 0))
        if 3 <= w < 11:
            steps.append(("l2", w - 3))
    steps.append(("cumulate", 0))
    for tb in range(TB):
        steps.append(("decay", tb))
        if tb < 2:
            steps.append(("unit", 12 + tb))
    w = 14
    for level in range(LEVELS):
        for what, tb in (("M", 0), ("M", 1), ("X", 0), ("M", 2), ("X", 1), ("M", 3), ("X", 2), ("X", 3)):
            if (what, tb) in (("X", 0), ("X", 2)) and w < 24:
                steps.append(("unit", w))
                w += 1
            steps.append((what, level, tb))
    for tb in range(TB):
        steps.append(("tokens", tb))
        steps.append(("solve", tb))
    for tb in range(TB):
        steps.append(("unit", 24 + tb))
        steps.append(("scan", tb))
    for tb in range(TB):
        steps.append(("values", tb))
    n = 2 * TB * GH
    for i in range(n + 3):
        if i < 4:
            steps.append(("unit", 28 + i))
        if i >= 3:
            steps.append(("pv", i - 3))
        if i < n:
            steps.append(("logits", i))
        if i >= 1 and i - 1 < n:
            steps.append(("probs", i - 1))
        if i == 4:
            steps += [("gdn_out", h) for h in range(GH)]
    for c in range(KC):
        steps.append(("unit", 32 + c))
    return steps


STEPS2 = second_block_steps()
JOBS, READERS = {}, []


def _jobs():
    def job(name, readers=1):
        JOBS[name] = len(READERS)
        READERS.append(readers)

    for st in STEPS2:
        kind, n = st[0], st[1:]
        if kind == "rates":
            job(("ba",))
        if kind == "cumulate":
            job(("cum",))
        if kind == "decay":
            job(("gcr", *n), 2)
            job(("br", *n))
            job(("kk", *n))
            job(("qk", *n))
        if kind == "M":
            job(("m", *n))
        if kind == "X":
            if n[0] < LEVELS - 1:
                job(("x", *n))
            job(("xt", *n))
        if kind == "tokens":
            job(("kt", *n), 2)
            job(("vt", *n))
        if kind == "solve":
            job(("wt", *n))
            job(("u", *n))
        if kind == "scan":
            if n[0]:
                job(("ws", *n))
            job(("o", *n))
            if n[0] < TB - 1:
                job(("su", *n))
        if kind == "values":
            job(("av", *n))
        if kind == "logits":
            job(("s", *n))
        if kind == "pv":
            job(("pt", *n))


_jobs()


class Chain:

    def __init__(self, eng, sem):
        self.eng, self.sem, self.n, self.at = eng, sem, 0, None

    def post(self, ins):
        ins.then_inc(self.sem, 1)
        self.n += 1
        return self.n

    def wait(self):
        self.eng.wait_ge(self.sem, self.n if self.at is None else self.at + self.n)

    def link(self, ins):
        self.post(ins)
        self.wait()


def build(nc, A, out):
    with ExitStack() as ctx:
        def sb(name, shape, dt=F32):
            return ctx.enter_context(nc.sbuf_tensor(name, shape, dt))

        def sem(name):
            return ctx.enter_context(nc.semaphore(name))

        PS = ctx.enter_context(nc.psum_tensor("PS", [P, 8, 512], F32))
        xres = sb("xres", [P, KC, T])
        act_hi = sb("act_hi", [P, KC, T], F32R)
        act_lo = sb("act_lo", [P, KC, T], F32R)
        raw = sb("raw", [P, RAW, D])
        w_hi = sb("w_hi", [P, SPLIT, D], F32R)
        w_lo = sb("w_lo", [P, SPLIT, D], F32R)
        ident = sb("ident", [P, P])
        ones = sb("ones", [P, P])
        upper = sb("upper", [P, P])
        iota = sb("iota", [P, P])
        cols = sb("cols", [P, N_COLS])
        ada = sb("ada", [P, 48])
        small = sb("small", [P, 176])
        ARENA = 31136
        arena = sb("arena", [P, ARENA])
        used = {}

        def region(name, start, *shape, dt=None):
            n = 1
            for s in shape:
                n *= s
            assert start + n <= ARENA, (name, start + n)
            used[name] = (start, start + n)
            ap = arena[:, start:start + n]
            if dt is not None:
                ap = ap.bitcast(dt)
            if len(shape) == 2:
                ap = ap.rearrange("p (a b) -> p a b", a=shape[0])
            if len(shape) == 3:
                ap = ap.rearrange("p (a b c) -> p a b c", a=shape[0], b=shape[1])
            return ap

        def col(name, c=0, n=1):
            return cols[:, COLS[name] + c:COLS[name] + c + n]

        eps = small[:, 0:1]
        cs = small[:, 8:16]
        cth = small[:, 16:24]
        gain1 = small[:, 24:32]
        gain2 = small[:, 32:40]
        dec = small[:, 40:44]
        hbr = small[:, 44:48]
        hbi = small[:, 48:52]
        sp = [small[:, 56 + 16 * i:60 + 16 * i] for i in range(6)]
        fgain = small[:, 160:168]

        xrp = region("xrp", 0, 4, 516)
        xc = region("xc", 2064, 4, 512)
        gg = region("gg", 4112, 4, 512)
        tr = region("tr", 6160, 4, 512)
        ti = region("ti", 8208, 4, 512)
        y = region("y", 10256, 8, 512)
        xa = region("xa", 14352, 2, 512)
        pc = region("pc", 15376, 2, 516)
        ada_w = region("ada_w", 16408, 2, 4096)
        sq = region("sq", 24600, 2, 512)
        rms = region("rms", 25624, 2, 512)
        tmp = region("tmp", 26648, 2, 512)
        rinv = region("rinv", 27672, 1, 512)[:, 0, :]
        lru_q = region("lru_q", 28184, 1, 512)[:, 0, :]
        bd_r = region("bd_r", 28696, 4, P)
        bd_i = region("bd_i", 29208, 4, P)
        iota_i = region("iota_i", 29720, 1, P, dt=mybir.dt.int32)[:, 0, :]
        halves = region("halves", 29848, 1, P)[:, 0, :]
        ba_w = region("ba_w", 29976, 1, 64)[:, 0, :]
        S = region("S", 0, TB * HEADS * 2, N_KEYS)
        stage_w = region("stage_w", 0, 2, N_KEYS * WT)
        qT = region("qT", 8192, HEADS, T)
        hot_i = region("hot_i", 8192, ONEHOT, P)
        hot_j = region("hot_j", 8192 + ONEHOT * P, ONEHOT, P)
        keys = region("keys", 12288, HEADS, 256)
        gel = region("gel", 12288, 2, 1024)
        cand = region("cand", 14336, HEADS, 256)
        eq = region("eq", 16384, 2048, 1)[:, :, 0]
        rep = region("rep", 18432, 1, 256)[:, 0, :]
        topv = region("topv", 18688, 16, TOPK)
        topi = region("topi", 18944, 16, TOPK, dt=U32)
        topf = region("topf", 19200, 16, TOPK)
        bestv = region("bestv", 19456, HEADS, TOPK)
        bestp = region("bestp", 19584, HEADS, TOPK, dt=U32)
        pick = region("pick", 19712, 2, 128, dt=U32)
        pickf = region("pickf", 19968, 2, 128)
        zs = region("zs", 20224, 2, 8)
        routed_sb = [region(f"routed{i}", 20240 + 384 * i, 3, 128) for i in range(TB)]
        routeT = region("routeT", 21776, 3, T)
        gate_q = region("gate_q", 0, 2, 2048)
        gel_q = region("gel_q", 4096, 2, 2048)
        craw = region("craw", 14336, 2, 512)

        cv = region("cv", 0, 12, T)
        th2 = region("th2", 6144, 2, T)
        AT = region("AT", 6144, TB, 512)
        IT = region("IT", 8192, TB, 512)
        Dm = region("Dm", 10240, TB, 512)
        DTm = region("DTm", 12288, TB, 512)
        M1 = region("M1", 14336, 2, 512)
        AO = region("AO", 15360, 2, 512)
        KB = region("KB", 16384, 2, 512)
        VB = region("VB", 17408, 2, 512)
        aq = region("aq", 18432, 4, T)
        ak = region("ak", 20480, 4, T)
        av = region("av", 22528, 4, T)
        masks = region("masks", 28184, LEVELS, P)
        ND = region("ND", 29080, 1, 512)[:, 0, :]
        state = region("state", 29592, 1, 512)[:, 0, :]
        cin = region("cin", 30104, 2, 516)
        az = region("az", 16384, 4, T)
        avt = region("avt", 6144, TB, 512)
        dz = region("dz", 10240, 4, T)
        L = region("L", 12288, 3, 512)
        PT = region("PT", 14336, 2, 512)
        mx = region("mx", 0, KC, T)
        small2 = sb("small2", [P, 464])
        ba_hi = sb("ba_hi", [P, KC, 8], F32R)
        ba_lo = sb("ba_lo", [P, KC, 8], F32R)

        def cols2(at, n):
            return small2[:, at:at + n]

        ba = cols2(0, 32)
        beta, dx, dax, dexp, dz_, dt1, dt2, dacc, rate = (cols2(32 + 16 * i, 16) for i in range(9))
        gcum = cols2(176, 48)
        egcum = cols2(224, 48)
        ngc = cols2(272, 16)
        bge = cols2(288, 16)
        ealog = cols2(304, 4)
        nmax = cols2(320, 32)
        psum_ = cols2(352, 32)
        prec = cols2(384, 32)
        hc2w = cols2(416, 48)

        def h4(ap):
            return ap.rearrange("p (h n) -> p h n", h=GH)

        def dram(name, shape):
            return nc.dram_tensor(name, shape, F32).ap()

        gates_d = dram("gates_d", [N_KEYS // QUAD, P, T // WT, QUAD * WT])
        gel_d = dram("gel_d", [N_KEYS // QUAD, P, QUAD, T])

        consts_in = sem("consts_in")
        x_in = sem("x_in")
        ada_in = [sem("ada_in0"), sem("ada_in1")]
        keys_in = sem("keys_in")
        blocks_in = sem("blocks_in")
        raw_in = [sem(f"raw_in{i}") for i in range(RAW)]
        pool_made = sem("pool_made")
        pool_chain = sem("pool_chain")
        hi_split = sem("hi_split")
        lo_split = sem("lo_split")
        unit_done = sem("unit_done")
        ada_done = sem("ada_done")
        sq_ready = sem("sq_ready")
        sq_used = sem("sq_used")
        sum_ready = sem("sum_ready")
        rms_ready = sem("rms_ready")
        rinv_ready = sem("rinv_ready")
        tmp_ready = sem("tmp_ready")
        ahi_ready = sem("ahi_ready")
        alo_ready = sem("alo_ready")
        c_tanh = sem("c_tanh")
        c_ready = sem("c_ready")
        dve_chain = sem("dve_chain")
        act_chain = sem("act_chain")
        z_act = sem("z_act")
        z_dve = sem("z_dve")
        xc_ready = sem("xc_ready")
        gates_ps = sem("gates_ps")
        gates_th = sem("gates_th")
        lam_exp = sem("lam_exp")
        lam_neg = sem("lam_neg")
        dec_ready = sem("dec_ready")
        s_ready = sem("s_ready")
        s_used = sem("s_used")
        root_ready = sem("root_ready")
        y_ready = sem("y_ready")
        yb_ready = sem("yb_ready")
        x_ready = sem("x_ready")
        q_sb = sem("q_sb")
        score_ps = sem("score_ps")
        score_sb = sem("score_sb")
        ex_in = sem("ex_in")
        ex_out = sem("ex_out")
        routed_ready = sem("routed_ready")
        route_ps = sem("route_ps")
        route_sb = sem("route_sb")
        gelu_done = sem("gelu_done")
        gel_st = [sem("gel_st0"), sem("gel_st1")]
        hot_ready = sem("hot_ready")
        gate_ps = sem("gate_ps")
        gate_sb = sem("gate_sb")
        gate_st = [sem("gate_st0"), sem("gate_st1")]
        gq_in = [sem("gq_in0"), sem("gq_in1")]
        eq_in = [sem("eq_in0"), sem("eq_in1")]
        craw_ready = sem("craw_ready")
        chi_ready = sem("chi_ready")
        clo_ready = sem("clo_ready")
        done_out = sem("done_out")
        bank_full = [sem(f"bank_full{b}") for b in range(2, 6)]
        bank_free = [sem(f"bank_free{b}") for b in range(2, 6)]
        pads_ready = sem("pads_ready")
        ba_in = sem("ba_in")
        ba_hi_r = sem("ba_hi_ready")
        ba_lo_r = sem("ba_lo_ready")
        p_act = sem("p_act")
        p_dve = sem("p_dve")
        conv_done = sem("conv_done")
        th_ready = sem("th_ready")
        cv_ready = sem("cv_ready")
        norm_ready = sem("norm_ready")
        ba_sb = sem("ba_sb")
        rate_in = sem("rate_in")
        rate_out = sem("rate_out")
        rate_ready = sem("rate_ready")
        cum_in = sem("cum_in")
        cum_out = sem("cum_out")
        rows_in = sem("rows_in")
        dl_ready = sem("dl_ready")
        dt_ready = sem("dt_ready")
        eg_ready = sem("eg_ready")
        at_ready = sem("at_ready")
        ao_ready = sem("ao_ready")
        m1_ready = sem("m1_ready")
        d_ready = sem("d_ready")
        tok_dve = sem("tok_dve")
        tok_act = sem("tok_act")
        wu_ready = sem("wu_ready")
        vn_ready = sem("vn_ready")
        o_ready = sem("o_ready")
        state_ready = sem("state_ready")
        avt_ready = sem("avt_ready")
        z_th = sem("z_th")
        l_ready = sem("l_ready")
        nm_ready = sem("nm_ready")
        e_ready = sem("e_ready")
        p_ready = sem("p_ready")
        pt_ready = sem("pt_ready")
        om_ready = sem("om_ready")
        pv_done = sem("pv_done")
        kd_chain = sem("kd_chain")
        mx_ready = sem("mx_ready")
        out_ready = sem("out_ready")

        def bank(*name):
            return 2 + JOBS[name] % 4

        def wait_full(eng, *name):
            n = JOBS[name]
            eng.wait_ge(bank_full[n % 4], n // 4 + 1)

        def wait_free(eng, *name):
            n = JOBS[name]
            if n >= 4:
                eng.wait_ge(bank_free[n % 4], sum(READERS[n % 4:n:4]))

        def full(ins, *name):
            ins.then_inc(bank_full[JOBS[name] % 4], 1)

        def freed(ins, *name):
            ins.then_inc(bank_free[JOBS[name] % 4], 1)

        block = ctx.enter_context(nc.Block())
        NQ = N_KEYS // QUAD
        HALF = N_KEYS // 2

        def z_of(u):
            if u < 4:
                return "xr", u
            if u < 8:
                return "gr", u - 4
            return ("xa", "gc", "gb")[(u - 8) % 3], (u - 8) // 3

        @block.sync
        def _(sp_):
            def unit(u, src):
                if u >= RAW:
                    sp_.wait_ge(lo_split, u - RAW + 1)
                sp_.dma_start(raw[:, u % RAW, :], src).then_inc(raw_in[u % RAW], 16)

            def ada_half(h):
                if h >= 2:
                    sp_.wait_ge(ada_done, h - 1)
                sp_.dma_start(ada_w[:, h % 2, :], A["w_ada"][h]).then_inc(ada_in[h % 2], 16)

            sp_.dma_start(xres[:, :, :], A["x"].rearrange("(c p) t -> p c t", p=P)).then_inc(x_in, 16)
            sp_.dma_start(cols[:, :], A["cols"]).then_inc(consts_in, 16)
            sp_.dma_start(ba_w, A["w_ba"]).then_inc(ba_in, 16)
            for h in range(2):
                ada_half(h)
            for u in range(RAW):
                unit(u, A["w_in"][u])
            for h in range(2, 6):
                ada_half(h)
            sp_.wait_ge(pool_made, 2)
            for h in range(8):
                lo = 64 * (h % 2)
                for bd, w in ((bd_r, "w_r"), (bd_i, "w_i")):
                    sp_.dma_start(bd[lo:lo + 64, h // 2, lo:lo + 64], A[w][h]).then_inc(blocks_in, 16)
            for u in range(RAW, 20):
                unit(u, A["w_in"][u])
                h = (u + 8) // 2
                if u % 2 == 0 and 6 <= h < 12:
                    ada_half(h)
            for u in range(U_OUT, U_Q):
                unit(u, A["w_out"][u - U_OUT])
            for u in range(U_Q, U_EU):
                unit(u, A["w_q"][u - U_Q])
            sp_.wait_ge(pool_made, 3)
            for c in range(2):
                sp_.dma_start(keys[64 * c:64 * c + 64, :, P * c:P * c + P], A["keys"][c]).then_inc(keys_in, 16)
            with sp_.Fori(0, N_KEYS // RAW) as r:
                for k in range(RAW):
                    sp_.wait_ge(lo_split, r * RAW + (U_EU + k - RAW + 1))
                    sp_.dma_start(raw[:, k, :], A["expert_u"][bass.ds(r * RAW + k, 1)].rearrange("a p n -> (a p) n")
                                  ).then_inc(raw_in[k], 16)
            for k in range(RAW):
                unit(U_EV + k, A["expert_v"][k])
            for b in range(2):
                sp_.wait_ge(gate_st[b], 16 * (T // WT // 2))
                sp_.wait_ge(gel_st[b], 16 * (N_KEYS // 4))

            def quad(i, b):
                sp_.dma_start(gate_q[:, b, :], gates_d[i].rearrange("a p c n -> (a p) (c n)") if not isinstance(i, int)
                              else gates_d[i].rearrange("p c n -> p (c n)")).then_inc(gq_in[b], 16)
                sp_.dma_start(gel_q[:, b, :], gel_d[i].rearrange("a p c n -> (a p) (c n)") if not isinstance(i, int)
                              else gel_d[i].rearrange("p c n -> p (c n)")).then_inc(eq_in[b], 16)

            quad(0, 0)
            quad(1, 1)
            with sp_.Fori(0, NQ // 2 - 1) as r:
                for b in range(2):
                    for k in range(QUAD):
                        sp_.wait_ge(lo_split, r * 8 + (U_EV + 4 * b + k + 1))
                        sp_.dma_start(raw[:, k, :], A["expert_v"][bass.ds(r * 8 + (4 * b + k + 4), 1)].rearrange(
                            "a p n -> (a p) n")).then_inc(raw_in[k], 16)
                    sp_.wait_ge(craw_ready, r * 8 + 4 * (b + 1))
                    quad(bass.ds(r * 2 + (b + 2), 1), b)
            for k in range(QUAD):
                unit(U_EV + N_KEYS - QUAD + k, A["expert_v"][N_KEYS - QUAD + k])
            for w in range(32):
                unit(U_IN2 + w, A["w_in2"][w])
            for w in range(8):
                unit(U_OUT2 + w, A["w_out2"][w])
            for c in range(KC):
                sp_.wait_ge(out_ready, c + 1)
                sp_.dma_start(out[c * P:(c + 1) * P, :], xres[:, c, :]).then_inc(done_out, 16)
            sp_.wait_ge(done_out, 16 * KC)

        @block.gpsimd
        def _(pool):
            chain = Chain(pool, pool_chain)
            chain.post(pool.memset(small[:, 0:8], EPS))
            chain.post(pool.memset(ones[:, :], 1.0))
            chain.post(pool.memset(ident[:, :], 0.0))
            chain.post(pool.memset(upper[:, :], 1.0))
            chain.post(pool.memset(halves[:, :], 1.0))
            chain.post(pool.memset(bd_r[:, :, :], 0.0))
            chain.post(pool.memset(bd_i[:, :, :], 0.0))
            for m in range(4):
                chain.post(pool.memset(xrp[:, m, 0:4], 0.0))
            for b in range(2):
                chain.post(pool.memset(pc[:, b, 0:4], 0.0))
            chain.post(pool.iota(iota_i[:, :], [[1, P]], base=0, channel_multiplier=0))
            chain.wait()
            chain.post(pool.tensor_copy(iota[:, :], iota_i[:, :]))
            chain.post(pool.affine_select(out=ident[:, :], in_=ident[:, :], compare_op=ALU.not_equal, fill=1.0,
                                          base=0, pattern=[[-1, P]], channel_multiplier=1))
            chain.post(pool.affine_select(out=upper[:, :], in_=upper[:, :], compare_op=ALU.is_ge, fill=0.0,
                                          base=0, pattern=[[1, P]], channel_multiplier=-1))
            chain.post(pool.affine_select(out=halves[:, 0:64], in_=halves[:, 0:64], compare_op=ALU.is_ge, fill=0.0,
                                          base=63, pattern=[[0, 64]], channel_multiplier=-1))
            chain.post(pool.affine_select(out=halves[:, 64:128], in_=halves[:, 64:128], compare_op=ALU.is_ge, fill=0.0,
                                          base=-64, pattern=[[0, 64]], channel_multiplier=1))
            chain.wait()
            pool.nop().then_inc(pool_made, 2)

            def lower(u, k, r=None):
                at = (lambda v: v) if r is None else (lambda v: r + v)
                pool.wait_ge(hi_split, at(u + 1))
                pool.tensor_tensor(w_lo[:, k % SPLIT, :], raw[:, k % RAW, :], w_hi[:, k % SPLIT, :].bitcast(F32),
                                   ALU.subtract).then_inc(lo_split, 1)

            for u in range(U_Q):
                lower(u, u)
            pool.wait_ge(y_ready, 8)
            pool.wait_ge(ahi_ready, 17)
            pool.memset(keys[:, :, :], 0.0).then_inc(pool_made, 1)
            for u in range(U_Q, U_EU):
                lower(u, u)
            chain.link(pool.iota(iota_i[:, :], [[1, P]], base=0, channel_multiplier=-1))
            for n in range(4):
                chain.post(pool.tensor_copy(ND[:, n * P:(n + 1) * P], iota_i[:, :]))
            chain.wait()
            for n in range(3):
                chain.post(pool.tensor_scalar(ND[:, n * P:(n + 1) * P], ND[:, n * P:(n + 1) * P],
                                              float(P * (n - 3)), 0.0, ALU.add, ALU.add))
            chain.post(pool.affine_select(out=ND[:, 384:512], in_=ND[:, 384:512], compare_op=ALU.is_ge, fill=-1.0e32,
                                          base=0, pattern=[[-1, P]], channel_multiplier=1))
            chain.link(pool.memset(masks[:, :, :], 0.0))
            for n in range(LEVELS):
                b = 1 << n
                odd = masks[:, n, :].rearrange("p (m e r) -> p m e r", e=2, r=b)[:, :, 1, :]
                chain.link(pool.memset(odd, 1.0))
                chain.link(pool.affine_select(out=odd, in_=odd, compare_op=ALU.is_ge, fill=0.0, base=0,
                                              pattern=[[-2 * b, P // (2 * b)], [0, b]], channel_multiplier=1))
                chain.link(pool.affine_select(out=odd, in_=odd, compare_op=ALU.is_ge, fill=0.0, base=b - 1,
                                              pattern=[[2 * b, P // (2 * b)], [0, b]], channel_multiplier=-1))
            pool.nop().then_inc(pool_made, 1)
            with pool.Fori(0, (U_IN2 - U_EU) // RAW) as r:
                for k in range(RAW):
                    lower(U_EU + k, k, r * RAW)
            for u in range(U_IN2, U_END):
                lower(u, u)

        @block.tensor
        def _(pe):
            def linear(u, k, bank, r=None):
                pe.wait_ge(lo_split, u + 1 if r is None else r + (u + 1))
                for c in range(KC):
                    for n, (w, x) in enumerate(((w_hi, act_hi), (w_lo, act_hi), (w_hi, act_lo))):
                        mm = pe.matmul(PS[:, bank, :], w[:, k % SPLIT, c * P:(c + 1) * P], x[:, c, :],
                                       start=(c == 0 and n == 0), stop=(c == KC - 1 and n == 2))
                mm.then_inc(unit_done, 1)

            def squares(first, count, index, mat):
                if index >= 2:
                    pe.wait_ge(rms_ready, index - 1)
                for c in range(count):
                    pe.wait_ge(sq_ready, first + c + 1)
                    mm = pe.matmul(PS[:, 6 + index % 2, :], mat[:, :], sq[:, (first + c) % 2, :],
                                   start=(c == 0), stop=(c == count - 1))
                    mm.then_inc(sq_used, 1)
                pe.wait_ge(sq_used, first + count)
                pe.nop().then_inc(sum_ready, 1)

            def ada_half(h):
                pe.wait_ge(ada_in[h % 2], 16 * (h // 2 + 1))
                w = ada_w[:, h % 2, :].rearrange("p (c n) -> p c n", c=KC)
                for n in range(4):
                    for c in range(KC):
                        mm = pe.matmul(PS[:, 5, 4 * h + n:4 * h + n + 1], w[:, c, n * P:(n + 1) * P], cs[:, c:c + 1],
                                       start=(c == 0), stop=(c == KC - 1))
                mm.then_inc(ada_done, 1)

            pe.wait_ge(pool_made, 2)
            squares(0, 8, 0, ones)
            pe.wait_ge(c_ready, 1)
            for h in range(4):
                ada_half(h)
            pe.wait_ge(alo_ready, 8)
            for u in range(U_OUT):
                kind, m = z_of(u)
                if 3 <= u < 11:
                    pe.wait_ge(z_act, u - 2)
                elif u >= 11:
                    if kind == "xa":
                        pe.wait_ge(z_act, 8 + m)
                    else:
                        pe.wait_ge(z_dve, 2 * m - (1 if kind == "gc" else 0))
                linear(u, u, u % 3)
                if u % 2 == 1 and (u - 1) // 2 < 8:
                    ada_half(4 + (u - 1) // 2)
                if 7 <= u < 11:
                    g = u - 7
                    pe.wait_ge(xc_ready, g + 1)
                    if g == 0:
                        pe.wait_ge(blocks_in, 16 * 16)
                    if g >= 1:
                        pe.wait_ge(gates_th, 2 * g)
                    pe.matmul(PS[:, 3, :], bd_r[:, g, :], xc[:, g, :], start=True, stop=True)
                    pe.matmul(PS[:, 4, :], bd_i[:, g, :], xc[:, g, :], start=True, stop=True).then_inc(gates_ps, 1)
            for c in range(8):
                squares(8 + c, 1, 1 + c, halves)
            pe.wait_ge(alo_ready, 16)
            for c in range(8):
                u = U_OUT + c
                if c < 3:
                    pe.wait_ge(z_dve, 8)
                    pe.wait_ge(z_act, 12)
                else:
                    pe.wait_ge(x_ready, c - 2)
                linear(u, u, u % 3)
            squares(16, 8, 9, ones)
            pe.wait_ge(alo_ready, 24)
            for c in range(8):
                if c < 3:
                    pe.wait_ge(x_ready, 8)
                else:
                    pe.wait_ge(q_sb, c - 2)
                linear(U_Q + c, U_Q + c, (U_Q + c) % 3)
            pe.wait_ge(q_sb, 8)
            pe.wait_ge(keys_in, 32)
            for n in range(TB * 4):
                tb, hp = n // 4, n % 4
                if n >= 2:
                    pe.wait_ge(score_sb, n - 1)
                for e in range(2):
                    mm = pe.matmul(PS[:, 3 + n % 2, 256 * e:256 * e + 256], qT[:, 2 * hp + e, tb * P:(tb + 1) * P],
                                   keys[:, 2 * hp + e, :], start=True, stop=True)
                mm.then_inc(score_ps, 1)
            pe.wait_ge(q_sb, 8)
            for k in range(2):
                linear(U_EU + k, k, k)
            with pe.Fori(0, (HALF - 2) // 2) as r:
                for k in range(2):
                    pe.wait_ge(gelu_done, r * 2 + (k + 1))
                    linear(U_EU + 2 + k, k, k, r * 2)
            for tb in range(TB):
                pe.wait_ge(routed_ready, tb + 1)
                if tb:
                    pe.wait_ge(route_sb, tb)
                for n in range(3):
                    mm = pe.transpose(PS[:, 2, n * P:(n + 1) * P], routed_sb[tb][:, n, :], ident[:, :])
                mm.then_inc(route_ps, 1)
            pe.wait_ge(route_sb, TB)

            def gate_group(g, k, r=None, first=False):
                at = (lambda v: v) if r is None else (lambda v: r + v)
                if not first:
                    pe.wait_ge(gate_sb, at(g - 3))
                pe.wait_ge(hot_ready, at(g + 1))
                for t in range(GROUP):
                    s = (GROUP * k + t) % ONEHOT
                    mm = pe.matmul(PS[:, 2 + k % 4, t * P:(t + 1) * P], hot_i[:, s, :], hot_j[:, s, :],
                                   start=True, stop=True)
                mm.then_inc(gate_ps, 1)

            def both(k, r_u, r_g, first=False):
                at = HALF + k
                pe.wait_ge(gelu_done, at - 1 if r_u is None else r_u + (at - 1))
                linear(U_EU + at, k, k % 2, r_u)
                for g in (2 * k, 2 * k + 1):
                    gate_group(g, g, r_g, first and g < 4)

            for k in range(8):
                both(k, None, None, True)
            with pe.Fori(0, HALF // 8 - 1) as r:
                for k in range(8):
                    both(8 + k, r * 8, r * 16)

            def experts(b, k, r=None, start=False, stop=False):
                at = (lambda v: v) if r is None else (lambda v: r + v)
                pe.wait_ge(lo_split, at(U_EV + b + 1))
                pe.wait_ge(clo_ready, at(b + 1))
                for c in range(KC):
                    for n, (w, x) in enumerate(((w_hi, act_hi), (w_lo, act_hi), (w_hi, act_lo))):
                        mm = pe.matmul(PS[:, c, :], w[:, k % SPLIT, c * P:(c + 1) * P], x[:, k % 2, :],
                                       start=(start and n == 0), stop=(stop and n == 2), skip_group_check=True)
                mm.then_inc(unit_done, 1)

            pe.wait_ge(gelu_done, N_KEYS)
            pe.wait_ge(gate_sb, T // GROUP)
            experts(0, 0, start=True)
            experts(1, 1)
            with pe.Fori(0, N_KEYS // 2 - 2) as r:
                for k in range(2):
                    experts(2 + k, k, r * 2)
            experts(N_KEYS - 2, 0)
            experts(N_KEYS - 1, 1, stop=True)
            pe.wait_ge(x_ready, 16)
            squares(24, 8, 10, ones)
            squares(32, 8, 11, ones)
            pe.wait_ge(alo_ready, 32)
            pe.wait_ge(pool_made, 4)

            def heads(name, lhs, rhs, at=None):
                b = bank(*name)
                wait_free(pe, *name)
                for h in range(GH):
                    mm = pe.matmul(PS[:, b, h * P:(h + 1) * P], lhs(h), rhs(h), start=True, stop=True)
                full(mm, *name)

            def turned(name, src, n=4):
                b = bank(*name)
                wait_free(pe, *name)
                for h in range(n):
                    mm = pe.transpose(PS[:, b, h * P:(h + 1) * P], src(h), ident[:, :])
                full(mm, *name)

            for st in STEPS2:
                kind, n, tb = st[0], st[1], st[-1]
                t = slice(tb * P, (tb + 1) * P)
                if kind == "unit":
                    if n == 32:
                        pe.wait_ge(alo_ready, 40)
                    if 2 <= n < 26:
                        pe.wait_ge(p_act, n - 1)
                    elif 26 <= n < 34:
                        pe.wait_ge(p_dve, n - 25)
                        if n >= 32:
                            pe.wait_ge(om_ready, 3 + n - 32)
                    elif n >= 34:
                        pe.wait_ge(mx_ready, n - 33)
                    linear(U_IN2 + n, n, n % 2)
                if kind == "rates":
                    pe.wait_ge(ba_lo_r, 1)
                    wait_free(pe, "ba")
                    for q in range(TB):
                        for c in range(KC):
                            for i, (x, w) in enumerate(((act_hi, ba_hi), (act_hi, ba_lo), (act_lo, ba_hi))):
                                mm = pe.matmul(PS[:, bank("ba"), 8 * q:8 * q + 8], x[:, c, q * P:(q + 1) * P], w[:, c, :],
                                               start=(c == 0 and i == 0), stop=(c == KC - 1 and i == 2))
                    full(mm, "ba")
                if kind == "l2":
                    squares(40 + n, 1, 12 + n, ones)
                if kind == "cumulate":
                    pe.wait_ge(rate_ready, 1)
                    wait_free(pe, "cum")
                    pe.matmul(PS[:, bank("cum"), 0:16], upper[:, :], rate, start=True, stop=True)
                    full(pe.matmul(PS[:, bank("cum"), 16:32], ones[:, :], rate, start=True, stop=True), "cum")
                if kind == "decay":
                    pe.wait_ge(rows_in, tb + 1)
                    for name, src in (("gcr", 0), ("br", 1)):
                        wait_free(pe, name, tb)
                        full(pe.matmul(PS[:, bank(name, tb), :], ones[:, :], M1[:, src, :], start=True, stop=True), name, tb)
                    pe.wait_ge(norm_ready, 8)
                    heads(("kk", tb), lambda h: cv[:, 4 + h, t], lambda h: cv[:, 4 + h, t])
                    heads(("qk", tb), lambda h: cv[:, 4 + h, t], lambda h: cv[:, h, t])
                if kind == "M":
                    pe.wait_ge(ao_ready, 4 * n + tb + 1)
                    pe.wait_ge(d_ready, 4 * n + tb + 1)
                    heads(("m", n, tb), lambda h: h4(AO[:, tb % 2, :])[:, h, :], lambda h: h4(Dm[:, tb, :])[:, h, :])
                if kind == "X":
                    pe.wait_ge(m1_ready, 4 * n + tb + 1)
                    if n < LEVELS - 1:
                        heads(("x", n, tb), lambda h: h4(DTm[:, tb, :])[:, h, :], lambda h: h4(M1[:, tb % 2, :])[:, h, :])
                    heads(("xt", n, tb), lambda h: h4(M1[:, tb % 2, :])[:, h, :], lambda h: h4(DTm[:, tb, :])[:, h, :])
                if kind == "tokens":
                    turned(("kt", tb), lambda h: cv[:, 4 + h, t])
                    pe.wait_ge(cv_ready, 12)
                    turned(("vt", tb), lambda h: cv[:, 8 + h, t])
                if kind == "solve":
                    pe.wait_ge(tok_dve, tb + 1)
                    pe.wait_ge(d_ready, 4 * LEVELS + tb + 1)
                    heads(("wt", tb), lambda h: h4(KB[:, tb % 2, :])[:, h, :], lambda h: h4(DTm[:, tb, :])[:, h, :])
                    heads(("u", tb), lambda h: h4(DTm[:, tb, :])[:, h, :], lambda h: h4(VB[:, tb % 2, :])[:, h, :])
                if kind == "scan":
                    pe.wait_ge(wu_ready, tb + 1)
                    if tb:
                        pe.wait_ge(state_ready, tb)
                        heads(("ws", tb), lambda h: h4(Dm[:, tb, :])[:, h, :], lambda h: h4(state)[:, h, :])
                        pe.wait_ge(vn_ready, tb)
                    else:
                        pe.wait_ge(at_ready, TB)
                    vn = M1[:, tb % 2, :] if tb else AT[:, 0, :]
                    wait_free(pe, "o", tb)
                    for h in range(GH):
                        o = PS[:, bank("o", tb), h * P:(h + 1) * P]
                        if tb:
                            pe.matmul(o, h4(state)[:, h, :], cv[:, h, t], start=True, stop=False)
                        mm = pe.matmul(o, h4(vn)[:, h, :], h4(IT[:, tb, :])[:, h, :], start=(tb == 0), stop=True)
                    full(mm, "o", tb)
                    if tb < TB - 1:
                        pe.wait_ge(tok_act, tb + 1)
                        heads(("su", tb), lambda h: cv[:, 4 + h, t], lambda h: h4(vn)[:, h, :])
                if kind == "values":
                    pe.wait_ge(p_act, 24)
                    turned(("av", tb), lambda m: av[:, m, t])
                if kind == "gdn_out":
                    squares(48 + n, 1, 20 + n, ones)
                if kind == "logits":
                    m, e, qb = n // 8, n // 4 % 2, n % 4
                    wait_free(pe, "s", n)
                    s64 = slice(64 * e, 64 * e + 64)
                    full(pe.matmul(PS[:, bank("s", n), 0:(qb + 1) * P], aq[s64, m, qb * P:(qb + 1) * P],
                                   ak[s64, m, 0:(qb + 1) * P], start=True, stop=True), "s", n)
                if kind == "pv":
                    m, e, qb = n // 8, n // 4 % 2, n % 4
                    pe.wait_ge(p_ready, n + 1)
                    turned(("pt", n), lambda kb: L[:, n % 3, kb * P:(kb + 1) * P], qb + 1)
                    if n == 0:
                        pe.wait_ge(p_dve, 8)
                        pe.wait_ge(avt_ready, TB)
                    if n % 8 == 0 and m >= 2:
                        pe.wait_ge(om_ready, m - 1)
                    pe.wait_ge(pt_ready, n + 1)
                    for kb in range(qb + 1):
                        mm = pe.matmul(PS[64 * e:64 * e + 64, m % 2, qb * P:(qb + 1) * P],
                                       avt[:, kb, P * m + 64 * e:P * m + 64 * e + 64], PT[:, n % 2, kb * P:(kb + 1) * P],
                                       start=(kb == 0), stop=(kb == qb))
                    mm.then_inc(pv_done, 1)
            squares(52, 8, 24, ones)

        @block.scalar
        def _(act):
            chain = Chain(act, act_chain)

            def upper_part(u, k, r=None):
                at = (lambda v: v) if r is None else (lambda v: r + v)
                if r is None:
                    act.wait_ge(raw_in[k % RAW], 16 * (u // RAW + 1))
                else:
                    act.wait_ge(raw_in[k % RAW], r * (16 // RAW) + 16 * (u // RAW + 1))
                if r is not None or u >= SPLIT:
                    act.wait_ge(unit_done, at(u - SPLIT + 1))
                act.activation(w_hi[:, k % SPLIT, :], raw[:, k % RAW, :], ACT.Copy).then_inc(hi_split, 1)

            def square(n, src):
                if n >= 2:
                    act.wait_ge(sq_used, n - 1)
                act.activation(sq[:, n % 2, :], src, ACT.Square).then_inc(sq_ready, 1)

            def root(index, width):
                act.wait_ge(sum_ready, index + 1)
                if index >= 2:
                    act.wait_ge(rinv_ready, index - 1)
                act.activation(rms[:, index % 2, :], PS[:, 6 + index % 2, :], ACT.Sqrt, bias=eps,
                               scale=1.0 / width).then_inc(rms_ready, 1)

            def operand(n, shift=None, chunk=None):
                act.wait_ge(tmp_ready, n + 1)
                if shift is None:
                    act.activation(act_hi[:, n % 8 if chunk is None else chunk, :], tmp[:, n % 2, :], ACT.Copy).then_inc(ahi_ready, 1)
                else:
                    act.activation(act_hi[:, n % 8 if chunk is None else chunk, :], tmp[:, n % 2, :], ACT.Identity, bias=shift).then_inc(ahi_ready, 1)

            act.wait_ge(consts_in, 16)
            act.activation(cth, col("c", 0, 8), ACT.Tanh, scale=0.5).then_inc(c_tanh, 1)
            act.wait_ge(ba_in, 16)
            act.activation(ba_hi[:, :, :].rearrange("p c n -> p (c n)"), ba_w[:, :], ACT.Copy).then_inc(ba_hi_r, 1)
            act.wait_ge(lam_neg, 1)
            act.activation(sp[1], sp[0], ACT.Exp, scale=-1.0).then_inc(lam_exp, 1)
            act.wait_ge(x_in, 16)
            for c in range(8):
                square(c, xres[:, c, :])
            act.wait_ge(pool_made, 2)
            root(0, D)
            for u in range(SPLIT):
                upper_part(u, u)
            for c in range(8):
                operand(c, ada[:, c:c + 1])
            for u in range(U_OUT):
                kind, m = z_of(u)
                act.wait_ge(unit_done, u + 1)
                upper_part(u + SPLIT, u + SPLIT)
                if kind == "xr":
                    act.activation(xrp[:, m, 3:515], PS[:, u % 3, :], ACT.Copy).then_inc(z_act, 1)
                if kind == "gr":
                    act.activation(gg[:, m, :], PS[:, u % 3, :], ACT.Gelu).then_inc(z_act, 1)
                if kind == "xa":
                    if m >= 2:
                        act.wait_ge(z_dve, 2 * (m - 2) + 1)
                    act.activation(xa[:, m % 2, :], PS[:, u % 3, :], ACT.Copy).then_inc(z_act, 1)
                if 8 <= u < 12:
                    g = u - 8
                    act.wait_ge(gates_ps, g + 1)
                    act.activation(tr[:, g, :], PS[:, 3, :], ACT.Tanh, bias=hbr[:, g:g + 1], scale=0.5).then_inc(gates_th, 1)
                    act.activation(ti[:, g, :], PS[:, 4, :], ACT.Tanh, bias=hbi[:, g:g + 1], scale=0.5).then_inc(gates_th, 1)
                if u == 12:
                    act.wait_ge(dec_ready, 1)
                    act.wait_ge(gates_th, 8)
                    for g in range(4):
                        act.activation(tr[:, g, :], tr[:, g, :], ACT.Tanh, bias=dec[:, g:g + 1],
                                       scale=dec[:, g:g + 1]).then_inc(s_ready, 1)
                if u == 17:
                    for g in range(4):
                        act.wait_ge(s_used, g + 1)
                        act.activation(tr[:, g, :], tr[:, g, :], ACT.Sqrt, scale=-1.0).then_inc(root_ready, 1)
            for c in range(10):
                if c < 8:
                    act.wait_ge(y_ready, c + 1)
                    square(8 + c, y[:, c, :])
                if 1 <= c < 9:
                    root(c, 64)
                if c >= 2:
                    operand(8 + c - 2)
            for c in range(8):
                act.wait_ge(unit_done, U_OUT + c + 1)
                upper_part(U_OUT + c + SPLIT, U_OUT + c + SPLIT)
            for c in range(8):
                act.wait_ge(x_ready, c + 1)
                square(16 + c, xres[:, c, :])
            root(9, D)
            for c in range(8):
                operand(16 + c, ada[:, 24 + c:25 + c])
            for c in range(8):
                act.wait_ge(unit_done, U_Q + c + 1)
                upper_part(U_Q + c + SPLIT, U_Q + c + SPLIT)
                act.activation(qT[:, c, :], PS[:, (U_Q + c) % 3, :], ACT.Copy).then_inc(q_sb, 1)
            for n in range(TB * 4):
                act.wait_ge(score_ps, n + 1)
                act.activation(S[:, 4 * n:4 * n + 4, :].rearrange("p a b -> p (a b)"), PS[:, 3 + n % 2, :],
                               ACT.Copy).then_inc(score_sb, 1)

            def expert_act(u, k, r=None, first=False):
                at = (lambda v: v) if r is None else (lambda v: r + v)
                act.wait_ge(unit_done, at(U_EU + u + 1))
                upper_part(U_EU + u + SPLIT, k + SPLIT, r)
                b = (k // 2) % 2
                if not first and k % 2 == 0:
                    if r is None:
                        act.wait_ge(gel_st[b], 16 * (u // 4))
                    else:
                        act.wait_ge(gel_st[b], r * 4 + 16 * (u // 4))
                act.activation(gel[:, b, 512 * (k % 2):512 * (k % 2) + 512], PS[:, k % 2, :], ACT.Gelu).then_inc(gelu_done, 1)

            def store_gel(u, k, quad_index, r=None):
                b = (k // 2) % 2
                act.wait_ge(gelu_done, u + 1 if r is None else r + (u + 1))
                dst = gel_d[quad_index]
                dst = dst.rearrange("p c n -> p (c n)") if isinstance(quad_index, int) else \
                    dst.rearrange("a p c n -> (a p) (c n)")
                act.dma_start(dst[:, 1024 * b:1024 * b + 1024], gel[:, b, :]).then_inc(gel_st[b], 16)

            def soft(tb):
                act.wait_ge(ex_in, tb + 1)
                act.activation(bestv[:, :, :], bestv[:, :, :], ACT.Exp).then_inc(ex_out, 1)

            for u in range(4):
                expert_act(u, u, first=True)
                if u % 2:
                    store_gel(u, u, 0)
            per = (HALF - 4) // 4 // 3
            for tb in range(3):
                with act.Fori(0, per) as r:
                    for k in range(4):
                        u = 4 + 4 * per * tb + k
                        expert_act(u, k, r * 4)
                        if k % 2:
                            store_gel(u, k, bass.ds(r + (1 + per * tb), 1), r * 4)
                soft(tb)
            soft(3)
            for tb in range(TB):
                act.wait_ge(route_ps, tb + 1)
                act.activation(routeT[:, :, tb * P:(tb + 1) * P], PS[:, 2, 0:384].rearrange("p (a b) -> p a b", a=3),
                               ACT.Copy).then_inc(route_sb, 1)

            def gate_copy(g, k, b, r=None):
                at = (lambda v: v) if r is None else (lambda v: r + v)
                act.wait_ge(gate_ps, at(g + 1))
                t0 = (GROUP * k) % WT
                act.activation(stage_w[:, b, :].rearrange("p (j t) -> p j t", t=WT)[:, :, t0:t0 + GROUP],
                               PS[:, 2 + k % 4, :].rearrange("p (t j) -> p j t", t=GROUP), ACT.Copy).then_inc(gate_sb, 1)

            def eight(r=None):
                for k in range(8):
                    ru = None if r is None else r * 8
                    rg = None if r is None else r * 16
                    u = HALF + k + (0 if r is None else 8)
                    expert_act(u, k, ru)
                    if k % 2:
                        q0 = HALF // QUAD + k // 4
                        store_gel(u, k, q0 if r is None else bass.ds(r * 2 + (q0 + 2), 1), ru)
                    b = k // 4
                    if r is not None and k % 4 == 0:
                        act.wait_ge(gate_st[b], r * 16 + 16)
                    for g in (2 * k, 2 * k + 1):
                        gate_copy(g + (0 if r is None else 16), g, b, rg)
                    if k % 4 == 3:
                        n = 8 * (b + 1) + (0 if r is None else 16)
                        act.wait_ge(gate_sb, n if r is None else r * 16 + n)
                        if r is None:
                            dst = gates_d[:, :, b, :].rearrange("q p n -> p q n")
                        else:
                            dst = gates_d[:, :, bass.ds(r * 2 + (b + 2), 1), :].rearrange("q p a n -> p q (a n)")
                        act.dma_start(dst, stage_w[:, b, :].rearrange("p (q n) -> p q n", n=QUAD * WT)
                                      ).then_inc(gate_st[b], 16)

            act.wait_ge(routed_ready, TB)
            eight()
            with act.Fori(0, HALF // 8 - 1) as r:
                eight(r)
            with act.Fori(0, N_KEYS // 4 - 1) as r:
                for k in range(4):
                    upper_part(U_EV + 2 + k, k + 2, r * 4)
            for u in range(N_KEYS - 2, N_KEYS + SPLIT):
                upper_part(U_EV + u, u)
            for c in range(8):
                act.wait_ge(x_ready, 8 + c + 1)
                square(24 + c, xres[:, c, :])
            root(10, D)
            for c in range(8):
                act.wait_ge(x_ready, 16 + c + 1)
                square(32 + c, xres[:, c, :])
            root(11, D)
            for c in range(8):
                operand(24 + c)

            def copy(dst, name, sem_=None, scale=1.0):
                wait_full(act, *name)
                act.activation(dst, PS[:, bank(*name), :], ACT.Copy, scale=scale).then_inc(sem_, 1)

            for st in STEPS2:
                kind, n, tb = st[0], st[1], st[-1]
                t = slice(tb * P, (tb + 1) * P)
                if kind == "unit":
                    act.wait_ge(unit_done, U_IN2 + n + 1)
                    if U_IN2 + n + SPLIT < U_END:
                        upper_part(U_IN2 + n + SPLIT, n + SPLIT)
                    if n < 12:
                        if n >= 2:
                            act.wait_ge(conv_done, n - 1)
                        else:
                            act.wait_ge(pads_ready, 1)
                        act.activation(cin[:, n % 2, 3:515], PS[:, n % 2, :], ACT.Copy).then_inc(p_act, 1)
                    elif n < 24:
                        dst = (aq, ak, av)[n // 4 - 3]
                        act.activation(dst[:, n % 4, :], PS[:, n % 2, :], ACT.Copy,
                                       scale=0.125 if n < 16 else 1.0).then_inc(p_act, 1)
                    elif n < 32:
                        if n >= 26:
                            act.wait_ge(p_dve, n - 25)
                        act.activation(AO[:, n % 2, :], PS[:, n % 2, :], ACT.Tanh, scale=0.5).then_inc(z_th, 1)
                    else:
                        act.activation(mx[:, n - 32, :], PS[:, n % 2, :], ACT.Copy).then_inc(mx_ready, 1)
                if kind == "conv" and n >= 1:
                    act.wait_ge(conv_done, n)
                    if n >= 3:
                        act.wait_ge(cv_ready, n - 2)
                    act.activation(th2[:, (n - 1) % 2, :], cv[:, n - 1, :], ACT.Tanh).then_inc(th_ready, 1)
                if kind == "rates":
                    act.wait_ge(ba_sb, 1)
                    b3 = ba.rearrange("p (q n) -> p q n", n=8)
                    act.activation(beta.rearrange("p (q n) -> p q n", n=4), b3[:, :, 0:4], ACT.Tanh, scale=0.5).then_inc(rate_out, 1)
                    act.activation(ealog, col("alog", 0, 4), ACT.Exp).then_inc(rate_out, 1)
                    act.wait_ge(rate_in, 1)
                    act.activation(dexp, dax, ACT.Exp, scale=-1.0).then_inc(rate_out, 1)
                if kind == "l2":
                    act.wait_ge(cv_ready, n + 1)
                    square(40 + n, cv[:, n, :])
                    root(12 + n, 1)
                if kind == "cumulate":
                    act.wait_ge(cum_in, 1)
                    act.activation(egcum, gcum, ACT.Exp).then_inc(cum_out, 1)
                if kind == "decay":
                    wait_full(act, "gcr", tb)
                    if tb:
                        act.wait_ge(at_ready, tb)
                    act.wait_ge(dl_ready, tb + 1)
                    freed(act.activation(AO[:, 1, :], PS[:, bank("gcr", tb), :], ACT.Exp), "gcr", tb)
                    act.activation(AO[:, 0, :], AO[:, 0, :], ACT.Exp).then_inc(dt_ready, 1)
                if kind == "M":
                    wait_full(act, "m", n, tb)
                    if n or tb >= 2:
                        act.wait_ge(d_ready, 4 * n + tb + 3)
                    ins = act.activation(M1[:, tb % 2, :], PS[:, bank("m", n, tb), :], ACT.Copy)
                    ins.then_inc(m1_ready, 1)
                    act.wait_ge(m1_ready, 4 * n + tb + 1)
                    freed(act.nop(), "m", n, tb)
                if kind == "tokens":
                    wait_full(act, "kt", tb)
                    act.wait_ge(tok_dve, tb + 1)
                    for h in range(GH):
                        ins = act.activation(cv[:, 4 + h, t], PS[:, bank("kt", tb), h * P:(h + 1) * P], ACT.Copy,
                                             scale=egcum[:, 32 + 4 * tb + h:33 + 4 * tb + h])
                        ins.then_inc(kd_chain, 1)
                    act.wait_ge(kd_chain, 4 * (tb + 1))
                    freed(act.nop(), "kt", tb)
                    act.nop().then_inc(tok_act, 1)
                if kind == "solve":
                    wait_full(act, "wt", tb)
                    freed(act.activation(Dm[:, tb, :], PS[:, bank("wt", tb), :], ACT.Copy), "wt", tb)
                    wait_full(act, "u", tb)
                    act.activation(AT[:, tb, :], PS[:, bank("u", tb), :], ACT.Copy).then_inc(wu_ready, 1)
                    act.wait_ge(wu_ready, tb + 1)
                    freed(act.nop(), "u", tb)
                if kind == "scan":
                    wait_full(act, "o", tb)
                    act.activation(cv[:, 8:12, t], h4(PS[:, bank("o", tb), :]), ACT.Copy).then_inc(o_ready, 1)
                    act.wait_ge(o_ready, tb + 1)
                    freed(act.nop(), "o", tb)
                if kind == "values":
                    wait_full(act, "av", tb)
                    act.activation(avt[:, tb, :], PS[:, bank("av", tb), :], ACT.Copy).then_inc(avt_ready, 1)
                    act.wait_ge(avt_ready, tb + 1)
                    freed(act.nop(), "av", tb)
                if kind == "gdn_out":
                    act.wait_ge(o_ready, TB)
                    square(48 + n, cv[:, 8 + n, :])
                    root(20 + n, P)
                    if n:
                        operand(32 + n - 1, chunk=4 + n - 1)
                    if n == GH - 1:
                        operand(32 + n, chunk=4 + n)
                if kind == "logits":
                    act.wait_ge(nm_ready, n + 1)
                    w = (n % 4 + 1) * P
                    act.activation(L[:, n % 3, 0:w], L[:, n % 3, 0:w], ACT.Exp, bias=nmax[:, n:n + 1],
                                   accum_out=psum_[:, n:n + 1]).then_inc(e_ready, 1)
                if kind == "pv":
                    w = (n % 4 + 1) * P
                    wait_full(act, "pt", n)
                    if n >= 2:
                        act.wait_ge(pv_done, n - 1)
                    act.activation(PT[:, n % 2, 0:w], PS[:, bank("pt", n), 0:w], ACT.Copy).then_inc(pt_ready, 1)
                    act.wait_ge(pt_ready, n + 1)
                    freed(act.nop(), "pt", n)
                    if n % 8 == 7:
                        operand(36 + n // 8, chunk=n // 8)
            for c in range(8):
                act.wait_ge(mx_ready, c + 1)
                square(52 + c, mx[:, c, :])
            root(24, D)

        @block.vector
        def _(dve):
            chain = Chain(dve, dve_chain)
            v = nc.vector

            def log1p(z, x, t1, t2, acc):
                chain.link(v.tensor_scalar(t1, x, 2.0, None, ALU.add))
                chain.link(v.reciprocal(t2, t1))
                chain.link(v.tensor_tensor(z, x, t2, ALU.mult))
                chain.link(v.tensor_tensor(t1, z, z, ALU.mult))
                chain.link(v.tensor_scalar(acc, t1, 1.0 / 19, 1.0 / 17, ALU.mult, ALU.add))
                for n in range(15, 0, -2):
                    chain.link(v.tensor_tensor(acc, acc, t1, ALU.mult))
                    chain.link(v.tensor_scalar(acc, acc, 1.0 / n, None, ALU.add))
                chain.link(v.tensor_tensor(acc, acc, z, ALU.mult))
                chain.link(v.tensor_scalar(acc, acc, 2.0, None, ALU.mult))

            def invert(index, read=0, by=None):
                dve.wait_ge(rms_ready, index + 1)
                if read:
                    dve.wait_ge(by or tmp_ready, read)
                v.reciprocal(rinv, rms[:, index % 2, :]).then_inc(rinv_ready, 1)
                dve.wait_ge(rinv_ready, index + 1)

            def scaled(n, src, gain):
                v.scalar_tensor_tensor(out=tmp[:, n % 2, :], in0=src, scalar=gain, in1=rinv, op0=ALU.mult,
                                       op1=ALU.mult).then_inc(tmp_ready, 1)

            def rest(n, shift=None, chunk=None):
                dve.wait_ge(tmp_ready, n + 1)
                dve.wait_ge(ahi_ready, n + 1)
                k = n % 8 if chunk is None else chunk
                v.scalar_tensor_tensor(out=act_lo[:, k, :], in0=tmp[:, n % 2, :],
                                       scalar=0.0 if shift is None else shift,
                                       in1=act_hi[:, k, :].bitcast(F32), op0=ALU.add,
                                       op1=ALU.subtract).then_inc(alo_ready, 1)

            def normed(n0, index, gains, shift):
                invert(index, n0)
                for c in range(9):
                    if c < 8:
                        if c >= 2:
                            dve.wait_ge(alo_ready, n0 + c - 1)
                        scaled(n0 + c, xres[:, c, :], gains[:, c:c + 1])
                    if c:
                        rest(n0 + c - 1, None if shift is None else shift[:, c - 1:c])

            dve.wait_ge(consts_in, 16)
            dve.wait_ge(c_tanh, 1)
            chain.link(v.scalar_tensor_tensor(out=cth, in0=cth, scalar=1.0, in1=col("c", 0, 8), op0=ALU.add, op1=ALU.mult))
            v.tensor_scalar(cs, cth, 0.5, None, ALU.mult).then_inc(c_ready, 1)
            lam = col("lam", 0, 4)
            chain.link(v.tensor_scalar(sp[2], lam, -1.0, None, ALU.mult))
            v.tensor_tensor(sp[0], lam, sp[2], ALU.max).then_inc(lam_neg, 1)
            chain.link(v.tensor_scalar(hbr, col("br", 0, 4), 0.5, None, ALU.mult))
            chain.link(v.tensor_scalar(hbi, col("bi", 0, 4), 0.5, None, ALU.mult))
            dve.wait_ge(lam_exp, 1)
            log1p(sp[3], sp[1], sp[4], sp[5], sp[0])
            chain.link(v.tensor_scalar(sp[2], sp[2], 0.0, None, ALU.max))
            chain.link(v.tensor_tensor(sp[2], sp[2], sp[0], ALU.add))
            v.tensor_scalar(dec, sp[2], -2.0, None, ALU.mult).then_inc(dec_ready, 1)
            dve.wait_ge(ba_hi_r, 1)
            v.tensor_tensor(ba_lo[:, :, :].rearrange("p c n -> p (c n)"), ba_w[:, :],
                            ba_hi[:, :, :].rearrange("p c n -> p (c n)").bitcast(F32), ALU.subtract).then_inc(ba_lo_r, 1)
            dve.wait_ge(ada_done, 4)
            chain.link(v.tensor_tensor(ada[:, 0:16], PS[:, 5, 0:16], col("bada", 0, 16), ALU.add))
            chain.link(v.scalar_tensor_tensor(out=gain1, in0=ada[:, 8:16], scalar=1.0, in1=col("n1", 0, 8),
                                              op0=ALU.add, op1=ALU.mult))
            dve.wait_ge(x_in, 16)
            normed(0, 0, gain1, ada[:, 0:8])

            for m in range(4):
                dve.wait_ge(z_act, m + 1)
                if m == 0:
                    dve.wait_ge(pool_made, 2)
                w = [col("cbw", 4 * k + m) for k in range(4)]
                chain.link(v.tensor_scalar(xc[:, m, :], xrp[:, m, 0:512], w[0], col("cbb", m), ALU.mult, ALU.add))
                for k in range(1, 4):
                    ins = v.scalar_tensor_tensor(out=xc[:, m, :], in0=xrp[:, m, k:k + 512], scalar=w[k],
                                                 in1=xc[:, m, :], op0=ALU.mult, op1=ALU.add)
                    if k < 3:
                        chain.link(ins)
                    else:
                        ins.then_inc(xc_ready, 1)

            def recur_1(g):
                dve.wait_ge(s_ready, g + 1)
                if g:
                    dve.wait_ge(s_used, g)
                    chain.wait()
                chain.link(v.tensor_scalar(lru_q, tr[:, g, :], -1.0, 1.0, ALU.mult, ALU.add))
                chain.link(v.reciprocal(lru_q, lru_q))
                chain.link(v.scalar_tensor_tensor(out=ti[:, g, :], in0=ti[:, g, :], scalar=1.0, in1=xc[:, g, :],
                                                  op0=ALU.add, op1=ALU.mult))
                chain.post(v.tensor_tensor(ti[:, g, :], ti[:, g, :], lru_q, ALU.mult))
                v.scalar_tensor_tensor(out=xc[:, g, :], in0=tr[:, g, :], scalar=1.0, in1=lru_q, op0=ALU.add,
                                       op1=ALU.mult).then_inc(s_used, 1)

            def recur_2(g):
                dve.wait_ge(root_ready, g + 1)
                chain.link(v.tensor_tensor(ti[:, g, :], ti[:, g, :], tr[:, g, :], ALU.mult))
                chain.link(v.tensor_tensor_scan(tr[:, g, :], xc[:, g, :], ti[:, g, :], 0.0, ALU.mult, ALU.add))
                v.tensor_tensor(y[:, 4 + g, :], tr[:, g, :], gg[:, g, :], ALU.mult).then_inc(y_ready, 1)

            for u in range(8, U_OUT):
                kind, m = z_of(u)
                if kind == "gc":
                    dve.wait_ge(unit_done, u + 1)
                    dve.wait_ge(z_act, 9 + m)
                    chain.wait()
                    ins = v.tensor_tensor(pc[:, m % 2, 2:514], PS[:, u % 3, :], xa[:, m % 2, :], ALU.mult)
                    ins.then_inc(z_dve, 1)
                    dve.wait_ge(z_dve, 2 * m + 1)
                    w = [col("caw", 4 * k + m) for k in range(3)]
                    chain.link(v.tensor_scalar(y[:, m, :], pc[:, m % 2, 0:512], w[0], None, ALU.mult))
                    for k in range(1, 3):
                        chain.link(v.scalar_tensor_tensor(out=y[:, m, :], in0=pc[:, m % 2, k:k + 512], scalar=w[k],
                                                          in1=y[:, m, :], op0=ALU.mult, op1=ALU.add))
                if kind == "gb":
                    dve.wait_ge(unit_done, u + 1)
                    v.tensor_tensor(y[:, m, :], PS[:, u % 3, :], y[:, m, :], ALU.mult).then_inc(z_dve, 1)
                    dve.wait_ge(z_dve, 2 * m + 2)
                    dve.nop().then_inc(y_ready, 1)
                if 13 <= u < 17:
                    recur_1(u - 13)
            for g in range(4):
                recur_2(g)
            dve.wait_ge(ada_done, 12)
            chain.link(v.tensor_tensor(ada[:, 16:48], PS[:, 5, 16:48], col("bada", 16, 32), ALU.add))
            chain.link(v.scalar_tensor_tensor(out=gain2, in0=ada[:, 32:40], scalar=1.0, in1=col("n2", 0, 8),
                                              op0=ALU.add, op1=ALU.mult))
            dve.wait_ge(unit_done, U_OUT)
            for c in range(9):
                if c < 8:
                    invert(1 + c, 8 + c)
                    if c >= 2:
                        dve.wait_ge(alo_ready, 8 + c - 1)
                    scaled(8 + c, y[:, c, :], col("gn", c))
                    dve.wait_ge(tmp_ready, 8 + c + 1)
                if c:
                    rest(8 + c - 1)
            for c in range(8):
                dve.wait_ge(unit_done, U_OUT + c + 1)
                v.scalar_tensor_tensor(out=xres[:, c, :], in0=PS[:, (U_OUT + c) % 3, :], scalar=ada[:, 16 + c:17 + c],
                                       in1=xres[:, c, :], op0=ALU.mult, op1=ALU.add).then_inc(x_ready, 1)
            dve.wait_ge(x_ready, 8)
            normed(16, 9, gain2, ada[:, 24:32])

            iota16 = iota[:, 0:16]
            for tb in range(TB):
                if tb:
                    chain.wait()
                for h in range(HEADS):
                    if h % 2 == 0:
                        dve.wait_ge(score_sb, 4 * tb + h // 2 + 1)
                    for c in range(2):
                        n = 2 * h + c
                        s = S[:, 16 * tb + n, :]
                        r = rep[:, 128 * c:128 * c + 128]
                        if h:
                            dve.wait_ge(dve_chain, chain.n - 5)
                        chain.link(v.max(topv[:, n, 0:8], s))
                        chain.post(v.max_index(topi[:, n, 0:8], topv[:, n, 0:8], s))
                        chain.link(v.match_replace(r, topv[:, n, 0:8], s, LOWEST))
                        chain.link(v.max(topv[:, n, 8:16], r))
                        chain.post(v.max_index(topi[:, n, 8:16], topv[:, n, 8:16], r))
                chain.wait()
                chain.post(v.tensor_copy(topf[:, :, :], topi[:, :, :]))
                tv = topv[:, :, :].rearrange("p (h c) k -> p h c k", c=2)
                for h in range(HEADS):
                    chain.post(v.tensor_tensor(cand[:, h, :].rearrange("p (a b) -> p a b", a=16),
                                               tv[:, h, 0, :].unsqueeze(2).to_broadcast([P, 16, 16]),
                                               tv[:, h, 1, :].unsqueeze(1).to_broadcast([P, 16, 16]), ALU.add))
                chain.wait()
                for h in range(HEADS):
                    s = cand[:, h, :]
                    chain.link(v.max(bestv[:, h, 0:8], s))
                    chain.post(v.max_index(bestp[:, h, 0:8], bestv[:, h, 0:8], s))
                    if h:
                        dve.wait_ge(dve_chain, chain.n - 2)
                    chain.link(v.match_replace(rep, bestv[:, h, 0:8], s, LOWEST))
                    chain.link(v.max(bestv[:, h, 8:16], rep))
                    chain.post(v.max_index(bestp[:, h, 8:16], bestv[:, h, 8:16], rep))
                chain.wait()
                chain.post(v.tensor_copy(zs[:, 0, :], bestv[:, :, 0]))
                bp = bestp[:, :, :].rearrange("p h k -> p (h k)")
                chain.post(v.tensor_single_scalar(pick[:, 0, :], bp, 4, ALU.logical_shift_right))
                chain.post(v.tensor_single_scalar(pick[:, 1, :], bp, 15, ALU.bitwise_and))
                chain.wait()
                v.tensor_tensor(bestv[:, :, :], bestv[:, :, :], zs[:, 0, :].unsqueeze(2).to_broadcast([P, HEADS, TOPK]),
                                ALU.subtract).then_inc(ex_in, 1)
                chain.link(v.tensor_copy(pickf[:, :, :], pick[:, :, :]))
                tf = topf[:, :, :].rearrange("p (h c) k -> p h c k", c=2)
                for c in range(2):
                    e3 = eq.rearrange("p (n a) -> p n a", a=16)
                    chain.link(v.tensor_tensor(e3, pickf[:, c, :].unsqueeze(2).to_broadcast([P, 128, 16]),
                                               iota16.unsqueeze(1).to_broadcast([P, 128, 16]), ALU.is_equal))
                    for h in range(HEADS):
                        eh = eq[:, 256 * h:256 * h + 256].rearrange("p (n a) -> p n a", a=16)
                        chain.post(v.tensor_tensor(eh, eh, tf[:, h, c, :].unsqueeze(1).to_broadcast([P, 16, 16]), ALU.mult))
                    chain.wait()
                    chain.link(v.tensor_reduce(routed_sb[tb][:, c, :], e3, AX_X, ALU.add))
                dve.wait_ge(ex_out, tb + 1)
                chain.link(v.tensor_reduce(zs[:, 0, :], bestv[:, :, :], AX_X, ALU.add))
                chain.link(v.reciprocal(zs[:, 1, :], zs[:, 0, :]))
                v.tensor_tensor(routed_sb[tb][:, 2, :].rearrange("p (h k) -> p h k", h=HEADS), bestv[:, :, :],
                                zs[:, 1, :].unsqueeze(2).to_broadcast([P, HEADS, TOPK]), ALU.mult).then_inc(routed_ready, 1)
                dve.wait_ge(routed_ready, tb + 1)

            def hot(g, r=None, rt=None, first=False):
                if not first:
                    dve.wait_ge(gate_ps, g - 3 if r is None else r + (g - 3))
                for t in range(GROUP):
                    tok = GROUP * g + t
                    s = tok % ONEHOT
                    at = slice(tok, tok + 1) if r is None else bass.ds(rt + tok, 1)
                    v.tensor_scalar(hot_i[:, s, :], iota[:, :], routeT[:, 0, at], None, ALU.is_equal)
                    ins = v.tensor_scalar(hot_j[:, s, :], iota[:, :], routeT[:, 1, at], routeT[:, 2, at],
                                          ALU.is_equal, ALU.mult)
                ins.then_inc(hot_ready, 1)

            dve.wait_ge(route_sb, TB)
            for g in range(4):
                hot(g, first=True)
            with dve.Fori(0, T // GROUP // 4 - 1) as r:
                for g in range(4):
                    hot(4 + g, r * 4, r * 16)

            def weigh(b, q, kq, r=None, first=False):
                at = (lambda n: n) if r is None else (lambda n: r + n)
                k = b % 2
                if not first:
                    dve.wait_ge(clo_ready, at(b - 1))
                    dve.wait_ge(unit_done, at(U_EV + b - 1))
                g = gate_q[:, q, :].rearrange("p (c j t) -> p c j t", j=QUAD, t=WT)[:, :, kq, :]
                e = gel_q[:, q, 512 * kq:512 * kq + 512].rearrange("p (c t) -> p c t", t=WT)
                v.tensor_tensor(craw[:, k, :].rearrange("p (c t) -> p c t", t=WT), g, e, ALU.mult).then_inc(craw_ready, 1)
                dve.wait_ge(craw_ready, at(b + 1))
                v.tensor_copy(act_hi[:, k, :], craw[:, k, :]).then_inc(chi_ready, 1)
                dve.wait_ge(chi_ready, at(b + 1))
                v.tensor_tensor(act_lo[:, k, :], craw[:, k, :], act_hi[:, k, :].bitcast(F32),
                                ALU.subtract).then_inc(clo_ready, 1)

            dve.wait_ge(unit_done, U_EV)
            dve.wait_ge(gate_ps, T // GROUP)
            for q in range(2):
                dve.wait_ge(gq_in[q], 16)
                dve.wait_ge(eq_in[q], 16)
                for kq in range(QUAD):
                    weigh(4 * q + kq, q, kq, first=(4 * q + kq < 2))
            with dve.Fori(0, NQ // 2 - 1) as r:
                for q in range(2):
                    dve.wait_ge(gq_in[q], r * 16 + 32)
                    dve.wait_ge(eq_in[q], r * 16 + 32)
                    for kq in range(QUAD):
                        weigh(8 + 4 * q + kq, q, kq, r * 8)
            dve.wait_ge(unit_done, U_IN2)
            for c in range(8):
                v.scalar_tensor_tensor(out=xres[:, c, :], in0=PS[:, c, :], scalar=ada[:, 40 + c:41 + c],
                                       in1=xres[:, c, :], op0=ALU.mult, op1=ALU.add).then_inc(x_ready, 1)
            invert(10, 24)
            for c in range(8):
                v.scalar_tensor_tensor(out=xres[:, c, :], in0=xres[:, c, :], scalar=col("fin", c), in1=rinv,
                                       op0=ALU.mult, op1=ALU.mult).then_inc(x_ready, 1)
            v.memset(cin[:, :, 0:4], 0.0).then_inc(pads_ready, 1)
            chain.post(v.tensor_scalar(hc2w, col("c2w", 0, 48), 0.5, None, ALU.mult))
            invert(11, 24, x_ready)
            for c in range(9):
                if c < 8:
                    if c >= 2:
                        dve.wait_ge(alo_ready, 24 + c - 1)
                    scaled(24 + c, xres[:, c, :], col("pre2", c))
                if c:
                    rest(24 + c - 1)

            def per_head(dst, name, scalars, at, ops=(ALU.mult,), second=None, last=None):
                wait_full(dve, *name)
                for h in range(GH):
                    chain.post(v.tensor_scalar(h4(dst)[:, h, :], PS[:, bank(*name), h * P:(h + 1) * P],
                                               scalars[:, at + h:at + h + 1], second, *ops))

            def all_heads(ap):
                return ap.unsqueeze(1).to_broadcast([P, GH, P])

            for st in STEPS2:
                kind, n, tb = st[0], st[1], st[-1]
                t = slice(tb * P, (tb + 1) * P)
                if kind == "conv":
                    if n < 12:
                        dve.wait_ge(p_act, n + 1)
                        w = [hc2w[:, 12 * k + n:12 * k + n + 1] for k in range(4)]
                        chain.wait()
                        chain.link(v.tensor_scalar(cv[:, n, :], cin[:, n % 2, 0:512], w[0], None, ALU.mult))
                        for k in range(1, 4):
                            ins = v.scalar_tensor_tensor(out=cv[:, n, :], in0=cin[:, n % 2, k:k + 512], scalar=w[k],
                                                         in1=cv[:, n, :], op0=ALU.mult, op1=ALU.add)
                            if k < 3:
                                chain.link(ins)
                            else:
                                ins.then_inc(conv_done, 1)
                    if n >= 1:
                        dve.wait_ge(th_ready, n)
                        v.scalar_tensor_tensor(out=cv[:, n - 1, :], in0=th2[:, (n - 1) % 2, :], scalar=1.0,
                                               in1=cv[:, n - 1, :], op0=ALU.add, op1=ALU.mult).then_inc(cv_ready, 1)
                if kind == "unit" and 24 <= n < 32:
                    dve.wait_ge(z_th, n - 23)
                    dst = az[:, n - 24, :] if n < 28 else dz[:, n - 28, :]
                    if n == 28:
                        dve.wait_ge(avt_ready, TB)
                    v.scalar_tensor_tensor(out=dst, in0=AO[:, n % 2, :], scalar=1.0, in1=PS[:, n % 2, :],
                                           op0=ALU.add, op1=ALU.mult).then_inc(p_dve, 1)
                if kind == "rates":
                    wait_full(dve, "ba")
                    freed(v.tensor_copy(ba, PS[:, bank("ba"), 0:32]), "ba")
                    dve.wait_ge(bank_free[JOBS[("ba",)] % 4], 1)
                    dve.nop().then_inc(ba_sb, 1)
                    b3 = ba.rearrange("p (q n) -> p q n", n=8)
                    chain.link(v.tensor_tensor(dx.rearrange("p (q n) -> p q n", n=4), b3[:, :, 4:8],
                                               col("dtb", 0, 4).unsqueeze(1).to_broadcast([P, TB, 4]), ALU.add))
                    chain.link(v.tensor_scalar(dt1, dx, -1.0, None, ALU.mult))
                    v.tensor_tensor(dax, dx, dt1, ALU.max).then_inc(rate_in, 1)
                    dve.wait_ge(rate_in, 1)
                    dve.wait_ge(rate_out, 3)
                    log1p(dz_, dexp, dt1, dt2, dacc)
                    chain.link(v.tensor_scalar(dx, dx, 0.0, None, ALU.max))
                    chain.link(v.tensor_tensor(dacc, dacc, dx, ALU.add))
                    chain.link(v.tensor_tensor(dacc.rearrange("p (q n) -> p q n", n=4), dacc.rearrange("p (q n) -> p q n", n=4),
                                               ealog.unsqueeze(1).to_broadcast([P, TB, 4]), ALU.mult))
                    chain.link(v.tensor_scalar(beta, beta, 0.5, 0.5, ALU.mult, ALU.add))
                    v.tensor_scalar(rate, dacc, -1.0, None, ALU.mult).then_inc(rate_ready, 1)
                    dve.wait_ge(rate_ready, 1)
                if kind == "l2":
                    if n:
                        invert(12 + n, n, norm_ready)
                    else:
                        invert(12, 32)
                    v.scalar_tensor_tensor(out=cv[:, n, :], in0=cv[:, n, :], scalar=float(P) ** -0.5 if n < 4 else 1.0,
                                           in1=rinv, op0=ALU.mult, op1=ALU.mult).then_inc(norm_ready, 1)
                if kind == "cumulate":
                    wait_full(dve, "cum")
                    chain.link(v.tensor_copy(gcum[:, 0:32], PS[:, bank("cum"), 0:32]))
                    freed(dve.nop(), "cum")
                    chain.post(v.tensor_scalar(ngc, gcum[:, 0:16], -1.0, None, ALU.mult))
                    v.tensor_tensor(gcum[:, 32:48], gcum[:, 16:32], gcum[:, 0:16], ALU.subtract).then_inc(cum_in, 1)
                    dve.wait_ge(cum_out, 1)
                    chain.link(v.tensor_tensor(bge, beta, egcum[:, 0:16], ALU.mult))
                if kind == "decay":
                    if tb:
                        wait_full(dve, "br", tb - 1)
                    for h in range(GH):
                        k = 4 * tb + h
                        chain.post(v.tensor_scalar(h4(M1[:, 0, :])[:, h, :], upper[:, :], rate[:, k:k + 1], None, ALU.mult))
                        chain.post(v.tensor_scalar(h4(M1[:, 1, :])[:, h, :], ident[:, :], beta[:, k:k + 1], None, ALU.mult))
                    chain.post(v.tensor_copy(h4(Dm[:, tb, :]), all_heads(ident[:, :])))
                    chain.post(v.tensor_copy(h4(DTm[:, tb, :]), all_heads(ident[:, :])))
                    chain.wait()
                    dve.nop().then_inc(rows_in, 1)
                    dve.nop().then_inc(d_ready, 1)
                    per_head(AO[:, 0, :], ("gcr", tb), ngc, 4 * tb, (ALU.add, ALU.min), 0.0)
                    chain.wait()
                    freed(dve.nop(), "gcr", tb)
                    dve.nop().then_inc(dl_ready, 1)
                    dve.wait_ge(dt_ready, tb + 1)
                    wait_full(dve, "br", tb)
                    chain.link(v.tensor_tensor(KB[:, 0, :], AO[:, 0, :], PS[:, bank("br", tb), :], ALU.mult))
                    freed(dve.nop(), "br", tb)
                    wait_full(dve, "kk", tb)
                    chain.post(v.tensor_tensor(AT[:, tb, :], KB[:, 0, :], PS[:, bank("kk", tb), :], ALU.mult))
                    wait_full(dve, "qk", tb)
                    chain.link(v.tensor_tensor(IT[:, tb, :], AO[:, 0, :], PS[:, bank("qk", tb), :], ALU.mult))
                    freed(dve.nop(), "kk", tb)
                    freed(dve.nop(), "qk", tb)
                    chain.post(v.tensor_tensor(h4(IT[:, tb, :]), h4(IT[:, tb, :]), all_heads(upper[:, :]), ALU.mult))
                    chain.link(v.tensor_tensor(cv[:, 0:4, t], cv[:, 0:4, t], h4(AO[:, 1, :]), ALU.mult))
                    dve.nop().then_inc(at_ready, 1)
                if kind == "M":
                    if n or tb >= 2:
                        wait_full(dve, "m", *((n, tb - 2) if tb >= 2 else (n - 1, tb + 2)))
                    v.tensor_tensor(h4(AO[:, tb % 2, :]), h4(AT[:, tb, :]), all_heads(masks[:, n, :]),
                                    ALU.mult).then_inc(ao_ready, 1)
                if kind == "X":
                    if n < LEVELS - 1:
                        wait_full(dve, "x", n, tb)
                    wait_full(dve, "xt", n, tb)
                    chain.post(v.tensor_tensor(DTm[:, tb, :], DTm[:, tb, :], PS[:, bank("xt", n, tb), :], ALU.subtract))
                    if n < LEVELS - 1:
                        chain.post(v.tensor_tensor(Dm[:, tb, :], Dm[:, tb, :], PS[:, bank("x", n, tb), :], ALU.subtract))
                    chain.wait()
                    if n < LEVELS - 1:
                        freed(dve.nop(), "x", n, tb)
                    freed(dve.nop(), "xt", n, tb)
                    dve.nop().then_inc(d_ready, 1)
                if kind == "tokens":
                    if tb >= 2:
                        wait_full(dve, "u", tb - 2)
                    per_head(KB[:, tb % 2, :], ("kt", tb), bge, 4 * tb)
                    per_head(VB[:, tb % 2, :], ("vt", tb), beta, 4 * tb)
                    chain.wait()
                    freed(dve.nop(), "kt", tb)
                    freed(dve.nop(), "vt", tb)
                    dve.nop().then_inc(tok_dve, 1)
                if kind == "scan":
                    if tb:
                        wait_full(dve, "ws", tb)
                        v.tensor_tensor(M1[:, tb % 2, :], AT[:, tb, :], PS[:, bank("ws", tb), :], ALU.subtract).then_inc(vn_ready, 1)
                        dve.wait_ge(vn_ready, tb)
                        freed(dve.nop(), "ws", tb)
                    if tb < TB - 1:
                        wait_full(dve, "su", tb)
                        if tb == 0:
                            chain.link(v.tensor_copy(state, PS[:, bank("su", tb), :]))
                        else:
                            for h in range(GH):
                                s_ = h4(state)[:, h, :]
                                k = 16 + 4 * tb + h
                                chain.post(v.scalar_tensor_tensor(out=s_, in0=s_, scalar=egcum[:, k:k + 1],
                                                                  in1=PS[:, bank("su", tb), h * P:(h + 1) * P],
                                                                  op0=ALU.mult, op1=ALU.add))
                            chain.wait()
                        freed(dve.nop(), "su", tb)
                        dve.nop().then_inc(state_ready, 1)
                if kind == "gdn_out":
                    if n == 0:
                        dve.wait_ge(unit_done, U_OUT2)
                        invert(20, 8, norm_ready)
                    else:
                        invert(20 + n, gdn_done + n, dve_chain)
                    chain.link(v.scalar_tensor_tensor(out=cv[:, 8 + n, :], in0=cv[:, 8 + n, :], scalar=col("gdn"),
                                                      in1=rinv, op0=ALU.mult, op1=ALU.mult))
                    if n == 0:
                        gdn_done = chain.n - 1
                    if n == 0:
                        dve.wait_ge(alo_ready, 32)
                    if n >= 2:
                        dve.wait_ge(alo_ready, 32 + n - 1)
                    v.scalar_tensor_tensor(out=tmp[:, n % 2, :], in0=cv[:, 8 + n, :], scalar=0.5, in1=dz[:, n, :],
                                           op0=ALU.mult, op1=ALU.mult).then_inc(tmp_ready, 1)
                    if n:
                        rest(32 + n - 1, chunk=4 + n - 1)
                    if n == GH - 1:
                        rest(32 + n, chunk=4 + n)
                if kind == "logits":
                    m, e, qb = n // 8, n // 4 % 2, n % 4
                    w = (qb + 1) * P
                    wait_full(dve, "s", n)
                    if n >= 3:
                        wait_full(dve, "pt", n - 3)
                    slope = 2.0 ** -(2 * m + e + 1)
                    v.scalar_tensor_tensor(out=L[:, n % 3, 0:w], in0=ND[:, 512 - w:512], scalar=slope,
                                           in1=PS[:, bank("s", n), 0:w], op0=ALU.mult, op1=ALU.add).then_inc(l_ready, 1)
                    dve.wait_ge(l_ready, n + 1)
                    freed(dve.nop(), "s", n)
                    v.tensor_reduce(nmax[:, n:n + 1], L[:, n % 3, 0:w], AX_X, ALU.max, negate=True).then_inc(nm_ready, 1)
                if kind == "probs":
                    w = (n % 4 + 1) * P
                    dve.wait_ge(e_ready, n + 1)
                    chain.link(v.reciprocal(prec[:, n:n + 1], psum_[:, n:n + 1]))
                    v.tensor_scalar(L[:, n % 3, 0:w], L[:, n % 3, 0:w], prec[:, n:n + 1], None, ALU.mult).then_inc(p_ready, 1)
                if kind == "pv" and n % 8 == 7:
                    m = n // 8
                    dve.wait_ge(pv_done, n + 1)
                    dve.wait_ge(alo_ready, 36 + m - 1)
                    v.scalar_tensor_tensor(out=tmp[:, m % 2, :], in0=PS[:, m % 2, :], scalar=0.5, in1=az[:, m, :],
                                           op0=ALU.mult, op1=ALU.mult).then_inc(tmp_ready, 1)
                    dve.wait_ge(tmp_ready, 36 + m + 1)
                    dve.nop().then_inc(om_ready, 1)
                    rest(36 + m, chunk=m)
            invert(24, gdn_done + 4, dve_chain)
            for c in range(8):
                chain.link(v.scalar_tensor_tensor(out=mx[:, c, :], in0=mx[:, c, :], scalar=col("post2", c), in1=rinv,
                                                  op0=ALU.mult, op1=ALU.mult))
                v.tensor_tensor(xres[:, c, :], xres[:, c, :], mx[:, c, :], ALU.add).then_inc(out_ready, 1)


def units(w, order=None):
    import numpy as np
    n = w.shape[1] // P
    u = w.reshape(KC, P, n, P).transpose(2, 1, 0, 3).reshape(n, P, D)
    return np.ascontiguousarray(u if order is None else u[order])


def kernel(**inputs):
    import numpy as _np
    import concourse.bacc as _bacc
    from concourse import mybir as _mybir
    from concourse.bass_utils import run_bass_kernel_spmd as _run

    a = {k: _np.asarray(v) for k, v in inputs.items()}
    w_in = list(range(12, 20)) + [b * 4 + m for m in range(4) for b in (2, 1, 0)]
    e = {
        "x": a["x"][0].T,
        "w_ada": a["w_ada"][0].reshape(KC, P, 12, 512).transpose(2, 1, 0, 3).reshape(12, P, 4096),
        "w_in": units(a["w_in"][0], w_in),
        "w_out": units(a["w_out"][0]),
        "w_q": units(a["w_q"][0]),
        "w_r": a["w_r"][0],
        "w_i": a["w_i"][0],
        "keys": a["sub_keys"][0].transpose(1, 3, 0, 2),
        "expert_u": a["expert_u"][0].reshape(N_KEYS, N_KEYS, KC, P).transpose(1, 3, 2, 0).reshape(N_KEYS, P, D),
        "expert_v": a["expert_v"][0].reshape(N_KEYS, N_KEYS, D).transpose(1, 0, 2),
    }
    w2 = a["w_in_2"][0]
    e["w_in2"] = units(w2[:, :4096], [4 * b + m for b in (4, 5, 6, 0, 1, 2, 3, 7) for m in range(4)])
    e["w_out2"] = units(a["w_out_2"][0])
    e["w_ba"] = w2[:, 4096:].reshape(KC, P, 8).transpose(1, 0, 2).reshape(P, 64)
    vectors = dict(n1=a["norm1_g"], n2=a["norm2_g"], fin=a["final_g"], pre2=a["norm_pre_w_2"], post2=a["norm_post_w_2"],
                   gn=_np.concatenate([a["gn_a"], a["gn_b"]], axis=-1), cbb=a["conv_b_b"], br=a["b_r"], bi=a["b_i"],
                   lam=a["lru_lambda"], gdn=a["gdn_norm_w_2"], caw=a["conv_a_w"], cbw=a["conv_b_w"], c2w=a["conv_w_2"],
                   bada=a["b_ada"], c=a["c"], alog=_np.repeat(a["a_log_2"][0], P), dtb=_np.repeat(a["dt_bias_2"][0], P))
    e["cols"] = _np.concatenate([vectors[k].reshape(-1, P).T for k in COLS], axis=1)
    nc = _bacc.Bacc("TRN2", target_bir_lowering=False, num_devices=1)
    arrays, aps = {}, {}
    for name, v in e.items():
        arrays[f"in_{name}"] = _np.ascontiguousarray(v)
        aps[name] = nc.dram_tensor(f"in_{name}", v.shape, F32, kind="ExternalInput").ap()
    out = nc.dram_tensor("out_0", (D, T), F32, kind="ExternalOutput").ap()
    build(nc, aps, out)
    r = _run(nc, [arrays], core_ids=[0])
    return r.results[0]["out_0"].T[None]
```

```python
from contextlib import ExitStack

import concourse.bass as bass
from concourse import mybir

P = 128
D = 1024
KC = D // P
T = 512
TB = T // P
F32 = mybir.dt.float32
F32R = mybir.dt.float32r
U32 = mybir.dt.uint32
ALU = mybir.AluOpType
ACT = mybir.ActivationFunctionType
AX_X = mybir.AxisListType.X

EPS = 1e-6
HEADS = 8
TOPK = 16
N_KEYS = 128
LOWEST = -3.0e38

RAW = 4
SPLIT = 2
U_IN = 0
U_OUT = U_IN + 20
U_Q = U_OUT + 8
U_EU = U_Q + 8
U_EV = U_EU + N_KEYS
U_IN2 = U_EV + N_KEYS
U_OUT2 = U_IN2 + 32
U_END = U_OUT2 + 8

QUAD = 4
WT = 32
GROUP = 4
ONEHOT = 16
TOK_PER_UNIT = 8

COLS = {}
_n = 0
for _name, _k in (("n1", 8), ("n2", 8), ("fin", 8), ("pre2", 8), ("post2", 8), ("gn", 8),
                  ("cbb", 4), ("br", 4), ("bi", 4), ("lam", 4), ("gdn", 1),
                  ("caw", 12), ("cbw", 16), ("c2w", 48), ("bada", 48), ("c", 8), ("alog", 4), ("dtb", 4)):
    COLS[_name] = _n
    _n += _k
N_COLS = _n


GH = 4
LEVELS = 7
MH = 8


def second_block_steps():
    steps = []
    slots = iter(range(MH * TB + 4))

    def attend():
        i = next(slots, None)
        if i is None:
            return
        if i >= 4:
            steps.append(("pv", i - 4))
        if 3 <= i < MH * TB + 3:
            steps.append(("turn", i - 3))
        if i < MH * TB:
            steps.append(("logits", i))
        if 1 <= i <= MH * TB:
            steps.append(("probs", i - 1))

    for w in range(28):
        if 12 <= w < 20:
            steps.append(("square", w - 12))
        steps.append(("unit", w))
        if 1 <= w <= 12:
            steps.append(("tanh", w - 1))
        if w <= 12:
            steps.append(("conv", w))
        if 12 <= w < 20:
            steps.append(("sum", w - 12))
        if w == 13:
            steps.append(("rates", 0))
        if w == 14:
            steps.append(("rates_turned", 0))
        if w == 16:
            steps.append(("cumulate", 0))
        if 13 <= w <= 20:
            steps.append(("scale", w - 13))
        if w >= 20 and w % 2 == 0:
            steps.append(("rows", w // 2 - 10))
        if w >= 20 and w % 2 == 1:
            steps.append(("products", w // 2 - 10))
            steps.append(("decay", w // 2 - 10))
    steps.append(("unit", 28))
    fill = 29
    steps += [("mask", 0, 0), ("mask", 0, 1)]
    for level in range(LEVELS):
        for what, tb in (("M", 0), ("M", 1), ("X", 0), ("M", 2), ("X", 1), ("M", 3), ("X", 2), ("X", 3)):
            if what == "X":
                if fill < 32:
                    steps.append(("unit", fill))
                elif fill == 32:
                    steps += [("values", q) for q in range(TB)]
                    attend()
                elif not (level == 6 and tb % 2):
                    attend()
                fill += 1
            steps.append((what, level, tb))
            if (what, level, tb) in (("X", 5, 1), ("X", 6, 1)):
                steps.append(("tokens", level - 5))
            if what == "M" and 4 * level + tb + 2 < 4 * LEVELS:
                steps.append(("mask", level + (tb + 2) // 4, (tb + 2) % 4))
    for kind, n in (("solve", 0), ("tokens", 2), ("solve", 1), ("read", 0), ("scan", 0), ("tokens", 3), ("solve", 2),
                    ("read", 1), ("scan", 1), ("solve", 3), ("read", 2), ("scan", 2), ("read", 3), ("scan", 3)):
        steps.append((kind, n))
        if kind == "scan":
            steps.append(("gsquare", n))
            if n >= 2:
                steps.append(("groot", n - 2))
        if kind in ("tokens", "read", "scan"):
            attend()
    steps.append(("gturn", 0))
    while len([st for st in steps if st[0] == "pv"]) < MH * TB:
        attend()
    steps.append(("gout", 0))
    assert next(slots, None) is None, "the attention is not over"
    for c in range(KC):
        steps.append(("unit", 32 + c))
    steps.append(("msum", 0))
    return steps


STEPS2 = second_block_steps()
JOBS, READERS = {}, []


def _jobs():
    def job(name, readers=1):
        JOBS[name] = len(READERS)
        READERS.append(readers)

    for st in STEPS2:
        kind, n = st[0], st[1:]
        if kind == "rates":
            job(("ba",))
        if kind == "rates_turned":
            job(("bat",))
        if kind == "cumulate":
            job(("cum",))
        if kind == "products":
            job(("gcr", *n), 2)
            job(("br", *n))
            job(("kk", *n))
            job(("qk", *n))
        if kind == "M":
            job(("m", *n))
        if kind == "X":
            if n[0] < LEVELS - 1:
                job(("x", *n))
            job(("xt", *n))
        if kind == "tokens":
            job(("kt", *n), 2)
            job(("vt", *n))
        if kind == "solve":
            job(("wt", *n))
            job(("u", *n))
        if kind == "read" and n[0]:
            job(("ws", *n))
        if kind == "scan":
            job(("o", *n))
            if n[0] < TB - 1:
                job(("su", *n))
        if kind == "values":
            job(("av", *n))
        if kind == "gturn":
            for h in range(GH):
                job(("gt", h))


_jobs()


class Chain:

    def __init__(self, eng, sem):
        self.eng, self.sem, self.n, self.at = eng, sem, 0, None

    def post(self, ins):
        ins.then_inc(self.sem, 1)
        self.n += 1
        return self.n

    def wait(self):
        self.eng.wait_ge(self.sem, self.n if self.at is None else self.at + self.n)

    def link(self, ins):
        self.post(ins)
        self.wait()


def build(nc, A, out):
    with ExitStack() as ctx:
        def sb(name, shape, dt=F32):
            return ctx.enter_context(nc.sbuf_tensor(name, shape, dt))

        def sem(name):
            return ctx.enter_context(nc.semaphore(name))

        PS = ctx.enter_context(nc.psum_tensor("PS", [P, 8, 512], F32))
        xres = sb("xres", [P, KC, T])
        act_hi = sb("act_hi", [P, KC, T], F32R)
        act_lo = sb("act_lo", [P, KC, T], F32R)
        raw = sb("raw", [P, RAW, D])
        w_hi = sb("w_hi", [P, SPLIT, D], F32R)
        w_lo = sb("w_lo", [P, SPLIT, D], F32R)
        ident = sb("ident", [P, P])
        ones = sb("ones", [P, P])
        upper = sb("upper", [P, P])
        iota = sb("iota", [P, P])
        cols = sb("cols", [P, N_COLS])
        ada = sb("ada", [P, 48])
        small = sb("small", [P, 176])
        ARENA = 31136
        arena = sb("arena", [P, ARENA])
        used = {}

        def region(name, start, *shape, dt=None):
            n = 1
            for s in shape:
                n *= s
            assert start + n <= ARENA, (name, start + n)
            used[name] = (start, start + n)
            ap = arena[:, start:start + n]
            if dt is not None:
                ap = ap.bitcast(dt)
            if len(shape) == 2:
                ap = ap.rearrange("p (a b) -> p a b", a=shape[0])
            if len(shape) == 3:
                ap = ap.rearrange("p (a b c) -> p a b c", a=shape[0], b=shape[1])
            return ap

        def col(name, c=0, n=1):
            return cols[:, COLS[name] + c:COLS[name] + c + n]

        eps = small[:, 0:1]
        cs = small[:, 8:16]
        cth = small[:, 16:24]
        gain1 = small[:, 24:32]
        gain2 = small[:, 32:40]
        dec = small[:, 40:44]
        hbr = small[:, 44:48]
        hbi = small[:, 48:52]
        sp = [small[:, 56 + 16 * i:60 + 16 * i] for i in range(6)]
        fgain = small[:, 160:168]
        fsq = small[:, 168:176]

        xrp = region("xrp", 0, 4, 516)
        xc = region("xc", 2064, 4, 512)
        gg = region("gg", 4112, 4, 512)
        tr = region("tr", 6160, 4, 512)
        ti = region("ti", 8208, 4, 512)
        y = region("y", 10256, 8, 512)
        xa = region("xa", 14352, 2, 512)
        pc = region("pc", 15376, 2, 516)
        ada_w = region("ada_w", 16408, 4, 2048)
        sq = region("sq", 24600, 2, 512)
        rms = region("rms", 25624, 2, 512)
        tmp = region("tmp", 26648, 2, 512)
        fin2 = region("fin2", 26648, KC, P)
        rinv = region("rinv", 27672, 1, 512)[:, 0, :]
        lru_q = region("lru_q", 28184, 1, 512)[:, 0, :]
        bd_r = region("bd_r", 28696, 4, P)
        bd_i = region("bd_i", 29208, 4, P)
        acc = region("acc", 30104, 2, 512)
        iota_i = region("iota_i", 29720, 1, P, dt=mybir.dt.int32)[:, 0, :]
        halves = region("halves", 29848, 1, P)[:, 0, :]
        ba_w = region("ba_w", 29976, 1, 64)[:, 0, :]
        S = region("S", 0, TB * HEADS * 2, N_KEYS)
        stage_w = region("stage_w", 0, 2, N_KEYS * WT)
        qT = region("qT", 8192, HEADS, T)
        hot_i = region("hot_i", 8192, ONEHOT, P)
        hot_j = region("hot_j", 8192 + ONEHOT * P, ONEHOT, P)
        keys = region("keys", 12288, HEADS, 256)
        gel = region("gel", 12288, 2, 1024)
        cand = region("cand", 14336, HEADS, 256)
        eq = region("eq", 16384, 2048, 1)[:, :, 0]
        rep = region("rep", 18432, 1, 256)[:, 0, :]
        topv = region("topv", 18688, 16, TOPK)
        topi = region("topi", 18944, 16, TOPK, dt=U32)
        topf = region("topf", 19200, 16, TOPK)
        bestv = region("bestv", 23312, TB * HEADS, TOPK)
        bestp = region("bestp", 19584, HEADS, TOPK, dt=U32)
        pick = region("pick", 19712, 2, 128, dt=U32)
        pickf = region("pickf", 19968, 2, 128)
        zs = region("zs", 23824, 2, TB * HEADS)
        routed_sb = [region(f"routed{i}", 20240 + 384 * i, 3, 128) for i in range(TB)]
        routeT = region("routeT", 21776, 3, T)
        gate_q = region("gate_q", 0, 2, 2048)
        gel_q = region("gel_q", 4096, 2, 2048)
        craw = region("craw", 14336, 2, 512)

        cv = region("cv", 0, 12, T)
        th2 = region("th2", 6144, 2, T)
        AT = region("AT", 6144, TB, 512)
        IT = region("IT", 8192, TB, 512)
        Dm = region("Dm", 10240, TB, 512)
        DTm = region("DTm", 12288, TB, 512)
        M1 = region("M1", 14336, 2, 512)
        AO = region("AO", 15360, 2, 512)
        KBd = region("KBd", 16384, 1, 512)[:, 0, :]
        KB = raw[:, 0, :].rearrange("p (a b) -> p a b", a=2)
        VB = raw[:, 1, :].rearrange("p (a b) -> p a b", a=2)
        avt = raw[:, 2:4, :].rearrange("p a (b c) -> p (a b) c", b=2)
        aq = region("aq", 18432, 4, T)
        ak = region("ak", 20480, 4, T)
        av = region("av", 22528, 4, T)
        masks = region("masks", 28184, LEVELS, P)
        ND = region("ND", 29080, 1, 512)[:, 0, :]
        state = region("state", 29592, 1, 512)[:, 0, :]
        cin = region("cin", 30104, 2, 516)
        az = region("az", 24600, 4, T)
        dz012 = region("dz012", 16896, 3, T)
        dz = [dz012[:, 0, :], dz012[:, 1, :], dz012[:, 2, :], region("dz3", 30104, 1, T)[:, 0, :]]
        L = region("L", 22528, 3, 512)
        PT = [region("PT0", 24064, 1, 512)[:, 0, :], region("PT1", 30616, 1, 512)[:, 0, :]]
        rr = region("rr", 29592, 1, 512)[:, 0, :]
        xsq = rr
        gres = region("gres", 12288, GH, T)
        otok = cv[:, 8:12, :]
        gscratch = region("gscratch", 10240, 4, P)
        mx = region("mx", 0, KC, T)
        small2 = sb("small2", [P, 496])
        ba_hi = sb("ba_hi", [P, KC, 8], F32R)
        ba_lo = sb("ba_lo", [P, KC, 8], F32R)

        def cols2(at, n):
            return small2[:, at:at + n]

        ba = cols2(0, 32)
        beta, dx, dax, dexp, dz_, dt1, dt2, dacc, rate = (cols2(32 + 16 * i, 16) for i in range(9))
        gcum = cols2(176, 48)
        egcum = cols2(224, 48)
        ngc = cols2(272, 16)
        bge = cols2(288, 16)
        ealog = cols2(304, 4)
        hgdn = cols2(308, 1)
        nmax = cols2(320, 32)
        gsum = cols2(464, 16)
        grms = cols2(480, 16)
        psum_ = cols2(352, 32)
        prec = cols2(384, 32)
        hc2w = cols2(416, 48)

        def h4(ap):
            return ap.rearrange("p (h n) -> p h n", h=GH)

        def dram(name, shape):
            return nc.dram_tensor(name, shape, F32).ap()

        gates_d = dram("gates_d", [N_KEYS // QUAD, P, T // WT, QUAD * WT])
        gel_d = dram("gel_d", [N_KEYS // QUAD, P, QUAD, T])

        consts_in = sem("consts_in")
        x_in = sem("x_in")
        ada_in = [sem(f"ada_in{i}") for i in range(4)]
        ada_used = sem("ada_used")
        ada_acc = sem("ada_acc")
        keys_in = sem("keys_in")
        blocks_in = sem("blocks_in")
        raw_in = [sem(f"raw_in{i}") for i in range(RAW)]
        pool_made = sem("pool_made")
        pool_chain = sem("pool_chain")
        hi_split = sem("hi_split")
        lo_split = sem("lo_split")
        unit_done = sem("unit_done")
        ada_done = sem("ada_done")
        sq_ready = sem("sq_ready")
        sq_used = sem("sq_used")
        sum_ready = sem("sum_ready")
        rms_ready = sem("rms_ready")
        rinv_ready = sem("rinv_ready")
        tmp_ready = sem("tmp_ready")
        ahi_ready = sem("ahi_ready")
        alo_ready = sem("alo_ready")
        c_tanh = sem("c_tanh")
        c_ready = sem("c_ready")
        dve_chain = sem("dve_chain")
        act_chain = sem("act_chain")
        z_act = sem("z_act")
        z_dve = sem("z_dve")
        xc_ready = sem("xc_ready")
        gates_ps = sem("gates_ps")
        gates_th = sem("gates_th")
        lam_exp = sem("lam_exp")
        lam_neg = sem("lam_neg")
        dec_ready = sem("dec_ready")
        s_ready = sem("s_ready")
        s_used = sem("s_used")
        root_ready = sem("root_ready")
        y_ready = sem("y_ready")
        y_scaled = sem("y_scaled")
        x_ready = sem("x_ready")
        q_sb = sem("q_sb")
        score_ps = sem("score_ps")
        score_sb = sem("score_sb")
        ex_in = sem("ex_in")
        ex_out = sem("ex_out")
        routed_ready = sem("routed_ready")
        route_ps = sem("route_ps")
        route_sb = sem("route_sb")
        gelu_done = sem("gelu_done")
        gel_st = [sem("gel_st0"), sem("gel_st1")]
        hot_ready = sem("hot_ready")
        gate_ps = sem("gate_ps")
        gate_sb = sem("gate_sb")
        gate_st = [sem("gate_st0"), sem("gate_st1")]
        gq_in = [sem("gq_in0"), sem("gq_in1")]
        eq_in = [sem("eq_in0"), sem("eq_in1")]
        craw_ready = sem("craw_ready")
        chi_ready = sem("chi_ready")
        clo_ready = sem("clo_ready")
        done_out = sem("done_out")
        bank_full = [sem(f"bank_full{b}") for b in range(2, 6)]
        bank_free = [sem(f"bank_free{b}") for b in range(2, 6)]
        pads_ready = sem("pads_ready")
        ba_in = sem("ba_in")
        ba_hi_r = sem("ba_hi_ready")
        ba_lo_r = sem("ba_lo_ready")
        fg_ready = sem("fg_ready")
        mean_ready = sem("mean_ready")
        rr_ready = sem("rr_ready")
        x1_ready = sem("x1_ready")
        z_done = sem("z_done")
        s_full = sem("s_full")
        pt_full = sem("pt_full")
        gn_done = sem("gn_done")
        gsq_ready = sem("gsq_ready")
        mix_squared = sem("mix_squared")
        sq_added = sem("sq_added")
        g_root = sem("g_root")
        g_scaled = sem("g_scaled")
        p_dve = sem("p_dve")
        conv_done = sem("conv_done")
        th_ready = sem("th_ready")
        cv_ready = sem("cv_ready")
        norm_ready = sem("norm_ready")
        ba_sb = sem("ba_sb")
        ba_row = sem("ba_row")
        rate_in = sem("rate_in")
        rate_out = sem("rate_out")
        rate_ready = sem("rate_ready")
        cum_in = sem("cum_in")
        cum_out = sem("cum_out")
        rows_in = sem("rows_in")
        dl_ready = sem("dl_ready")
        dt_ready = sem("dt_ready")
        at_ready = sem("at_ready")
        ao_ready = sem("ao_ready")
        m1_ready = sem("m1_ready")
        d_ready = sem("d_ready")
        tok_dve = sem("tok_dve")
        tok_act = sem("tok_act")
        wu_ready = sem("wu_ready")
        vn_ready = sem("vn_ready")
        o_ready = sem("o_ready")
        state_ready = sem("state_ready")
        avt_ready = sem("avt_ready")
        z_th = sem("z_th")
        l_ready = sem("l_ready")
        nm_ready = sem("nm_ready")
        e_ready = sem("e_ready")
        p_ready = sem("p_ready")
        pt_ready = sem("pt_ready")
        om_ready = sem("om_ready")
        pv_done = sem("pv_done")
        kd_chain = sem("kd_chain")
        mx_ready = sem("mx_ready")
        out_ready = sem("out_ready")

        def bank(*name):
            return 2 + JOBS[name] % 4

        def wait_full(eng, *name):
            n = JOBS[name]
            eng.wait_ge(bank_full[n % 4], n // 4 + 1)

        def wait_free(eng, *name):
            n = JOBS[name]
            if n >= 4:
                eng.wait_ge(bank_free[n % 4], sum(READERS[n % 4:n:4]))

        def unit_bank(n):
            return n % 4 if n < 12 else n % 2

        def made(n):
            return n + 1 if n < 8 else n - 7 if n < 24 else n - 15

        def freed_by(name):
            n = JOBS[name]
            return sum(READERS[n % 4:n + 1:4])

        def full(ins, *name):
            ins.then_inc(bank_full[JOBS[name] % 4], 1)

        def freed(ins, *name):
            ins.then_inc(bank_free[JOBS[name] % 4], 1)

        block = ctx.enter_context(nc.Block())
        NQ = N_KEYS // QUAD
        ADA_AFTER = {3: 4, 5: 5, U_OUT + 1: 6, U_OUT + 2: 7, U_OUT + 3: 8, U_OUT + 4: 9, U_Q + 2: 10, U_Q + 4: 11}
        Y_ORDER = (0, 1, 4, 5, 6, 2, 7, 3)
        Y_SQUARE = (11, 14, 15, 16, 17, 18, 19, 20)
        Y_SUM = (12, 15, 16, 17, 18, 19, 20, 20)
        Y_SCALE = (13, 16, 17, 18, 19, 20, 20, 20)
        GATE_BANKS = ((3, 4), (6, 7))
        X_ORDER = (6, 7, 0, 1, 2, 3, 4, 5)
        GATES = 5
        N1 = 48
        N2 = N1 + T // TOK_PER_UNIT

        def z_of(u):
            if u < 4:
                return "xr", u
            if u < 8:
                return "gr", u - 4
            return ("xa", "gc", "gb")[(u - 8) % 3], (u - 8) // 3

        @block.sync
        def _(sp_):
            def unit(u, src):
                if u >= RAW:
                    sp_.wait_ge(lo_split, u - RAW + 1)
                sp_.dma_start(raw[:, u % RAW, :], src).then_inc(raw_in[u % RAW], 16)

            def ada_half(h):
                for i in (2 * h, 2 * h + 1):
                    if i >= 4:
                        sp_.wait_ge(ada_used, i - 3)
                    sp_.dma_start(ada_w[:, i % 4, :], A["w_ada"][h][:, 2048 * (i % 2):2048 * (i % 2) + 2048]
                                  ).then_inc(ada_in[i % 4], 16)

            sp_.dma_start(cols[:, :], A["cols"]).then_inc(consts_in, 16)
            ada_half(0)
            sp_.dma_start(xres[:, :, :], A["x"].rearrange("(c p) t -> p c t", p=P)).then_inc(x_in, 16)
            ada_half(1)
            sp_.dma_start(ba_w, A["w_ba"]).then_inc(ba_in, 16)
            for h in range(2, 4):
                ada_half(h)
            for u in range(RAW):
                unit(u, A["w_in"][u])
            for h in range(4, 6):
                ada_half(h)
            sp_.wait_ge(pool_made, 2)
            for h in range(8):
                lo = 64 * (h % 2)
                for bd, w in ((bd_r, "w_r"), (bd_i, "w_i")):
                    sp_.dma_start(bd[lo:lo + 64, h // 2, lo:lo + 64], A[w][h]).then_inc(blocks_in, 16)
            for u in range(RAW, 20):
                unit(u, A["w_in"][u])
                if u in (12, 14):
                    ada_half(u // 2)
            for u in range(U_OUT, U_Q):
                unit(u, A["w_out"][u - U_OUT])
                if u - U_OUT in (4, 5):
                    ada_half(4 + u - U_OUT)
            for u in range(U_Q, U_EU):
                unit(u, A["w_q"][u - U_Q])
                if u - U_Q in (2, 3):
                    ada_half(8 + u - U_Q)
            sp_.wait_ge(pool_made, 3)
            for c in range(2):
                sp_.dma_start(keys[64 * c:64 * c + 64, :, P * c:P * c + P], A["keys"][c]).then_inc(keys_in, 16)
            def quad(i, b):
                sp_.dma_start(gate_q[:, b, :], gates_d[i].rearrange("a p c n -> (a p) (c n)") if not isinstance(i, int)
                              else gates_d[i].rearrange("p c n -> p (c n)")).then_inc(gq_in[b], 16)
                sp_.dma_start(gel_q[:, b, :], gel_d[i].rearrange("a p c n -> (a p) (c n)") if not isinstance(i, int)
                              else gel_d[i].rearrange("p c n -> p (c n)")).then_inc(eq_in[b], 16)

            def expert_u(first, r):
                for k in range(RAW):
                    sp_.wait_ge(lo_split, r * RAW + (U_EU + first + k - RAW + 1))
                    sp_.dma_start(raw[:, k, :], A["expert_u"][bass.ds(r * RAW + (first + k), 1)].rearrange(
                        "a p n -> (a p) n")).then_inc(raw_in[k], 16)

            ahead = N2 + 8
            with sp_.Fori(0, ahead // RAW) as r:
                expert_u(0, r)
            for b in range(2):
                sp_.wait_ge(gate_st[b], 16 * (T // WT // 2))
                sp_.wait_ge(gel_st[b], 16 * 2)
            quad(0, 0)
            quad(1, 1)
            with sp_.Fori(0, (N_KEYS - ahead) // RAW) as r:
                expert_u(ahead, r)
            for k in range(RAW):
                unit(U_EV + k, A["expert_v"][k])
            for b in range(2):
                sp_.wait_ge(gel_st[b], 16 * (N_KEYS // 4))
            with sp_.Fori(0, NQ // 2 - 1) as r:
                for b in range(2):
                    for k in range(QUAD):
                        sp_.wait_ge(lo_split, r * 8 + (U_EV + 4 * b + k + 1))
                        sp_.dma_start(raw[:, k, :], A["expert_v"][bass.ds(r * 8 + (4 * b + k + 4), 1)].rearrange(
                            "a p n -> (a p) n")).then_inc(raw_in[k], 16)
                    sp_.wait_ge(craw_ready, r * 8 + 4 * (b + 1))
                    quad(bass.ds(r * 2 + (b + 2), 1), b)
            for k in range(QUAD):
                unit(U_EV + N_KEYS - QUAD + k, A["expert_v"][N_KEYS - QUAD + k])
            for w in range(32):
                unit(U_IN2 + w, A["w_in2"][w])
            for w in range(8):
                if w == 2:
                    sp_.wait_ge(pv_done, MH * TB)
                    sp_.wait_ge(wu_ready, TB)
                unit(U_OUT2 + w, A["w_out2"][w])
            for c in range(KC):
                sp_.wait_ge(out_ready, c + 1)
                sp_.dma_start(out[c * P:(c + 1) * P, :], xres[:, c, :]).then_inc(done_out, 16)
            sp_.wait_ge(done_out, 16 * KC)

        @block.gpsimd
        def _(pool):
            chain = Chain(pool, pool_chain)
            chain.post(pool.memset(small[:, 0:8], EPS))
            chain.post(pool.memset(ones[:, :], 1.0))
            chain.post(pool.memset(ident[:, :], 0.0))
            chain.post(pool.memset(upper[:, :], 1.0))
            chain.post(pool.memset(halves[:, :], 1.0))
            chain.post(pool.memset(bd_r[:, :, :], 0.0))
            chain.post(pool.memset(bd_i[:, :, :], 0.0))
            for m in range(4):
                chain.post(pool.memset(xrp[:, m, 0:4], 0.0))
            for b in range(2):
                chain.post(pool.memset(pc[:, b, 0:4], 0.0))
            chain.post(pool.iota(iota_i[:, :], [[1, P]], base=0, channel_multiplier=0))
            chain.wait()
            chain.post(pool.tensor_copy(iota[:, :], iota_i[:, :]))
            chain.post(pool.affine_select(out=ident[:, :], in_=ident[:, :], compare_op=ALU.not_equal, fill=1.0,
                                          base=0, pattern=[[-1, P]], channel_multiplier=1))
            chain.post(pool.affine_select(out=upper[:, :], in_=upper[:, :], compare_op=ALU.is_ge, fill=0.0,
                                          base=0, pattern=[[1, P]], channel_multiplier=-1))
            chain.post(pool.affine_select(out=halves[:, 0:64], in_=halves[:, 0:64], compare_op=ALU.is_ge, fill=0.0,
                                          base=63, pattern=[[0, 64]], channel_multiplier=-1))
            chain.post(pool.affine_select(out=halves[:, 64:128], in_=halves[:, 64:128], compare_op=ALU.is_ge, fill=0.0,
                                          base=-64, pattern=[[0, 64]], channel_multiplier=1))
            chain.wait()
            pool.nop().then_inc(pool_made, 2)

            def lower(u, k, r=None):
                at = (lambda v: v) if r is None else (lambda v: r + v)
                pool.wait_ge(hi_split, at(u + 1))
                pool.tensor_tensor(w_lo[:, k % SPLIT, :], raw[:, k % RAW, :], w_hi[:, k % SPLIT, :].bitcast(F32),
                                   ALU.subtract).then_inc(lo_split, 1)

            for u in range(U_Q):
                lower(u, u)
            lower(U_Q, U_Q)
            pool.wait_ge(y_ready, 8)
            pool.wait_ge(ahi_ready, 17)
            pool.memset(keys[:, :, :], 0.0).then_inc(pool_made, 1)
            for u in range(U_Q + 1, U_EU):
                lower(u, u)
            chain.link(pool.iota(iota_i[:, :], [[1, P]], base=0, channel_multiplier=-1))
            for n in range(4):
                chain.post(pool.tensor_copy(ND[:, n * P:(n + 1) * P], iota_i[:, :]))
            chain.wait()
            for n in range(3):
                chain.post(pool.tensor_scalar(ND[:, n * P:(n + 1) * P], ND[:, n * P:(n + 1) * P],
                                              float(P * (n - 3)), 0.0, ALU.add, ALU.add))
            chain.post(pool.affine_select(out=ND[:, 384:512], in_=ND[:, 384:512], compare_op=ALU.is_ge, fill=-1.0e32,
                                          base=0, pattern=[[-1, P]], channel_multiplier=1))
            chain.link(pool.memset(masks[:, :, :], 0.0))
            for n in range(LEVELS):
                b = 1 << n
                odd = masks[:, n, :].rearrange("p (m e r) -> p m e r", e=2, r=b)[:, :, 1, :]
                chain.link(pool.memset(odd, 1.0))
                chain.link(pool.affine_select(out=odd, in_=odd, compare_op=ALU.is_ge, fill=0.0, base=0,
                                              pattern=[[-2 * b, P // (2 * b)], [0, b]], channel_multiplier=1))
                chain.link(pool.affine_select(out=odd, in_=odd, compare_op=ALU.is_ge, fill=0.0, base=b - 1,
                                              pattern=[[2 * b, P // (2 * b)], [0, b]], channel_multiplier=-1))
            pool.nop().then_inc(pool_made, 1)
            with pool.Fori(0, (U_IN2 - U_EU) // RAW) as r:
                for k in range(RAW):
                    lower(U_EU + k, k, r * RAW)
            for u in range(U_IN2, U_IN2 + SPLIT):
                lower(u, u)
            for i in range(1, KC):
                pool.wait_ge(sq_ready, 24 + i + 1)
                if i > 1:
                    pool.wait_ge(sq_added, i - 1)
                pool.tensor_tensor(xsq, sq[:, 0, :] if i == 1 else xsq, sq[:, i % 2, :], ALU.add).then_inc(sq_added, 1)
            for st in STEPS2:
                kind, n, tb = st[0], st[1], st[-1]
                if kind == "unit" and U_IN2 + n + SPLIT < U_END:
                    lower(U_IN2 + n + SPLIT, n + SPLIT)
                    if 2 <= n < 10:
                        if n == 2:
                            pool.wait_ge(rinv_ready, 11)
                            pool.wait_ge(alo_ready, 32)
                            pool.wait_ge(sq_ready, 32)
                        pool.tensor_tensor(xres[:, n - 2, :], xres[:, n - 2, :], rinv, ALU.mult).then_inc(x1_ready, 1)
                if kind == "mask":
                    if n == 0 and tb == 0:
                        pool.wait_ge(at_ready, TB)
                        pool.wait_ge(pool_made, 4)
                    if n or tb >= 2:
                        wait_full(pool, "m", *((n, tb - 2) if tb >= 2 else (n - 1, tb + 2)))
                    pool.tensor_tensor(h4(AO[:, tb % 2, :]), h4(AT[:, tb, :]),
                                       masks[:, n, :].unsqueeze(1).to_broadcast([P, GH, P]), ALU.mult).then_inc(ao_ready, 1)

        @block.tensor
        def _(pe):
            def linear(u, k, bank, r=None, split=None, order=range(KC), between=None):
                pe.wait_ge(lo_split, u + 1 if r is None else r + (u + 1))
                for i, c in enumerate(order):
                    if split is not None:
                        pe.wait_ge(alo_ready, split + i + 1)
                    for n, (w, x) in enumerate(((w_hi, act_hi), (w_lo, act_hi), (w_hi, act_lo))):
                        mm = pe.matmul(PS[:, bank, :], w[:, k % SPLIT, c * P:(c + 1) * P], x[:, c, :],
                                       start=(i == 0 and n == 0), stop=(i == KC - 1 and n == 2))
                    if between:
                        between(i, c)
                mm.then_inc(unit_done, 1)

            def squares(first, count, index, mat):
                for c in range(count):
                    square_sum(first, c, count, index, mat)

            def square_sum(first, c, count, index, mat):
                if index >= 2 and c == 0:
                    pe.wait_ge(rms_ready, index - 1)
                pe.wait_ge(sq_ready, first + c + 1)
                mm = pe.matmul(PS[:, 6 + index % 2, :], mat[:, :], sq[:, (first + c) % 2, :],
                               start=(c == 0), stop=(c == count - 1))
                mm.then_inc(sq_used, 1)
                if c == count - 1:
                    pe.wait_ge(sq_used, first + count)
                    pe.nop().then_inc(sum_ready, 1)

            def ada_half(h):
                pe.wait_ge(ada_acc, h + 1)
                for n in range(4):
                    mm = pe.matmul(PS[:, 5, 4 * h + n:4 * h + n + 1], acc[:, h % 2, n * P:(n + 1) * P], ones[:, 0:1],
                                   start=True, stop=True)
                mm.then_inc(ada_done, 1)

            pe.wait_ge(pool_made, 2)
            squares(0, 8, 0, ones)
            for h in range(4):
                ada_half(h)
            for u in range(U_OUT):
                kind, m = z_of(u)
                if 3 <= u < 11:
                    pe.wait_ge(z_act, u - 2)
                elif u >= 11:
                    if kind == "xa":
                        pe.wait_ge(z_act, 8 + m)
                    else:
                        pe.wait_ge(z_dve, 2 * m - (1 if kind == "gc" else 0))
                linear(u, u, u % 3, split=0 if u == 0 else None)
                if u in ADA_AFTER:
                    ada_half(ADA_AFTER[u])
                if GATES <= u < GATES + 4:
                    g = u - GATES
                    pe.wait_ge(xc_ready, g + 1)
                    if g == 0:
                        pe.wait_ge(blocks_in, 16 * 16)
                    if g >= 2:
                        pe.wait_ge(gates_th, 2 * (g - 1))
                    if g == 1:
                        pe.wait_ge(rms_ready, 1)
                    r_bank, i_bank = GATE_BANKS[g % 2]
                    pe.matmul(PS[:, r_bank, :], bd_r[:, g, :], xc[:, g, :], start=True, stop=True)
                    pe.matmul(PS[:, i_bank, :], bd_i[:, g, :], xc[:, g, :], start=True, stop=True).then_inc(gates_ps, 1)
                if u == Y_SUM[0]:
                    pe.wait_ge(gates_th, 8)
                for i in range(8):
                    if Y_SUM[i] == u:
                        squares(8 + i, 1, 1 + i, halves)
            for i in range(8):
                if Y_SUM[i] == 20:
                    squares(8 + i, 1, 1 + i, halves)
            for c in range(8):
                u = U_OUT + c
                if c < 3:
                    pe.wait_ge(z_dve, 8)
                    pe.wait_ge(z_act, 12)
                else:
                    pe.wait_ge(x_ready, c - 2)
                if c == 0:
                    linear(u, u, u % 3, split=8, order=Y_ORDER)
                else:
                    linear(u, u, u % 3)
                if u in ADA_AFTER:
                    ada_half(ADA_AFTER[u])
            pe.wait_ge(sq_used, 24)
            pe.matmul(PS[:, 7, :], ones[:, :], rms[:, 0, :], start=True, stop=True).then_inc(sum_ready, 1)
            for c in range(8):
                if c < 3:
                    pe.wait_ge(x_ready, 8)
                else:
                    pe.wait_ge(q_sb, c - 2)
                linear(U_Q + c, U_Q + c, (U_Q + c) % 3, split=16 if c == 0 else None)
                if U_Q + c in ADA_AFTER:
                    ada_half(ADA_AFTER[U_Q + c])
            pe.wait_ge(q_sb, 8)
            pe.wait_ge(keys_in, 32)
            for n in range(TB * 4):
                tb, hp = n // 4, n % 4
                if n >= 2:
                    pe.wait_ge(score_sb, n - 1)
                for e in range(2):
                    mm = pe.matmul(PS[:, 3 + n % 2, 256 * e:256 * e + 256], qT[:, 2 * hp + e, tb * P:(tb + 1) * P],
                                   keys[:, 2 * hp + e, :], start=True, stop=True)
                mm.then_inc(score_ps, 1)
            pe.wait_ge(q_sb, 8)
            for k in range(2):
                linear(U_EU + k, k, k)
            with pe.Fori(0, (N1 - 2) // 2) as r:
                for k in range(2):
                    pe.wait_ge(gelu_done, r * 2 + (k + 1))
                    linear(U_EU + 2 + k, k, k, r * 2)
            def gate_group(g, k, r=None, first=False):
                at = (lambda v: v) if r is None else (lambda v: r + v)
                if not first:
                    pe.wait_ge(gate_sb, at(g - 3))
                pe.wait_ge(hot_ready, at(g + 1))
                for t in range(GROUP):
                    s = (GROUP * k + t) % ONEHOT
                    mm = pe.matmul(PS[:, 2 + k % 4, t * P:(t + 1) * P], hot_i[:, s, :], hot_j[:, s, :],
                                   start=True, stop=True)
                mm.then_inc(gate_ps, 1)

            def both(k, r_u, r_g):
                at = N1 + k
                pe.wait_ge(gelu_done, at - 1 if r_u is None else r_u + (at - 1))
                linear(U_EU + at, k, k % 2, r_u)
                for g in (2 * k, 2 * k + 1):
                    gate_group(g, g, r_g)

            for k in range(8):
                if k < 2:
                    pe.wait_ge(gelu_done, N1 + k - 1)
                    linear(U_EU + N1 + k, k, k)
                if k == 0:
                    for tb in range(TB):
                        pe.wait_ge(routed_ready, tb + 1)
                        if tb:
                            pe.wait_ge(route_sb, tb)
                        for n in range(3):
                            mm = pe.transpose(PS[:, 2, n * P:(n + 1) * P], routed_sb[tb][:, n, :], ident[:, :])
                        mm.then_inc(route_ps, 1)
                if k == 1:
                    for g in range(4):
                        gate_group(g, g, None, True)
                if k >= 2:
                    both(k, None, None)
            with pe.Fori(0, (N2 - N1) // 8 - 1) as r:
                for k in range(8):
                    both(8 + k, r * 8, r * 16)
            with pe.Fori(0, (N_KEYS - N2) // 2) as r:
                for k in range(2):
                    pe.wait_ge(gelu_done, r * 2 + (N2 + k - 1))
                    linear(U_EU + N2 + k, k, k, r * 2)

            def experts(b, k, r=None, start=False, stop=False):
                at = (lambda v: v) if r is None else (lambda v: r + v)
                pe.wait_ge(lo_split, at(U_EV + b + 1))
                pe.wait_ge(clo_ready, at(b + 1))
                for c in range(KC):
                    for n, (w, x) in enumerate(((w_hi, act_hi), (w_lo, act_hi), (w_hi, act_lo))):
                        mm = pe.matmul(PS[:, c, :], w[:, k % SPLIT, c * P:(c + 1) * P], x[:, k % 2, :],
                                       start=(start and n == 0), stop=(stop and n == 2), skip_group_check=True)
                mm.then_inc(unit_done, 1)

            pe.wait_ge(gelu_done, N_KEYS)
            pe.wait_ge(gate_sb, T // GROUP)
            experts(0, 0, start=True)
            experts(1, 1)
            with pe.Fori(0, N_KEYS // 2 - 2) as r:
                for k in range(2):
                    experts(2 + k, k, r * 2)
            experts(N_KEYS - 2, 0)
            experts(N_KEYS - 1, 1, stop=True)
            pe.wait_ge(pool_made, 4)

            def heads(name, lhs, rhs, at=None):
                b = bank(*name)
                wait_free(pe, *name)
                for h in range(GH):
                    mm = pe.matmul(PS[:, b, h * P:(h + 1) * P], lhs(h), rhs(h), start=True, stop=True)
                full(mm, *name)

            def both_sums(i, c):
                if i == 0:
                    pe.wait_ge(fg_ready, 1)
                pe.wait_ge(sq_ready, 24 + i + 1)
                mm = pe.matmul(PS[:, 7, :], fin2[:, c, :], sq[:, i % 2, :], start=(i == 0), stop=(i == KC - 1))
                mm.then_inc(sq_used, 1)
                if i == KC - 1:
                    pe.wait_ge(sq_added, KC - 1)
                    pe.matmul(PS[:, 6, :], ones[:, :], xsq, start=True, stop=True).then_inc(sq_added, 1)
                    pe.wait_ge(sq_used, 24 + KC)
                    pe.wait_ge(sq_added, KC)
                    pe.nop().then_inc(sum_ready, 2)

            def turned(name, src, n=4):
                b = bank(*name)
                wait_free(pe, *name)
                for h in range(n):
                    mm = pe.transpose(PS[:, b, h * P:(h + 1) * P], src(h), ident[:, :])
                full(mm, *name)

            for st in STEPS2:
                kind, n, tb = st[0], st[1], st[-1]
                t = slice(tb * P, (tb + 1) * P)
                if kind == "unit":
                    if n == 0:
                        pe.wait_ge(x_ready, 11)
                    if n == 1:
                        pe.wait_ge(x_ready, 16)
                    if 4 <= n < 32:
                        pe.wait_ge(p_dve, n - (3 if n < 12 else 1))
                    if 32 <= n < 34:
                        pe.wait_ge(om_ready, 3 + n - 32)
                    elif n >= 34:
                        pe.wait_ge(mx_ready, n - 33)
                    linear(U_IN2 + n, n, unit_bank(n), split={0: 24, 32: 32}.get(n), order=X_ORDER if n == 0 else range(KC),
                           between=both_sums if n == 0 else None)
                if kind == "rates":
                    pe.wait_ge(ba_lo_r, 1)
                    pe.wait_ge(p_dve, 12)
                    wait_free(pe, "ba")
                    for c in range(KC):
                        for i, (w, x) in enumerate(((ba_hi, act_hi), (ba_lo, act_hi), (ba_hi, act_lo))):
                            mm = pe.matmul(PS[0:8, bank("ba"), :], w[:, c, :], x[:, c, :],
                                           start=(c == 0 and i == 0), stop=(c == KC - 1 and i == 2))
                    full(mm, "ba")
                if kind == "rates_turned":
                    pe.wait_ge(ba_row, 1)
                    wait_free(pe, "bat")
                    for q in range(TB):
                        mm = pe.transpose(PS[:, bank("bat"), 8 * q:8 * q + 8], th2[0:8, 0, q * P:(q + 1) * P], ident[0:8, 0:8])
                    full(mm, "bat")
                if kind == "sum":
                    squares(32 + n, 1, 12 + n, ones)
                if kind == "cumulate":
                    pe.wait_ge(rate_ready, 1)
                    wait_free(pe, "cum")
                    pe.matmul(PS[:, bank("cum"), 0:16], upper[:, :], rate, start=True, stop=True)
                    full(pe.matmul(PS[:, bank("cum"), 16:32], ones[:, :], rate, start=True, stop=True), "cum")
                if kind == "products":
                    pe.wait_ge(rows_in, tb + 1)
                    for name, src in (("gcr", 0), ("br", 1)):
                        wait_free(pe, name, tb)
                        full(pe.matmul(PS[:, bank(name, tb), :], ones[:, :], M1[:, src, :], start=True, stop=True), name, tb)
                    pe.wait_ge(norm_ready, 8)
                    heads(("kk", tb), lambda h: cv[:, 4 + h, t], lambda h: cv[:, 4 + h, t])
                    heads(("qk", tb), lambda h: cv[:, 4 + h, t], lambda h: cv[:, h, t])
                if kind == "M":
                    pe.wait_ge(ao_ready, 4 * n + tb + 1)
                    pe.wait_ge(d_ready, 4 * n + tb + 1)
                    heads(("m", n, tb), lambda h: h4(AO[:, tb % 2, :])[:, h, :], lambda h: h4(Dm[:, tb, :])[:, h, :])
                if kind == "X":
                    pe.wait_ge(m1_ready, 4 * n + tb + 1)
                    if n < LEVELS - 1:
                        heads(("x", n, tb), lambda h: h4(DTm[:, tb, :])[:, h, :], lambda h: h4(M1[:, tb % 2, :])[:, h, :])
                    heads(("xt", n, tb), lambda h: h4(M1[:, tb % 2, :])[:, h, :], lambda h: h4(DTm[:, tb, :])[:, h, :])
                if kind == "tokens":
                    turned(("kt", tb), lambda h: cv[:, 4 + h, t])
                    pe.wait_ge(cv_ready, 12)
                    turned(("vt", tb), lambda h: cv[:, 8 + h, t])
                if kind == "solve":
                    pe.wait_ge(tok_dve, tb + 1)
                    pe.wait_ge(d_ready, 4 * LEVELS + tb + 1)
                    heads(("wt", tb), lambda h: h4(KB[:, tb % 2, :])[:, h, :], lambda h: h4(DTm[:, tb, :])[:, h, :])
                    heads(("u", tb), lambda h: h4(DTm[:, tb, :])[:, h, :], lambda h: h4(VB[:, tb % 2, :])[:, h, :])
                if kind == "read" and tb:
                    pe.wait_ge(wu_ready, tb + 1)
                    pe.wait_ge(state_ready, tb)
                    heads(("ws", tb), lambda h: h4(Dm[:, tb, :])[:, h, :], lambda h: h4(state)[:, h, :])
                if kind == "scan":
                    if tb:
                        pe.wait_ge(vn_ready, tb)
                    else:
                        pe.wait_ge(wu_ready, 1)
                        pe.wait_ge(at_ready, TB)
                    vn = M1[:, tb % 2, :] if tb else AT[:, 0, :]
                    wait_free(pe, "o", tb)
                    for h in range(GH):
                        o = PS[:, bank("o", tb), h * P:(h + 1) * P]
                        if tb:
                            pe.matmul(o, cv[:, h, t], h4(state)[:, h, :], start=True, stop=False)
                        mm = pe.matmul(o, h4(IT[:, tb, :])[:, h, :], h4(vn)[:, h, :], start=(tb == 0), stop=True)
                    full(mm, "o", tb)
                    if tb < TB - 1:
                        pe.wait_ge(tok_act, tb + 1)
                        heads(("su", tb), lambda h: cv[:, 4 + h, t], lambda h: h4(vn)[:, h, :])
                if kind == "values":
                    pe.wait_ge(p_dve, 24)
                    turned(("av", tb), lambda m: av[:, m, t])
                if kind == "gturn":
                    for h in range(GH):
                        wait_free(pe, "gt", h)
                        for q in range(TB):
                            pe.wait_ge(g_scaled, 4 * q + h + 1)
                            mm = pe.transpose(PS[:, bank("gt", h), q * P:(q + 1) * P], otok[:, h, q * P:(q + 1) * P], ident[:, :])
                        full(mm, "gt", h)
                if kind == "logits":
                    m, e, qb = n // 8, n // 4 % 2, n % 4
                    if n:
                        pe.wait_ge(l_ready, n)
                    else:
                        pe.wait_ge(rms_ready, 20)
                        pe.wait_ge(p_dve, 20)
                    s64 = slice(64 * e, 64 * e + 64)
                    pe.matmul(PS[:, 6, 0:(qb + 1) * P], aq[s64, m, qb * P:(qb + 1) * P],
                              ak[s64, m, 0:(qb + 1) * P], start=True, stop=True).then_inc(s_full, 1)
                if kind == "turn":
                    pe.wait_ge(p_ready, n + 1)
                    if n:
                        pe.wait_ge(pt_ready, n)
                    for kb in range(n % 4 + 1):
                        mm = pe.transpose(PS[:, 7, kb * P:(kb + 1) * P], L[:, n % 3, kb * P:(kb + 1) * P], ident[:, :])
                    mm.then_inc(pt_full, 1)
                if kind == "pv":
                    m, e, qb = n // 8, n // 4 % 2, n % 4
                    if n == 0:
                        pe.wait_ge(p_dve, 32)
                        pe.wait_ge(avt_ready, TB)
                    if n % 8 == 0 and m >= 2:
                        pe.wait_ge(om_ready, m - 1)
                    pe.wait_ge(pt_ready, n + 1)
                    for kb in range(qb + 1):
                        mm = pe.matmul(PS[64 * e:64 * e + 64, m % 2, qb * P:(qb + 1) * P],
                                       avt[:, kb, P * m + 64 * e:P * m + 64 * e + 64], PT[n % 2][:, kb * P:(kb + 1) * P],
                                       start=(kb == 0), stop=(kb == qb))
                    mm.then_inc(pv_done, 1)
                if kind == "msum":
                    pe.wait_ge(mix_squared, 1)
                    pe.matmul(PS[:, 6, :], ones[:, :], sq[:, 0, :], start=True, stop=True).then_inc(sum_ready, 1)

        @block.scalar
        def _(act):
            chain = Chain(act, act_chain)

            def upper_part(u, k, r=None):
                at = (lambda v: v) if r is None else (lambda v: r + v)
                if r is None:
                    act.wait_ge(raw_in[k % RAW], 16 * (u // RAW + 1))
                else:
                    act.wait_ge(raw_in[k % RAW], r * (16 // RAW) + 16 * (u // RAW + 1))
                if r is not None or u >= SPLIT:
                    act.wait_ge(unit_done, at(u - SPLIT + 1))
                act.activation(w_hi[:, k % SPLIT, :], raw[:, k % RAW, :], ACT.Copy).then_inc(hi_split, 1)

            def square(n, src):
                if n >= 2:
                    act.wait_ge(sq_used, n - 1)
                act.activation(sq[:, n % 2, :], src, ACT.Square).then_inc(sq_ready, 1)

            def root(index, width):
                act.wait_ge(sum_ready, index + 1)
                if index >= 2:
                    act.wait_ge(rinv_ready, index - 1)
                act.activation(rms[:, index % 2, :], PS[:, 6 + index % 2, :], ACT.Sqrt, bias=eps,
                               scale=1.0 / width).then_inc(rms_ready, 1)

            def operand(n, shift=None, chunk=None):
                act.wait_ge(tmp_ready, made(n))
                if shift is None:
                    act.activation(act_hi[:, n % 8 if chunk is None else chunk, :], tmp[:, n % 2, :], ACT.Copy).then_inc(ahi_ready, 1)
                else:
                    act.activation(act_hi[:, n % 8 if chunk is None else chunk, :], tmp[:, n % 2, :], ACT.Identity, bias=shift).then_inc(ahi_ready, 1)

            act.wait_ge(consts_in, 16)
            act.activation(cth, col("c", 0, 8), ACT.Tanh, scale=0.5).then_inc(c_tanh, 1)
            act.wait_ge(x_in, 16)
            for c in range(8):
                square(c, xres[:, c, :])
            act.wait_ge(pool_made, 2)
            root(0, D)
            for u in range(SPLIT):
                upper_part(u, u)
            for c in range(8):
                operand(c, ada[:, c:c + 1])
            act.wait_ge(ba_in, 16)
            act.activation(ba_hi[:, :, :].rearrange("p c n -> p (c n)"), ba_w[:, :], ACT.Copy).then_inc(ba_hi_r, 1)
            act.wait_ge(lam_neg, 1)
            act.activation(sp[1], sp[0], ACT.Exp, scale=-1.0).then_inc(lam_exp, 1)
            for u in range(U_OUT):
                kind, m = z_of(u)
                act.wait_ge(unit_done, u + 1)
                upper_part(u + SPLIT, u + SPLIT)
                if kind == "xr":
                    act.activation(xrp[:, m, 3:515], PS[:, u % 3, :], ACT.Copy).then_inc(z_act, 1)
                if kind == "gr":
                    act.activation(gg[:, m, :], PS[:, u % 3, :], ACT.Gelu).then_inc(z_act, 1)
                if kind == "xa":
                    if m >= 2:
                        act.wait_ge(z_dve, 2 * (m - 2) + 1)
                    act.activation(xa[:, m % 2, :], PS[:, u % 3, :], ACT.Copy).then_inc(z_act, 1)
                if GATES + 1 <= u < GATES + 5:
                    g = u - GATES - 1
                    act.wait_ge(gates_ps, g + 1)
                    r_bank, i_bank = GATE_BANKS[g % 2]
                    act.activation(tr[:, g, :], PS[:, r_bank, :], ACT.Tanh, bias=hbr[:, g:g + 1], scale=0.5).then_inc(gates_th, 1)
                    act.activation(ti[:, g, :], PS[:, i_bank, :], ACT.Tanh, bias=hbi[:, g:g + 1], scale=0.5).then_inc(gates_th, 1)
                if GATES + 2 <= u < GATES + 6:
                    g = u - GATES - 2
                    if g == 0:
                        act.wait_ge(dec_ready, 1)
                    act.wait_ge(gates_th, 2 * g + 2)
                    act.activation(tr[:, g, :], tr[:, g, :], ACT.Tanh, bias=dec[:, g:g + 1],
                                   scale=dec[:, g:g + 1]).then_inc(s_ready, 1)
                for i in range(8):
                    if Y_SUM[i] == u:
                        root(1 + i, 64)
                for i in range(8):
                    if Y_SQUARE[i] == u:
                        act.wait_ge(y_ready, i + 1)
                        square(8 + i, y[:, Y_ORDER[i], :])
                if u == GATES + 7:
                    for g in range(4):
                        act.wait_ge(s_used, g + 1)
                        act.activation(tr[:, g, :], tr[:, g, :], ACT.Sqrt, scale=-1.0).then_inc(root_ready, 1)
            def y_upper(i):
                act.wait_ge(y_scaled, i + 1)
                act.activation(act_hi[:, Y_ORDER[i], :], y[:, Y_ORDER[i], :], ACT.Copy).then_inc(ahi_ready, 1)

            act.wait_ge(y_ready, 8)
            square(15, y[:, Y_ORDER[7], :])
            for i in range(5):
                y_upper(i)
            root(7, 64)
            y_upper(5)
            root(8, 64)
            y_upper(6)
            y_upper(7)
            for c in range(8):
                act.wait_ge(unit_done, U_OUT + c + 1)
                upper_part(U_OUT + c + SPLIT, U_OUT + c + SPLIT)
                act.wait_ge(x_ready, c + 1)
                square(16 + c, xres[:, c, :])
            root(9, D)
            for c in range(8):
                operand(16 + c, ada[:, 24 + c:25 + c])
            for c in range(8):
                act.wait_ge(unit_done, U_Q + c + 1)
                upper_part(U_Q + c + SPLIT, U_Q + c + SPLIT)
                act.activation(qT[:, c, :], PS[:, (U_Q + c) % 3, :], ACT.Copy).then_inc(q_sb, 1)
            for n in range(TB * 4):
                act.wait_ge(score_ps, n + 1)
                act.activation(S[:, 4 * n:4 * n + 4, :].rearrange("p a b -> p (a b)"), PS[:, 3 + n % 2, :],
                               ACT.Copy).then_inc(score_sb, 1)

            def expert_act(u, k, r=None, first=False):
                at = (lambda v: v) if r is None else (lambda v: r + v)
                act.wait_ge(unit_done, at(U_EU + u + 1))
                upper_part(U_EU + u + SPLIT, k + SPLIT, r)
                b = (k // 2) % 2
                if not first and k % 2 == 0:
                    if r is None:
                        act.wait_ge(gel_st[b], 16 * (u // 4))
                    else:
                        act.wait_ge(gel_st[b], r * 4 + 16 * (u // 4))
                act.activation(gel[:, b, 512 * (k % 2):512 * (k % 2) + 512], PS[:, k % 2, :], ACT.Gelu).then_inc(gelu_done, 1)

            def store_gel(u, k, quad_index, r=None):
                b = (k // 2) % 2
                act.wait_ge(gelu_done, u + 1 if r is None else r + (u + 1))
                dst = gel_d[quad_index]
                dst = dst.rearrange("p c n -> p (c n)") if isinstance(quad_index, int) else \
                    dst.rearrange("a p c n -> (a p) (c n)")
                act.dma_start(dst[:, 1024 * b:1024 * b + 1024], gel[:, b, :]).then_inc(gel_st[b], 16)

            for u in range(4):
                expert_act(u, u, first=True)
                if u % 2:
                    store_gel(u, u, 0)
            with act.Fori(0, N1 // QUAD - 1) as r:
                for k in range(4):
                    expert_act(4 + k, k, r * 4)
                    if k % 2:
                        store_gel(4 + k, k, bass.ds(r + 1, 1), r * 4)
            act.wait_ge(ex_in, TB)
            act.activation(bestv[:, :, :], bestv[:, :, :], ACT.Exp).then_inc(ex_out, 1)
            for tb in range(TB):
                act.wait_ge(route_ps, tb + 1)
                act.activation(routeT[:, :, tb * P:(tb + 1) * P], PS[:, 2, 0:384].rearrange("p (a b) -> p a b", a=3),
                               ACT.Copy).then_inc(route_sb, 1)

            def gate_copy(g, k, b, r=None):
                at = (lambda v: v) if r is None else (lambda v: r + v)
                act.wait_ge(gate_ps, at(g + 1))
                t0 = (GROUP * k) % WT
                act.activation(stage_w[:, b, :].rearrange("p (j t) -> p j t", t=WT)[:, :, t0:t0 + GROUP],
                               PS[:, 2 + k % 4, :].rearrange("p (t j) -> p j t", t=GROUP), ACT.Copy).then_inc(gate_sb, 1)

            def eight(r=None):
                for k in range(8):
                    ru = None if r is None else r * 8
                    rg = None if r is None else r * 16
                    u = N1 + k + (0 if r is None else 8)
                    expert_act(u, k, ru)
                    if k % 2:
                        q0 = N1 // QUAD + k // 4
                        store_gel(u, k, q0 if r is None else bass.ds(r * 2 + (q0 + 2), 1), ru)
                    b = k // 4
                    if r is not None and k % 4 == 0:
                        act.wait_ge(gate_st[b], r * 16 + 16)
                    for g in (2 * k, 2 * k + 1):
                        gate_copy(g + (0 if r is None else 16), g, b, rg)
                    if k % 4 == 3:
                        n = 8 * (b + 1) + (0 if r is None else 16)
                        act.wait_ge(gate_sb, n if r is None else r * 16 + n)
                        if r is None:
                            dst = gates_d[:, :, b, :].rearrange("q p n -> p q n")
                        else:
                            dst = gates_d[:, :, bass.ds(r * 2 + (b + 2), 1), :].rearrange("q p a n -> p q (a n)")
                        act.dma_start(dst, stage_w[:, b, :].rearrange("p (q n) -> p q n", n=QUAD * WT)
                                      ).then_inc(gate_st[b], 16)

            act.wait_ge(routed_ready, TB)
            eight()
            with act.Fori(0, (N2 - N1) // 8 - 1) as r:
                eight(r)
            with act.Fori(0, (N_KEYS - N2) // QUAD) as r:
                for k in range(QUAD):
                    expert_act(N2 + k, k, r * 4)
                    if k % 2:
                        store_gel(N2 + k, k, bass.ds(r + N2 // QUAD, 1), r * 4)
            with act.Fori(0, N_KEYS // 4 - 1) as r:
                for k in range(4):
                    upper_part(U_EV + 2 + k, k + 2, r * 4)
            for u in range(N_KEYS - 2, N_KEYS + SPLIT):
                upper_part(U_EV + u, u)
            act.wait_ge(fg_ready, 1)
            for i, c in enumerate(X_ORDER):
                act.wait_ge(x_ready, 8 + i + 1)
                act.activation(act_hi[:, c, :], xres[:, c, :], ACT.Copy, scale=fgain[:, c:c + 1]).then_inc(ahi_ready, 1)
                if i >= 2:
                    act.wait_ge(sq_added, max(1, i - 2))
                square(24 + i, xres[:, c, :])
            root(10, D)
            upper_part(U_IN2 + 2, 2)
            act.wait_ge(mean_ready, 2)
            act.activation(rms[:, 1, :], tmp[:, 1, :], ACT.Sqrt, bias=eps).then_inc(rms_ready, 1)
            upper_part(U_IN2 + 3, 3)

            for st in STEPS2:
                kind, n, tb = st[0], st[1], st[-1]
                t = slice(tb * P, (tb + 1) * P)
                if kind == "unit":
                    act.wait_ge(unit_done, U_IN2 + n + 1)
                    if n >= 2 and U_IN2 + n + SPLIT < U_END:
                        upper_part(U_IN2 + n + SPLIT, n + SPLIT)
                    if 24 <= n < 32:
                        if n >= 26:
                            act.wait_ge(z_done, n - 25)
                        act.wait_ge(p_dve, n + 1)
                        src = az[:, n - 24, :] if n < 28 else dz[n - 28]
                        act.activation(tmp[:, n % 2, :], src, ACT.Tanh, scale=0.5).then_inc(z_th, 1)
                    if n >= 32:
                        act.activation(mx[:, n - 32, :], PS[:, n % 2, :], ACT.Copy).then_inc(mx_ready, 1)
                if kind == "tanh":
                    act.wait_ge(conv_done, n + 1)
                    if n >= 2:
                        act.wait_ge(cv_ready, n - 1)
                    act.activation(th2[:, n % 2, :], cv[:, n, :], ACT.Tanh).then_inc(th_ready, 1)
                if kind == "square":
                    act.wait_ge(cv_ready, n + 1)
                    square(32 + n, cv[:, n, :])
                if kind == "sum":
                    root(12 + n, 1)
                if kind == "rates_turned":
                    act.wait_ge(ba_sb, 1)
                    b3 = ba.rearrange("p (q n) -> p q n", n=8)
                    act.activation(beta.rearrange("p (q n) -> p q n", n=4), b3[:, :, 0:4], ACT.Tanh, scale=0.5).then_inc(rate_out, 1)
                    act.activation(ealog, col("alog", 0, 4), ACT.Exp).then_inc(rate_out, 1)
                    act.wait_ge(rate_in, 1)
                    act.activation(dexp, dax, ACT.Exp, scale=-1.0).then_inc(rate_out, 1)
                if kind == "cumulate":
                    act.wait_ge(cum_in, 1)
                    act.activation(egcum, gcum, ACT.Exp).then_inc(cum_out, 1)
                if kind == "decay":
                    wait_full(act, "gcr", tb)
                    if tb:
                        act.wait_ge(at_ready, tb)
                    act.wait_ge(dl_ready, tb + 1)
                    freed(act.activation(AO[:, 1, :], PS[:, bank("gcr", tb), :], ACT.Exp), "gcr", tb)
                    act.activation(AO[:, 0, :], AO[:, 0, :], ACT.Exp).then_inc(dt_ready, 1)
                if kind == "M":
                    wait_full(act, "m", n, tb)
                    if n or tb >= 2:
                        act.wait_ge(d_ready, 4 * n + tb + 3)
                    ins = act.activation(M1[:, tb % 2, :], PS[:, bank("m", n, tb), :], ACT.Copy)
                    ins.then_inc(m1_ready, 1)
                    act.wait_ge(m1_ready, 4 * n + tb + 1)
                    freed(act.nop(), "m", n, tb)
                if kind == "tokens":
                    wait_full(act, "kt", tb)
                    act.wait_ge(tok_dve, tb + 1)
                    for h in range(GH):
                        ins = act.activation(cv[:, 4 + h, t], PS[:, bank("kt", tb), h * P:(h + 1) * P], ACT.Copy,
                                             scale=egcum[:, 32 + 4 * tb + h:33 + 4 * tb + h])
                        ins.then_inc(kd_chain, 1)
                    act.wait_ge(kd_chain, 4 * (tb + 1))
                    freed(act.nop(), "kt", tb)
                    act.nop().then_inc(tok_act, 1)
                if kind == "solve":
                    wait_full(act, "wt", tb)
                    freed(act.activation(Dm[:, tb, :], PS[:, bank("wt", tb), :], ACT.Copy), "wt", tb)
                    wait_full(act, "u", tb)
                    act.activation(AT[:, tb, :], PS[:, bank("u", tb), :], ACT.Copy).then_inc(wu_ready, 1)
                    act.wait_ge(wu_ready, tb + 1)
                    freed(act.nop(), "u", tb)
                if kind == "scan":
                    wait_full(act, "o", tb)
                    act.activation(otok[:, :, t], h4(PS[:, bank("o", tb), :]), ACT.Copy).then_inc(o_ready, 1)
                    act.wait_ge(o_ready, tb + 1)
                    freed(act.nop(), "o", tb)
                if kind == "values":
                    wait_full(act, "av", tb)
                    if tb == 0:
                        act.wait_ge(lo_split, U_OUT2)
                    act.activation(avt[:, tb, :], PS[:, bank("av", tb), :], ACT.Copy).then_inc(avt_ready, 1)
                    act.wait_ge(avt_ready, tb + 1)
                    freed(act.nop(), "av", tb)
                if kind == "gsquare":
                    if n == 0:
                        act.wait_ge(bank_full[JOBS[("o", 0)] % 4], JOBS[("o", 0)] // 4 + 1)
                    for h in range(GH):
                        if n:
                            act.wait_ge(gsq_ready, 4 * (n - 1) + h + 1)
                        act.activation(gscratch[:, h, :], otok[:, h, t], ACT.Square,
                                       accum_out=gsum[:, 4 * n + h:4 * n + h + 1]).then_inc(gsq_ready, 1)
                if kind == "groot":
                    own = slice(0, 12) if n == 0 else slice(12, 16)
                    act.wait_ge(gsq_ready, own.stop)
                    act.activation(grms[:, own], gsum[:, own], ACT.Sqrt, bias=eps, scale=1.0 / P).then_inc(g_root, 1)
                if kind == "logits":
                    act.wait_ge(nm_ready, n + 1)
                    w = (n % 4 + 1) * P
                    act.activation(L[:, n % 3, 0:w], L[:, n % 3, 0:w], ACT.Exp, bias=nmax[:, n:n + 1],
                                   accum_out=psum_[:, n:n + 1]).then_inc(e_ready, 1)
                if kind == "turn":
                    w = (n % 4 + 1) * P
                    act.wait_ge(pt_full, n + 1)
                    if n >= 2:
                        act.wait_ge(pv_done, n - 1)
                    act.activation(PT[n % 2][:, 0:w], PS[:, 7, 0:w], ACT.Copy).then_inc(pt_ready, 1)
                if kind == "pv" and n % 8 == 7:
                    operand(32 + n // 8, chunk=n // 8)
                if kind == "gout":
                    act.wait_ge(pv_done, MH * TB)
                    for h in range(GH):
                        act.wait_ge(gn_done, h + 1)
                        act.activation(act_hi[:, 4 + h, :], gres[:, h, :], ACT.Copy).then_inc(ahi_ready, 1)
            root(20, D)

        @block.vector
        def _(dve):
            chain = Chain(dve, dve_chain)
            v = nc.vector

            def log1p(z, x, t1, t2, acc):
                chain.link(v.tensor_scalar(t1, x, 2.0, None, ALU.add))
                chain.link(v.reciprocal(t2, t1))
                chain.link(v.tensor_tensor(z, x, t2, ALU.mult))
                chain.link(v.tensor_tensor(t1, z, z, ALU.mult))
                chain.link(v.tensor_scalar(acc, t1, 1.0 / 19, 1.0 / 17, ALU.mult, ALU.add))
                for n in range(15, 0, -2):
                    chain.link(v.tensor_tensor(acc, acc, t1, ALU.mult))
                    chain.link(v.tensor_scalar(acc, acc, 1.0 / n, None, ALU.add))
                chain.link(v.tensor_tensor(acc, acc, z, ALU.mult))
                chain.link(v.tensor_scalar(acc, acc, 2.0, None, ALU.mult))

            def invert(index, read=0, by=None):
                dve.wait_ge(rms_ready, index + 1)
                if read:
                    dve.wait_ge(by or tmp_ready, read)
                v.reciprocal(rinv, rms[:, index % 2, :]).then_inc(rinv_ready, 1)
                dve.wait_ge(rinv_ready, index + 1)

            def scaled(n, src, gain):
                v.scalar_tensor_tensor(out=tmp[:, n % 2, :], in0=src, scalar=gain, in1=rinv, op0=ALU.mult,
                                       op1=ALU.mult).then_inc(tmp_ready, 1)

            def rest(n, shift=None, chunk=None):
                dve.wait_ge(tmp_ready, made(n))
                dve.wait_ge(ahi_ready, n + 1)
                k = n % 8 if chunk is None else chunk
                v.scalar_tensor_tensor(out=act_lo[:, k, :], in0=tmp[:, n % 2, :],
                                       scalar=0.0 if shift is None else shift,
                                       in1=act_hi[:, k, :].bitcast(F32), op0=ALU.add,
                                       op1=ALU.subtract).then_inc(alo_ready, 1)

            def normed(n0, index, gains, shift, last=(0, None)):
                if index is not None:
                    invert(index, *last)
                for c in range(9):
                    if c < 8:
                        if c >= 2:
                            dve.wait_ge(alo_ready, n0 + c - 1)
                        scaled(n0 + c, xres[:, c, :], gains[:, c:c + 1])
                    if c:
                        rest(n0 + c - 1, None if shift is None else shift[:, c - 1:c])

            def weighted(h):
                if h >= 2:
                    dve.wait_ge(ada_done, h - 1)
                for c in range(KC):
                    i = 2 * h + c // 4
                    if c % 4 == 0:
                        dve.wait_ge(ada_in[i % 4], 16 * (i // 4 + 1))
                    w = ada_w[:, i % 4, 512 * (c % 4):512 * (c % 4) + 512]
                    if c == 0:
                        ins = v.tensor_scalar(acc[:, h % 2, :], w, cs[:, 0:1], None, ALU.mult)
                    else:
                        ins = v.scalar_tensor_tensor(out=acc[:, h % 2, :], in0=w, scalar=cs[:, c:c + 1], in1=acc[:, h % 2, :],
                                                     op0=ALU.mult, op1=ALU.add)
                    chain.link(ins)
                    if c % 4 == 3:
                        dve.nop().then_inc(ada_used, 1)
                dve.nop().then_inc(ada_acc, 1)

            dve.wait_ge(consts_in, 16)
            dve.wait_ge(c_tanh, 1)
            chain.link(v.scalar_tensor_tensor(out=cth, in0=cth, scalar=1.0, in1=col("c", 0, 8), op0=ALU.add, op1=ALU.mult))
            v.tensor_scalar(cs, cth, 0.5, None, ALU.mult).then_inc(c_ready, 1)
            dve.wait_ge(c_ready, 1)
            for h in range(3):
                weighted(h)
            invert(0)
            weighted(3)
            dve.wait_ge(ada_done, 4)
            chain.link(v.tensor_tensor(ada[:, 0:16], PS[:, 5, 0:16], col("bada", 0, 16), ALU.add))
            chain.link(v.scalar_tensor_tensor(out=gain1, in0=ada[:, 8:16], scalar=1.0, in1=col("n1", 0, 8),
                                              op0=ALU.add, op1=ALU.mult))
            normed(0, None, gain1, ada[:, 0:8])
            lam = col("lam", 0, 4)
            chain.link(v.tensor_scalar(sp[2], lam, -1.0, None, ALU.mult))
            v.tensor_tensor(sp[0], lam, sp[2], ALU.max).then_inc(lam_neg, 1)
            chain.link(v.tensor_scalar(hbr, col("br", 0, 4), 0.5, None, ALU.mult))
            chain.link(v.tensor_scalar(hbi, col("bi", 0, 4), 0.5, None, ALU.mult))
            dve.wait_ge(lam_exp, 1)
            log1p(sp[3], sp[1], sp[4], sp[5], sp[0])
            chain.link(v.tensor_scalar(sp[2], sp[2], 0.0, None, ALU.max))
            chain.link(v.tensor_tensor(sp[2], sp[2], sp[0], ALU.add))
            v.tensor_scalar(dec, sp[2], -2.0, None, ALU.mult).then_inc(dec_ready, 1)
            dve.wait_ge(ba_hi_r, 1)
            v.tensor_tensor(ba_lo[:, :, :].rearrange("p c n -> p (c n)"), ba_w[:, :],
                            ba_hi[:, :, :].rearrange("p c n -> p (c n)").bitcast(F32), ALU.subtract).then_inc(ba_lo_r, 1)

            for m in range(4):
                if m < 2:
                    weighted(4 + m)
                dve.wait_ge(z_act, m + 1)
                if m == 0:
                    dve.wait_ge(pool_made, 2)
                w = [col("cbw", 4 * k + m) for k in range(4)]
                chain.link(v.tensor_scalar(xc[:, m, :], xrp[:, m, 0:512], w[0], col("cbb", m), ALU.mult, ALU.add))
                for k in range(1, 4):
                    ins = v.scalar_tensor_tensor(out=xc[:, m, :], in0=xrp[:, m, k:k + 512], scalar=w[k],
                                                 in1=xc[:, m, :], op0=ALU.mult, op1=ALU.add)
                    if k < 3:
                        chain.link(ins)
                    else:
                        ins.then_inc(xc_ready, 1)

            def recur_1(g):
                dve.wait_ge(s_ready, g + 1)
                if g:
                    dve.wait_ge(s_used, g)
                    chain.wait()
                chain.link(v.tensor_scalar(lru_q, tr[:, g, :], -1.0, 1.0, ALU.mult, ALU.add))
                chain.link(v.reciprocal(lru_q, lru_q))
                chain.link(v.scalar_tensor_tensor(out=ti[:, g, :], in0=ti[:, g, :], scalar=1.0, in1=xc[:, g, :],
                                                  op0=ALU.add, op1=ALU.mult))
                chain.post(v.tensor_tensor(ti[:, g, :], ti[:, g, :], lru_q, ALU.mult))
                v.scalar_tensor_tensor(out=xc[:, g, :], in0=tr[:, g, :], scalar=1.0, in1=lru_q, op0=ALU.add,
                                       op1=ALU.mult).then_inc(s_used, 1)

            def recur_2(g):
                dve.wait_ge(root_ready, g + 1)
                chain.link(v.tensor_tensor(ti[:, g, :], ti[:, g, :], tr[:, g, :], ALU.mult))
                chain.link(v.tensor_tensor_scan(tr[:, g, :], xc[:, g, :], ti[:, g, :], 0.0, ALU.mult, ALU.add))
                v.tensor_tensor(y[:, 4 + g, :], tr[:, g, :], gg[:, g, :], ALU.mult).then_inc(y_ready, 1)

            def scale_y(i):
                c = Y_ORDER[i]
                if i:
                    invert(1 + i, i, y_scaled)
                else:
                    invert(1, 8)
                v.scalar_tensor_tensor(out=y[:, c, :], in0=y[:, c, :], scalar=col("gn", c), in1=rinv, op0=ALU.mult,
                                       op1=ALU.mult).then_inc(y_scaled, 1)

            for u in range(8, U_OUT):
                kind, m = z_of(u)
                if kind == "gc":
                    dve.wait_ge(unit_done, u + 1)
                    dve.wait_ge(z_act, 9 + m)
                    chain.wait()
                    ins = v.tensor_tensor(pc[:, m % 2, 2:514], PS[:, u % 3, :], xa[:, m % 2, :], ALU.mult)
                    ins.then_inc(z_dve, 1)
                    dve.wait_ge(z_dve, 2 * m + 1)
                    w = [col("caw", 4 * k + m) for k in range(3)]
                    chain.link(v.tensor_scalar(y[:, m, :], pc[:, m % 2, 0:512], w[0], None, ALU.mult))
                    for k in range(1, 3):
                        chain.link(v.scalar_tensor_tensor(out=y[:, m, :], in0=pc[:, m % 2, k:k + 512], scalar=w[k],
                                                          in1=y[:, m, :], op0=ALU.mult, op1=ALU.add))
                if kind == "gb":
                    dve.wait_ge(unit_done, u + 1)
                    v.tensor_tensor(y[:, m, :], PS[:, u % 3, :], y[:, m, :], ALU.mult).then_inc(z_dve, 1)
                    dve.wait_ge(z_dve, 2 * m + 2)
                    dve.nop().then_inc(y_ready, 1)
                if GATES + 3 <= u < GATES + 7:
                    recur_1(u - GATES - 3)
                if GATES + 8 <= u < GATES + 12:
                    recur_2(u - GATES - 8)
                for i in range(8):
                    if Y_SCALE[i] == u:
                        scale_y(i)
            chain.wait()
            dve.wait_ge(ada_done, 6)
            chain.link(v.tensor_tensor(ada[:, 16:24], PS[:, 5, 16:24], col("bada", 16, 8), ALU.add))
            for i in range(8):
                if Y_SCALE[i] == 20:
                    scale_y(i)
                dve.wait_ge(ahi_ready, 8 + i + 1)
                v.tensor_tensor(act_lo[:, Y_ORDER[i], :], y[:, Y_ORDER[i], :], act_hi[:, Y_ORDER[i], :].bitcast(F32),
                                ALU.subtract).then_inc(alo_ready, 1)
            def add_square(c):
                dve.wait_ge(sq_ready, 16 + c + 1)
                if c:
                    dve.wait_ge(sq_used, 16 + c)
                    ins = v.tensor_tensor(rms[:, 0, :], rms[:, 0, :], sq[:, c % 2, :], ALU.add)
                else:
                    dve.wait_ge(rinv_ready, 9)
                    ins = v.tensor_copy(rms[:, 0, :], sq[:, 0, :])
                ins.then_inc(sq_used, 1)

            for c in range(8):
                if c < 4:
                    weighted(6 + c)
                if c == 6:
                    dve.wait_ge(ada_done, 10)
                    chain.link(v.tensor_tensor(ada[:, 24:40], PS[:, 5, 24:40], col("bada", 24, 16), ALU.add))
                    chain.link(v.scalar_tensor_tensor(out=gain2, in0=ada[:, 32:40], scalar=1.0, in1=col("n2", 0, 8),
                                                      op0=ALU.add, op1=ALU.mult))
                dve.wait_ge(unit_done, U_OUT + c + 1)
                v.scalar_tensor_tensor(out=xres[:, c, :], in0=PS[:, (U_OUT + c) % 3, :], scalar=ada[:, 16 + c:17 + c],
                                       in1=xres[:, c, :], op0=ALU.mult, op1=ALU.add).then_inc(x_ready, 1)
                if c:
                    add_square(c - 1)
            add_square(7)
            dve.wait_ge(x_ready, 8)
            normed(16, 9, gain2, ada[:, 24:32], (8, y_scaled))
            for h in (10, 11):
                weighted(h)
            dve.wait_ge(ada_done, 12)
            chain.link(v.tensor_tensor(ada[:, 40:48], PS[:, 5, 40:48], col("bada", 40, 8), ALU.add))

            iota16 = iota[:, 0:16]
            for tb in range(TB):
                if tb:
                    chain.wait()
                for h in range(HEADS):
                    if h % 2 == 0:
                        dve.wait_ge(score_sb, 4 * tb + h // 2 + 1)
                    for c in range(2):
                        n = 2 * h + c
                        s = S[:, 16 * tb + n, :]
                        r = rep[:, 128 * c:128 * c + 128]
                        if h:
                            dve.wait_ge(dve_chain, chain.n - 5)
                        chain.link(v.max(topv[:, n, 0:8], s))
                        chain.post(v.max_index(topi[:, n, 0:8], topv[:, n, 0:8], s))
                        chain.link(v.match_replace(r, topv[:, n, 0:8], s, LOWEST))
                        chain.link(v.max(topv[:, n, 8:16], r))
                        chain.post(v.max_index(topi[:, n, 8:16], topv[:, n, 8:16], r))
                chain.wait()
                chain.post(v.tensor_copy(topf[:, :, :], topi[:, :, :]))
                tv = topv[:, :, :].rearrange("p (h c) k -> p h c k", c=2)
                for h in range(HEADS):
                    chain.post(v.tensor_tensor(cand[:, h, :].rearrange("p (a b) -> p a b", a=16),
                                               tv[:, h, 0, :].unsqueeze(2).to_broadcast([P, 16, 16]),
                                               tv[:, h, 1, :].unsqueeze(1).to_broadcast([P, 16, 16]), ALU.add))
                chain.wait()
                for h in range(HEADS):
                    s = cand[:, h, :]
                    best = bestv[:, HEADS * tb + h, :]
                    chain.link(v.max(best[:, 0:8], s))
                    chain.post(v.max_index(bestp[:, h, 0:8], best[:, 0:8], s))
                    if h:
                        dve.wait_ge(dve_chain, chain.n - 2)
                    chain.link(v.match_replace(rep, best[:, 0:8], s, LOWEST))
                    chain.link(v.max(best[:, 8:16], rep))
                    chain.post(v.max_index(bestp[:, h, 8:16], best[:, 8:16], rep))
                chain.wait()
                bv = bestv[:, HEADS * tb:HEADS * tb + HEADS, :]
                zt = zs[:, 0, HEADS * tb:HEADS * tb + HEADS]
                chain.post(v.tensor_copy(zt, bv[:, :, 0]))
                bp = bestp[:, :, :].rearrange("p h k -> p (h k)")
                chain.post(v.tensor_single_scalar(pick[:, 0, :], bp, 4, ALU.logical_shift_right))
                chain.post(v.tensor_single_scalar(pick[:, 1, :], bp, 15, ALU.bitwise_and))
                chain.wait()
                v.tensor_tensor(bv, bv, zt.unsqueeze(2).to_broadcast([P, HEADS, TOPK]), ALU.subtract).then_inc(ex_in, 1)
                chain.link(v.tensor_copy(pickf[:, :, :], pick[:, :, :]))
                tf = topf[:, :, :].rearrange("p (h c) k -> p h c k", c=2)
                for c in range(2):
                    e3 = eq.rearrange("p (n a) -> p n a", a=16)
                    chain.link(v.tensor_tensor(e3, pickf[:, c, :].unsqueeze(2).to_broadcast([P, 128, 16]),
                                               iota16.unsqueeze(1).to_broadcast([P, 128, 16]), ALU.is_equal))
                    for h in range(HEADS):
                        eh = eq[:, 256 * h:256 * h + 256].rearrange("p (n a) -> p n a", a=16)
                        chain.post(v.tensor_tensor(eh, eh, tf[:, h, c, :].unsqueeze(1).to_broadcast([P, 16, 16]), ALU.mult))
                    chain.wait()
                    chain.link(v.tensor_reduce(routed_sb[tb][:, c, :], e3, AX_X, ALU.add))
            dve.wait_ge(ex_out, 1)
            chain.link(v.tensor_reduce(zs[:, 0, :], bestv[:, :, :], AX_X, ALU.add))
            chain.link(v.reciprocal(zs[:, 1, :], zs[:, 0, :]))
            for tb in range(TB):
                own = slice(HEADS * tb, HEADS * tb + HEADS)
                v.tensor_tensor(routed_sb[tb][:, 2, :].rearrange("p (h k) -> p h k", h=HEADS), bestv[:, own, :],
                                zs[:, 1, own].unsqueeze(2).to_broadcast([P, HEADS, TOPK]), ALU.mult).then_inc(routed_ready, 1)

            def hot(g, r=None, rt=None, first=False):
                if not first:
                    dve.wait_ge(gate_ps, g - 3 if r is None else r + (g - 3))
                for t in range(GROUP):
                    tok = GROUP * g + t
                    s = tok % ONEHOT
                    at = slice(tok, tok + 1) if r is None else bass.ds(rt + tok, 1)
                    v.tensor_scalar(hot_i[:, s, :], iota[:, :], routeT[:, 0, at], None, ALU.is_equal)
                    ins = v.tensor_scalar(hot_j[:, s, :], iota[:, :], routeT[:, 1, at], routeT[:, 2, at],
                                          ALU.is_equal, ALU.mult)
                ins.then_inc(hot_ready, 1)

            dve.wait_ge(route_sb, TB)
            for g in range(4):
                hot(g, first=True)
            with dve.Fori(0, T // GROUP // 4 - 1) as r:
                for g in range(4):
                    hot(4 + g, r * 4, r * 16)

            def weigh(b, q, kq, r=None, first=False):
                at = (lambda n: n) if r is None else (lambda n: r + n)
                k = b % 2
                if not first:
                    dve.wait_ge(clo_ready, at(b - 1))
                g = gate_q[:, q, :].rearrange("p (c j t) -> p c j t", j=QUAD, t=WT)[:, :, kq, :]
                e = gel_q[:, q, 512 * kq:512 * kq + 512].rearrange("p (c t) -> p c t", t=WT)
                v.tensor_tensor(craw[:, k, :].rearrange("p (c t) -> p c t", t=WT), g, e, ALU.mult).then_inc(craw_ready, 1)
                dve.wait_ge(craw_ready, at(b + 1))
                dve.wait_ge(unit_done, U_EV if first else at(U_EV + b - 1))
                v.tensor_copy(act_hi[:, k, :], craw[:, k, :]).then_inc(chi_ready, 1)
                dve.wait_ge(chi_ready, at(b + 1))
                v.tensor_tensor(act_lo[:, k, :], craw[:, k, :], act_hi[:, k, :].bitcast(F32),
                                ALU.subtract).then_inc(clo_ready, 1)

            dve.wait_ge(gate_ps, T // GROUP)
            for q in range(2):
                dve.wait_ge(gq_in[q], 16)
                dve.wait_ge(eq_in[q], 16)
                for kq in range(QUAD):
                    weigh(4 * q + kq, q, kq, first=(4 * q + kq < 2))
            with dve.Fori(0, NQ // 2 - 1) as r:
                for q in range(2):
                    dve.wait_ge(gq_in[q], r * 16 + 32)
                    dve.wait_ge(eq_in[q], r * 16 + 32)
                    for kq in range(QUAD):
                        weigh(8 + 4 * q + kq, q, kq, r * 8)
            chain.post(v.tensor_tensor(fgain, col("fin", 0, 8), col("pre2", 0, 8), ALU.mult))
            chain.link(v.tensor_tensor(fsq, col("fin", 0, 8), col("fin", 0, 8), ALU.mult))
            for c in range(KC):
                chain.post(v.tensor_scalar(fin2[:, c, :], ones[:, :], fsq[:, c:c + 1], None, ALU.mult))
            chain.wait()
            dve.nop().then_inc(fg_ready, 1)
            dve.wait_ge(fg_ready, 1)
            dve.wait_ge(unit_done, U_IN2)
            for i in range(9):
                if i < 8:
                    c = X_ORDER[i]
                    v.scalar_tensor_tensor(out=xres[:, c, :], in0=PS[:, c, :], scalar=ada[:, 40 + c:41 + c],
                                           in1=xres[:, c, :], op0=ALU.mult, op1=ALU.add).then_inc(x_ready, 1)
                if i:
                    c = X_ORDER[i - 1]
                    dve.wait_ge(x_ready, 8 + i)
                    dve.wait_ge(ahi_ready, 24 + i)
                    v.scalar_tensor_tensor(out=act_lo[:, c, :], in0=xres[:, c, :], scalar=fgain[:, c:c + 1],
                                           in1=act_hi[:, c, :].bitcast(F32), op0=ALU.mult,
                                           op1=ALU.subtract).then_inc(alo_ready, 1)
            v.memset(cin[:, :, 0:4], 0.0).then_inc(pads_ready, 1)
            chain.post(v.tensor_scalar(hgdn, col("gdn"), 0.5, None, ALU.mult))
            chain.link(v.tensor_scalar(hc2w, col("c2w", 0, 48), 0.5, None, ALU.mult))
            dve.wait_ge(sum_ready, 12)
            invert(10, 16)
            v.scalar_tensor_tensor(out=tmp[:, 0, :], in0=PS[:, 7, :], scalar=1.0 / D, in1=rinv, op0=ALU.mult,
                                   op1=ALU.mult).then_inc(mean_ready, 1)
            dve.wait_ge(mean_ready, 1)
            v.tensor_tensor(tmp[:, 1, :], tmp[:, 0, :], rinv, ALU.mult).then_inc(mean_ready, 1)
            dve.wait_ge(rms_ready, 12)
            v.reciprocal(rr, rms[:, 1, :]).then_inc(rinv_ready, 1)
            dve.wait_ge(rinv_ready, 12)
            v.tensor_tensor(rr, rr, rinv, ALU.mult).then_inc(rr_ready, 1)
            dve.wait_ge(rr_ready, 1)

            def per_head(dst, name, scalars, at, ops=(ALU.mult,), second=None, last=None):
                wait_full(dve, *name)
                for h in range(GH):
                    chain.post(v.tensor_scalar(h4(dst)[:, h, :], PS[:, bank(*name), h * P:(h + 1) * P],
                                               scalars[:, at + h:at + h + 1], second, *ops))

            def all_heads(ap):
                return ap.unsqueeze(1).to_broadcast([P, GH, P])

            for st in STEPS2:
                kind, n, tb = st[0], st[1], st[-1]
                t = slice(tb * P, (tb + 1) * P)
                if kind == "conv":
                    if n < 12:
                        dve.wait_ge(unit_done, U_IN2 + n + 1)
                        if n >= 2:
                            dve.wait_ge(conv_done, n - 1)
                        else:
                            dve.wait_ge(pads_ready, 1)
                        v.tensor_tensor(cin[:, n % 2, 3:515], PS[:, unit_bank(n), :], rr, ALU.mult).then_inc(p_dve, 1)
                    if n < 12:
                        w = [hc2w[:, 12 * k + n:12 * k + n + 1] for k in range(4)]
                        dve.wait_ge(p_dve, n + 1)
                        chain.link(v.tensor_scalar(cv[:, n, :], cin[:, n % 2, 0:512], w[0], None, ALU.mult))
                        for k in range(1, 4):
                            ins = v.scalar_tensor_tensor(out=cv[:, n, :], in0=cin[:, n % 2, k:k + 512], scalar=w[k],
                                                         in1=cv[:, n, :], op0=ALU.mult, op1=ALU.add)
                            if k < 3:
                                chain.link(ins)
                            else:
                                ins.then_inc(conv_done, 1)
                    if n >= 1:
                        dve.wait_ge(th_ready, n)
                        v.scalar_tensor_tensor(out=cv[:, n - 1, :], in0=th2[:, (n - 1) % 2, :], scalar=1.0,
                                               in1=cv[:, n - 1, :], op0=ALU.add, op1=ALU.mult).then_inc(cv_ready, 1)
                if kind == "unit" and 12 <= n < 32:
                    dve.wait_ge(unit_done, U_IN2 + n + 1)
                    if n < 16:
                        v.scalar_tensor_tensor(out=aq[:, n - 12, :], in0=PS[:, n % 2, :], scalar=0.125, in1=rr,
                                               op0=ALU.mult, op1=ALU.mult).then_inc(p_dve, 1)
                    else:
                        dst = ak[:, n - 16, :] if n < 20 else av[:, n - 20, :] if n < 24 else \
                            az[:, n - 24, :] if n < 28 else dz[n - 28]
                        if n == 31:
                            dve.wait_ge(conv_done, 12)
                        v.tensor_tensor(dst, PS[:, n % 2, :], rr, ALU.mult).then_inc(p_dve, 1)
                if kind == "unit" and n >= 32:
                    c = n - 32
                    dve.wait_ge(mx_ready, c + 1)
                    chain.link(v.tensor_tensor(sq[:, min(c, 1), :], mx[:, c, :], mx[:, c, :], ALU.mult))
                    if c:
                        chain.link(v.tensor_tensor(sq[:, 0, :], sq[:, 0, :], sq[:, 1, :], ALU.add))
                    if c == KC - 1:
                        dve.nop().then_inc(mix_squared, 1)
                if (kind == "unit" and 25 <= n < 32) or (kind == "values" and n == 0):
                    k = n - 25 if kind == "unit" else 7
                    dve.wait_ge(z_th, k + 1)
                    dve.wait_ge(p_dve, 25 + k)
                    dst = az[:, k, :] if k < 4 else dz[k - 4]
                    v.scalar_tensor_tensor(out=dst, in0=tmp[:, k % 2, :], scalar=1.0, in1=dst,
                                           op0=ALU.add, op1=ALU.mult).then_inc(z_done, 1)
                if kind == "rates":
                    wait_full(dve, "ba")
                    dve.wait_ge(cv_ready, 12)
                    v.tensor_tensor(th2[0:8, 0, :], PS[0:8, bank("ba"), :], rr[0:8, :], ALU.mult).then_inc(ba_row, 1)
                    dve.wait_ge(ba_row, 1)
                    freed(dve.nop(), "ba")
                if kind == "rates_turned":
                    wait_full(dve, "bat")
                    b3 = ba.rearrange("p (q n) -> p q n", n=8)
                    freed(v.tensor_copy(ba, PS[:, bank("bat"), 0:32]), "bat")
                    dve.wait_ge(bank_free[JOBS[("bat",)] % 4], 1)
                    dve.nop().then_inc(ba_sb, 1)
                    chain.link(v.tensor_tensor(dx.rearrange("p (q n) -> p q n", n=4), b3[:, :, 4:8],
                                               col("dtb", 0, 4).unsqueeze(1).to_broadcast([P, TB, 4]), ALU.add))
                    chain.link(v.tensor_scalar(dt1, dx, -1.0, None, ALU.mult))
                    v.tensor_tensor(dax, dx, dt1, ALU.max).then_inc(rate_in, 1)
                    dve.wait_ge(rate_in, 1)
                    dve.wait_ge(rate_out, 3)
                    log1p(dz_, dexp, dt1, dt2, dacc)
                    chain.link(v.tensor_scalar(dx, dx, 0.0, None, ALU.max))
                    chain.link(v.tensor_tensor(dacc, dacc, dx, ALU.add))
                    chain.link(v.tensor_tensor(dacc.rearrange("p (q n) -> p q n", n=4), dacc.rearrange("p (q n) -> p q n", n=4),
                                               ealog.unsqueeze(1).to_broadcast([P, TB, 4]), ALU.mult))
                    chain.link(v.tensor_scalar(beta, beta, 0.5, 0.5, ALU.mult, ALU.add))
                    v.tensor_scalar(rate, dacc, -1.0, None, ALU.mult).then_inc(rate_ready, 1)
                    dve.wait_ge(rate_ready, 1)
                if kind == "scale":
                    if n:
                        invert(12 + n, n, norm_ready)
                    else:
                        invert(12, 8, x1_ready)
                    v.scalar_tensor_tensor(out=cv[:, n, :], in0=cv[:, n, :], scalar=float(P) ** -0.5 if n < 4 else 1.0,
                                           in1=rinv, op0=ALU.mult, op1=ALU.mult).then_inc(norm_ready, 1)
                if kind == "cumulate":
                    wait_full(dve, "cum")
                    chain.link(v.tensor_copy(gcum[:, 0:32], PS[:, bank("cum"), 0:32]))
                    freed(dve.nop(), "cum")
                    chain.post(v.tensor_scalar(ngc, gcum[:, 0:16], -1.0, None, ALU.mult))
                    v.tensor_tensor(gcum[:, 32:48], gcum[:, 16:32], gcum[:, 0:16], ALU.subtract).then_inc(cum_in, 1)
                    dve.wait_ge(cum_out, 1)
                    chain.link(v.tensor_tensor(bge, beta, egcum[:, 0:16], ALU.mult))
                if kind == "rows":
                    if tb:
                        wait_full(dve, "br", tb - 1)
                    for h in range(GH):
                        k = 4 * tb + h
                        chain.post(v.tensor_scalar(h4(M1[:, 0, :])[:, h, :], upper[:, :], rate[:, k:k + 1], None, ALU.mult))
                        chain.post(v.tensor_scalar(h4(M1[:, 1, :])[:, h, :], ident[:, :], beta[:, k:k + 1], None, ALU.mult))
                    chain.post(v.tensor_copy(h4(Dm[:, tb, :]), all_heads(ident[:, :])))
                    chain.post(v.tensor_copy(h4(DTm[:, tb, :]), all_heads(ident[:, :])))
                    chain.wait()
                    dve.nop().then_inc(rows_in, 1)
                    dve.nop().then_inc(d_ready, 1)
                if kind == "decay":
                    per_head(AO[:, 0, :], ("gcr", tb), ngc, 4 * tb, (ALU.add, ALU.min), 0.0)
                    chain.wait()
                    freed(dve.nop(), "gcr", tb)
                    dve.nop().then_inc(dl_ready, 1)
                    dve.wait_ge(dt_ready, tb + 1)
                    wait_full(dve, "br", tb)
                    chain.link(v.tensor_tensor(KBd, AO[:, 0, :], PS[:, bank("br", tb), :], ALU.mult))
                    freed(dve.nop(), "br", tb)
                    wait_full(dve, "kk", tb)
                    chain.post(v.tensor_tensor(AT[:, tb, :], KBd, PS[:, bank("kk", tb), :], ALU.mult))
                    wait_full(dve, "qk", tb)
                    chain.link(v.tensor_tensor(IT[:, tb, :], AO[:, 0, :], PS[:, bank("qk", tb), :], ALU.mult))
                    freed(dve.nop(), "kk", tb)
                    freed(dve.nop(), "qk", tb)
                    chain.post(v.tensor_tensor(h4(IT[:, tb, :]), h4(IT[:, tb, :]), all_heads(upper[:, :]), ALU.mult))
                    chain.link(v.tensor_tensor(cv[:, 0:4, t], cv[:, 0:4, t], h4(AO[:, 1, :]), ALU.mult))
                    dve.nop().then_inc(at_ready, 1)
                if kind == "X":
                    if n < LEVELS - 1:
                        wait_full(dve, "x", n, tb)
                    wait_full(dve, "xt", n, tb)
                    chain.post(v.tensor_tensor(DTm[:, tb, :], DTm[:, tb, :], PS[:, bank("xt", n, tb), :], ALU.subtract))
                    if n < LEVELS - 1:
                        chain.post(v.tensor_tensor(Dm[:, tb, :], Dm[:, tb, :], PS[:, bank("x", n, tb), :], ALU.subtract))
                    chain.wait()
                    if n < LEVELS - 1:
                        freed(dve.nop(), "x", n, tb)
                    freed(dve.nop(), "xt", n, tb)
                    dve.nop().then_inc(d_ready, 1)
                if kind == "tokens":
                    if tb == 0:
                        dve.wait_ge(lo_split, U_OUT2 + 2)
                    if tb >= 2:
                        wait_full(dve, "u", tb - 2)
                    per_head(KB[:, tb % 2, :], ("kt", tb), bge, 4 * tb)
                    per_head(VB[:, tb % 2, :], ("vt", tb), beta, 4 * tb)
                    chain.wait()
                    freed(dve.nop(), "kt", tb)
                    freed(dve.nop(), "vt", tb)
                    dve.nop().then_inc(tok_dve, 1)
                if kind == "read" and tb:
                    wait_full(dve, "ws", tb)
                    v.tensor_tensor(M1[:, tb % 2, :], AT[:, tb, :], PS[:, bank("ws", tb), :], ALU.subtract).then_inc(vn_ready, 1)
                    dve.wait_ge(vn_ready, tb)
                    freed(dve.nop(), "ws", tb)
                if kind == "scan":
                    if tb < TB - 1:
                        wait_full(dve, "su", tb)
                        if tb == 0:
                            dve.wait_ge(p_dve, 32)
                        if tb == 0:
                            chain.link(v.tensor_copy(state, PS[:, bank("su", tb), :]))
                        else:
                            for h in range(GH):
                                s_ = h4(state)[:, h, :]
                                k = 16 + 4 * tb + h
                                chain.post(v.scalar_tensor_tensor(out=s_, in0=s_, scalar=egcum[:, k:k + 1],
                                                                  in1=PS[:, bank("su", tb), h * P:(h + 1) * P],
                                                                  op0=ALU.mult, op1=ALU.add))
                            chain.wait()
                        freed(dve.nop(), "su", tb)
                        dve.nop().then_inc(state_ready, 1)
                if kind == "groot":
                    own = slice(0, 12) if n == 0 else slice(12, 16)
                    dve.wait_ge(g_root, n + 1)
                    chain.link(v.reciprocal(gsum[:, own], grms[:, own]))
                    for k in range(own.start, own.stop):
                        o = otok[:, k % 4, (k // 4) * P:(k // 4 + 1) * P]
                        v.tensor_scalar(o, o, gsum[:, k:k + 1], None, ALU.mult).then_inc(g_scaled, 1)
                if kind == "gturn":
                    dve.wait_ge(wu_ready, TB)
                    for h in range(GH):
                        wait_full(dve, "gt", h)
                        v.scalar_tensor_tensor(out=gres[:, h, :], in0=PS[:, bank("gt", h), :], scalar=hgdn, in1=dz[h],
                                               op0=ALU.mult, op1=ALU.mult).then_inc(gn_done, 1)
                    dve.wait_ge(gn_done, GH)
                    for h in range(GH):
                        freed(dve.nop(), "gt", h)
                if kind == "gout":
                    dve.wait_ge(pv_done, MH * TB)
                    for h in range(GH):
                        dve.wait_ge(ahi_ready, 36 + h + 1)
                        v.tensor_tensor(act_lo[:, 4 + h, :], gres[:, h, :], act_hi[:, 4 + h, :].bitcast(F32),
                                        ALU.subtract).then_inc(alo_ready, 1)
                if kind == "logits":
                    m, e, qb = n // 8, n // 4 % 2, n % 4
                    w = (qb + 1) * P
                    dve.wait_ge(s_full, n + 1)
                    if n == 0:
                        dve.wait_ge(avt_ready, TB)
                    if n >= 3:
                        dve.wait_ge(pt_full, n - 2)
                    slope = 2.0 ** -(2 * m + e + 1)
                    v.scalar_tensor_tensor(out=L[:, n % 3, 0:w], in0=ND[:, 512 - w:512], scalar=slope,
                                           in1=PS[:, 6, 0:w], op0=ALU.mult, op1=ALU.add).then_inc(l_ready, 1)
                    dve.wait_ge(l_ready, n + 1)
                    v.tensor_reduce(nmax[:, n:n + 1], L[:, n % 3, 0:w], AX_X, ALU.max, negate=True).then_inc(nm_ready, 1)
                if kind == "probs":
                    w = (n % 4 + 1) * P
                    dve.wait_ge(e_ready, n + 1)
                    chain.link(v.reciprocal(prec[:, n:n + 1], psum_[:, n:n + 1]))
                    v.tensor_scalar(L[:, n % 3, 0:w], L[:, n % 3, 0:w], prec[:, n:n + 1], None, ALU.mult).then_inc(p_ready, 1)
                if kind == "pv" and n % 8 == 7:
                    m = n // 8
                    dve.wait_ge(pv_done, n + 1)
                    if m == 0:
                        dve.wait_ge(z_done, 8)
                    else:
                        dve.wait_ge(alo_ready, 32 + m)
                    v.scalar_tensor_tensor(out=tmp[:, m % 2, :], in0=PS[:, m % 2, :], scalar=0.5, in1=az[:, m, :],
                                           op0=ALU.mult, op1=ALU.mult).then_inc(tmp_ready, 1)
                    dve.wait_ge(tmp_ready, made(32 + m))
                    dve.nop().then_inc(om_ready, 1)
                    rest(32 + m, chunk=m)
            dve.wait_ge(x1_ready, 8)
            dve.wait_ge(gn_done, GH)
            invert(20)
            for c in range(8):
                chain.link(v.scalar_tensor_tensor(out=mx[:, c, :], in0=mx[:, c, :], scalar=col("post2", c), in1=rinv,
                                                  op0=ALU.mult, op1=ALU.mult))
                v.scalar_tensor_tensor(out=xres[:, c, :], in0=xres[:, c, :], scalar=col("fin", c), in1=mx[:, c, :],
                                       op0=ALU.mult, op1=ALU.add).then_inc(out_ready, 1)


def units(w, order=None):
    import numpy as np
    n = w.shape[1] // P
    u = w.reshape(KC, P, n, P).transpose(2, 1, 0, 3).reshape(n, P, D)
    return np.ascontiguousarray(u if order is None else u[order])


def kernel(**inputs):
    import numpy as _np
    import concourse.bacc as _bacc
    from concourse import mybir as _mybir
    from concourse.bass_utils import run_bass_kernel_spmd as _run

    a = {k: _np.asarray(v) for k, v in inputs.items()}
    w_in = list(range(12, 20)) + [b * 4 + m for m in range(4) for b in (2, 1, 0)]
    e = {
        "x": a["x"][0].T,
        "w_ada": a["w_ada"][0].reshape(KC, P, 12, 512).transpose(2, 1, 0, 3).reshape(12, P, 4096),
        "w_in": units(a["w_in"][0], w_in),
        "w_out": units(a["w_out"][0]),
        "w_q": units(a["w_q"][0]),
        "w_r": a["w_r"][0],
        "w_i": a["w_i"][0],
        "keys": a["sub_keys"][0].transpose(1, 3, 0, 2),
        "expert_u": a["expert_u"][0].reshape(N_KEYS, N_KEYS, KC, P).transpose(1, 3, 2, 0).reshape(N_KEYS, P, D),
        "expert_v": a["expert_v"][0].reshape(N_KEYS, N_KEYS, D).transpose(1, 0, 2),
    }
    w2 = a["w_in_2"][0]
    e["w_in2"] = units(w2[:, :4096], [4 * b + m for b in (4, 5, 6, 0, 1, 2, 3, 7) for m in range(4)])
    e["w_out2"] = units(a["w_out_2"][0])
    e["w_ba"] = w2[:, 4096:].reshape(KC, P, 8).transpose(1, 0, 2).reshape(P, 64)
    vectors = dict(n1=a["norm1_g"], n2=a["norm2_g"], fin=a["final_g"], pre2=a["norm_pre_w_2"], post2=a["norm_post_w_2"],
                   gn=_np.concatenate([a["gn_a"], a["gn_b"]], axis=-1), cbb=a["conv_b_b"], br=a["b_r"], bi=a["b_i"],
                   lam=a["lru_lambda"], gdn=a["gdn_norm_w_2"], caw=a["conv_a_w"], cbw=a["conv_b_w"], c2w=a["conv_w_2"],
                   bada=a["b_ada"], c=a["c"], alog=_np.repeat(a["a_log_2"][0], P), dtb=_np.repeat(a["dt_bias_2"][0], P))
    e["cols"] = _np.concatenate([vectors[k].reshape(-1, P).T for k in COLS], axis=1)
    nc = _bacc.Bacc("TRN2", target_bir_lowering=False, num_devices=1)
    arrays, aps = {}, {}
    for name, v in e.items():
        arrays[f"in_{name}"] = _np.ascontiguousarray(v)
        aps[name] = nc.dram_tensor(f"in_{name}", v.shape, F32, kind="ExternalInput").ap()
    out = nc.dram_tensor("out_0", (D, T), F32, kind="ExternalOutput").ap()
    build(nc, aps, out)
    r = _run(nc, [arrays], core_ids=[0])
    return r.results[0]["out_0"].T[None]
```
